# Optimizing a Trainium2 kernel written in Bass

```python
import math
import jax, jax.numpy as jnp
from jax import lax
import numpy as np

D_MODEL = 1024
BATCH = 1
SEQ = 256
DEPTH = 1

RWKV_HEADS = 8
RWKV_HD = 64
RWKV_W = RWKV_HEADS * RWKV_HD
DECAY_LORA = 64
ICLR_LORA = 64
VRES_LORA = 32
GATE_LORA = 128
LNX_EPS = 64e-5
SB_HEADS = 8
SB_HD = 64
SB_W = SB_HEADS * SB_HD
SB_BLOCK = 128
MEM_LEN = 256
MEM_HEADS = 4
MEM_HD = 128
MEM_W = MEM_HEADS * MEM_HD
N_BRANCH = 3
BRANCH_W = 512
D_FF = 2816
CONV_W = 3
NORM_EPS = 1e-6

RWKV_SPLITS = (RWKV_W, RWKV_W, RWKV_W, DECAY_LORA, ICLR_LORA, GATE_LORA)
RWKV_COLS = sum(RWKV_SPLITS)
IN_COLS = RWKV_COLS + 3 * SB_W + MEM_W + N_BRANCH * D_MODEL


def rms_norm(x, g, eps=NORM_EPS):
    xf = x.astype(jnp.float32)
    y = xf * lax.rsqrt(jnp.mean(xf * xf, axis=-1, keepdims=True) + eps)
    return (y * g.astype(jnp.float32)).astype(x.dtype)

def split_heads(t, h, d):
    return t.reshape(t.shape[:-1] + (h, d))

def token_shift(p, mu):
    prev = jnp.pad(p, ((0, 0), (1, 0), (0, 0)))[:, :-1]
    return p + (prev - p) * mu

def rwkv7_recurrence(r, decay, k, v, kk, a):
    b, t, h, n = r.shape
    xs = tuple(jnp.moveaxis(z, 1, 0) for z in (r, decay, k, v, kk, a))

    def step(S, inp):
        r_t, w_t, k_t, v_t, kk_t, a_t = inp
        sa = jnp.einsum('bhij,bhj->bhi', S, -kk_t)
        S = (S * w_t[:, :, None, :]
             + sa[..., None] * (kk_t * a_t)[:, :, None, :]
             + v_t[..., None] * k_t[:, :, None, :])
        y_t = jnp.einsum('bhij,bhj->bhi', S, r_t)
        return S, y_t

    S0 = jnp.zeros((b, h, n, n), jnp.float32)
    _, ys = lax.scan(step, S0, xs)
    return jnp.moveaxis(ys, 0, 1)

def rwkv7_branch(p, mu, w0, w2, a0, a2, g2, k_k, k_a, r_k, lnx_g, lnx_b, v_first, vres):
    dt = p.dtype
    p = token_shift(p, mu)
    idx = list(np.cumsum(RWKV_SPLITS)[:-1])
    r, k, v, wl, al, gl = jnp.split(p, idx, axis=-1)
    f32 = jnp.float32
    w = -jax.nn.softplus(-(w0 + jnp.tanh(wl) @ w2).astype(f32)) - 0.5
    decay = jnp.exp(-jnp.exp(w))
    a = jax.nn.sigmoid((a0 + al @ a2).astype(f32))
    g = jax.nn.sigmoid(gl) @ g2
    if vres is None:
        v_first = v
    else:
        v0, v1, v2 = vres
        v = v + (v_first - v) * jax.nn.sigmoid(v0 + (v @ v1) @ v2)
    kk = split_heads((k * k_k).astype(f32), RWKV_HEADS, RWKV_HD)
    kk = kk / jnp.maximum(jnp.sqrt(jnp.sum(kk * kk, axis=-1, keepdims=True)), 1e-12)
    k = k.astype(f32) * (1.0 + (a - 1.0) * k_a.astype(f32))
    rh = split_heads(r.astype(f32), RWKV_HEADS, RWKV_HD)
    kh = split_heads(k, RWKV_HEADS, RWKV_HD)
    vh = split_heads(v.astype(f32), RWKV_HEADS, RWKV_HD)
    ah = split_heads(a, RWKV_HEADS, RWKV_HD)
    dh = split_heads(decay, RWKV_HEADS, RWKV_HD)
    y = rwkv7_recurrence(rh, dh, kh, vh, kk, ah)
    mean = jnp.mean(y, axis=-1, keepdims=True)
    var = jnp.mean(jnp.square(y - mean), axis=-1, keepdims=True)
    y = (y - mean) * lax.rsqrt(var + LNX_EPS)
    y = y.reshape(y.shape[:2] + (RWKV_W,)) * lnx_g.astype(f32) + lnx_b.astype(f32)
    bonus = jnp.sum(rh * kh * r_k.astype(f32), axis=-1, keepdims=True) * vh
    y = (y + bonus.reshape(y.shape)) * g.astype(f32)
    return y.astype(dt), v_first

def stick_breaking_attention(q, k, v):
    t_len = q.shape[2]
    scale = SB_HD ** -0.5
    outs = []
    for blk in range(t_len // SB_BLOCK):
        start = blk * SB_BLOCK
        end = start + SB_BLOCK
        qb = q[:, :, start:end]
        kb = k[:, :, :end]
        vb = v[:, :, :end]
        z = jnp.einsum('bhqd,bhkd->bhqk', qb, kb).astype(jnp.float32) * scale
        t_idx = start + jnp.arange(SB_BLOCK)
        s_idx = jnp.arange(end)
        mask = s_idx[None, :] < t_idx[:, None]
        log_1mb = jnp.where(mask, jax.nn.log_sigmoid(-z), 0.0)
        log_between = lax.cumsum(log_1mb, axis=3, reverse=True) - log_1mb
        attn = jnp.where(mask, jnp.exp(jax.nn.log_sigmoid(z) + log_between), 0.0)
        outs.append(jnp.einsum('bhqk,bhkd->bhqd', attn.astype(v.dtype), vb))
    return jnp.concatenate(outs, axis=2)

def stick_breaking_branch(p, q_g, k_g):
    b, t, _ = p.shape
    q, k, v = jnp.split(p, 3, axis=-1)
    q = rms_norm(split_heads(q, SB_HEADS, SB_HD), q_g).transpose(0, 2, 1, 3)
    k = rms_norm(split_heads(k, SB_HEADS, SB_HD), k_g).transpose(0, 2, 1, 3)
    v = split_heads(v, SB_HEADS, SB_HD).transpose(0, 2, 1, 3)
    o = stick_breaking_attention(q, k, v)
    return o.transpose(0, 2, 1, 3).reshape(b, t, SB_W)

def memory_branch(q, mem, mem_g, w_kv, q_g, k_g):
    b, t, _ = q.shape
    kv = rms_norm(mem, mem_g) @ w_kv
    mk, mv = jnp.split(kv, 2, axis=-1)
    qh = rms_norm(split_heads(q, MEM_HEADS, MEM_HD), q_g)
    kh = rms_norm(split_heads(mk, MEM_HEADS, MEM_HD), k_g)
    vh = split_heads(mv, MEM_HEADS, MEM_HD)
    s = jnp.einsum('bthd,bmhd->bhtm', qh, kh).astype(jnp.float32) * (MEM_HD ** -0.5)
    pr = jax.nn.softmax(s, axis=-1).astype(vh.dtype)
    o = jnp.einsum('bhtm,bmhd->bthd', pr, vh)
    return o.reshape(b, t, MEM_W)

def conv_ffn(x, g, w_up, conv_w, conv_b, w_down):
    h = rms_norm(x, g) @ w_up
    t = h.shape[1]
    hp = jnp.pad(h, ((0, 0), (CONV_W - 1, 0), (0, 0)))
    acc = conv_b + hp[:, 0:t] * conv_w[0]
    for i in range(1, CONV_W):
        acc = acc + hp[:, i:i + t] * conv_w[i]
    gate, val = jnp.split(acc, 2, axis=-1)
    return (jax.nn.silu(gate) * val) @ w_down

def first_inputs(seed: int = 0) -> dict:
    key = jax.random.key(seed)
    ks = jax.random.split(key, 40)
    f32 = jnp.float32
    nrm = lambda k, s, sc: jax.random.normal(k, s, f32) * sc
    gain = lambda k, s: 1.0 + 0.05 * jax.random.normal(k, s, f32)
    L = DEPTH
    return {
        "x": nrm(ks[0], (BATCH, SEQ, D_MODEL), 1.0),
        "mem": nrm(ks[1], (BATCH, MEM_LEN, D_MODEL), 1.0),
        "norm1_g": gain(ks[2], (L, D_MODEL)),
        "w_in": nrm(ks[3], (L, D_MODEL, IN_COLS), D_MODEL ** -0.5),
        "shift_mu": jax.random.uniform(ks[4], (L, RWKV_COLS), f32, 0.0, 1.0),
        "decay_w0": jax.random.uniform(ks[5], (L, RWKV_W), f32, -6.0, 1.0),
        "decay_w2": nrm(ks[6], (L, DECAY_LORA, RWKV_W), 0.5 * DECAY_LORA ** -0.5),
        "iclr_a0": nrm(ks[7], (L, RWKV_W), 0.1),
        "iclr_a2": nrm(ks[8], (L, ICLR_LORA, RWKV_W), ICLR_LORA ** -0.5),
        "gate_g2": nrm(ks[9], (L, GATE_LORA, RWKV_W), GATE_LORA ** -0.5),
        "k_k": 0.85 + 0.05 * jax.random.normal(ks[10], (L, RWKV_W), f32),
        "k_a": gain(ks[11], (L, RWKV_W)),
        "r_k": nrm(ks[12], (L, RWKV_HEADS, RWKV_HD), 0.1),
        "lnx_g": gain(ks[13], (L, RWKV_W)),
        "lnx_b": nrm(ks[14], (L, RWKV_W), 0.02),
        "vres_v0": 1.0 + 0.1 * jax.random.normal(ks[15], (L - 1, RWKV_W), f32),
        "vres_v1": nrm(ks[16], (L - 1, RWKV_W, VRES_LORA), RWKV_W ** -0.5),
        "vres_v2": nrm(ks[17], (L - 1, VRES_LORA, RWKV_W), VRES_LORA ** -0.5),
        "sb_q_norm_g": gain(ks[18], (L, SB_HD)),
        "sb_k_norm_g": gain(ks[19], (L, SB_HD)),
        "mem_norm_g": gain(ks[20], (L, D_MODEL)),
        "w_mem_kv": nrm(ks[21], (L, D_MODEL, 2 * MEM_W), D_MODEL ** -0.5),
        "mem_q_norm_g": gain(ks[22], (L, MEM_HD)),
        "mem_k_norm_g": gain(ks[23], (L, MEM_HD)),
        "w_branch": nrm(ks[24], (L, N_BRANCH, BRANCH_W, D_MODEL), BRANCH_W ** -0.5),
        "w_out": nrm(ks[25], (L, D_MODEL, D_MODEL), D_MODEL ** -0.5),
        "norm2_g": gain(ks[26], (L, D_MODEL)),
        "w_up": nrm(ks[27], (L, D_MODEL, 2 * D_FF), D_MODEL ** -0.5),
        "conv_w": nrm(ks[28], (L, CONV_W, 2 * D_FF), CONV_W ** -0.5),
        "conv_b": nrm(ks[29], (L, 2 * D_FF), 0.02),
        "w_down": nrm(ks[30], (L, D_FF, D_MODEL), D_FF ** -0.5),
    }

def first_block(x, mem, norm1_g, w_in, shift_mu, decay_w0, decay_w2, iclr_a0, iclr_a2, gate_g2,
              k_k, k_a, r_k, lnx_g, lnx_b, vres_v0, vres_v1, vres_v2, sb_q_norm_g, sb_k_norm_g,
              mem_norm_g, w_mem_kv, mem_q_norm_g, mem_k_norm_g, w_branch, w_out, norm2_g,
              w_up, conv_w, conv_b, w_down):
    b, t, _ = x.shape
    cut = [RWKV_COLS, RWKV_COLS + 3 * SB_W, RWKV_COLS + 3 * SB_W + MEM_W]
    v_first = None
    for l in range(DEPTH):
        h = rms_norm(x, norm1_g[l])
        proj = h @ w_in[l]
        p_rwkv, p_sb, q_mem, gate_logits = jnp.split(proj, cut, axis=-1)
        vres = None if l == 0 else (vres_v0[l - 1], vres_v1[l - 1], vres_v2[l - 1])
        y_a, v_first = rwkv7_branch(p_rwkv, shift_mu[l], decay_w0[l], decay_w2[l], iclr_a0[l],
                                    iclr_a2[l], gate_g2[l], k_k[l], k_a[l], r_k[l], lnx_g[l],
                                    lnx_b[l], v_first, vres)
        y_b = stick_breaking_branch(p_sb, sb_q_norm_g[l], sb_k_norm_g[l])
        y_m = memory_branch(q_mem, mem, mem_norm_g[l], w_mem_kv[l], mem_q_norm_g[l], mem_k_norm_g[l])
        ys = jnp.stack([y_a, y_b.astype(y_a.dtype), y_m.astype(y_a.dtype)], axis=2)
        branch_out = jnp.einsum('btnc,ncd->btnd', ys, w_branch[l])
        gates = jax.nn.sigmoid(gate_logits.reshape(b, t, N_BRANCH, D_MODEL))
        merged = jnp.sum(gates * branch_out, axis=2)
        x = x + merged @ w_out[l]
        x = x + conv_ffn(x, norm2_g[l], w_up[l], conv_w[l], conv_b[l], w_down[l])
    return x


D_MIX = D_MODEL
ATTN_HEADS = 8
ATTN_HD = 64
ATTN_W = ATTN_HEADS * ATTN_HD
MOBA_BLOCK = 256
MOBA_TOPK = 3
Q_BLOCK = 128
REC_HEADS = 4
REC_DK = 128
REC_DV = 128
REC_W = REC_HEADS * REC_DK
REC_VW = REC_HEADS * REC_DV
REC_CHUNK = 64
PEER_HEADS = 8
PEER_NKEYS = 128
PEER_N = PEER_NKEYS * PEER_NKEYS
PEER_DKEY = 256
PEER_TOPK = 16
PEER_TOKEN_BLOCK = 128
IN_WIDTHS = [ATTN_W, ATTN_W, ATTN_W, REC_W, REC_W, REC_VW, REC_VW]
IN_COLS_2 = sum(IN_WIDTHS)
IN_SPLITS = [int(c) for c in np.cumsum(IN_WIDTHS)[:-1]]


def rmsnorm(x, g):
    xf = x.astype(jnp.float32)
    y = xf * lax.rsqrt(jnp.mean(xf * xf, axis=-1, keepdims=True) + NORM_EPS)
    return (y * g.astype(jnp.float32)).astype(x.dtype)

def alibi_slopes(n):
    return 2.0 ** (-8.0 * jnp.arange(1, n + 1, dtype=jnp.float32) / n)

def moba_attention(q, k, v):
    B, S, H, hd = q.shape
    nb = -(-S // MOBA_BLOCK)
    pad = nb * MOBA_BLOCK - S
    kp = jnp.pad(k, ((0, 0), (0, pad), (0, 0), (0, 0)))
    vp = jnp.pad(v, ((0, 0), (0, pad), (0, 0), (0, 0)))
    kb = kp.reshape(B, nb, MOBA_BLOCK, H, hd).transpose(0, 3, 1, 2, 4)
    vb = vp.reshape(B, nb, MOBA_BLOCK, H, hd).transpose(0, 3, 1, 2, 4)
    kmean = jnp.mean(kb.astype(jnp.float32), axis=3)
    gate = jnp.einsum('bshd,bhnd->bhsn', q.astype(jnp.float32), kmean)
    pos = jnp.arange(S)
    past = jnp.arange(nb)[None, :] < (pos // MOBA_BLOCK)[:, None]
    gate = jnp.where(past[None, None], gate, -jnp.inf)
    ksel = min(MOBA_TOPK, nb)
    _, sel = lax.top_k(gate, ksel)
    nq = S // Q_BLOCK
    qq = q.reshape(B, nq, Q_BLOCK, H, hd).transpose(0, 1, 3, 2, 4).reshape(B * nq, H, Q_BLOCK, hd)
    ss = sel.reshape(B, H, nq, Q_BLOCK, ksel).transpose(0, 2, 1, 3, 4).reshape(B * nq, H, Q_BLOCK, ksel)
    b_idx = jnp.repeat(jnp.arange(B, dtype=jnp.int32), nq)
    qb_idx = jnp.tile(jnp.arange(nq, dtype=jnp.int32), B)
    slopes = alibi_slopes(H)
    scale = hd ** -0.5
    off = jnp.arange(MOBA_BLOCK)
    gather = jax.vmap(lambda kk, s: kk[s])

    def one_block(args):
        qblk, sblk, b, qi = args
        kh = kb[b]
        vh = vb[b]
        tpos = qi * Q_BLOCK + jnp.arange(Q_BLOCK)
        own = (qi * Q_BLOCK) // MOBA_BLOCK
        k_s = gather(kh, sblk).astype(jnp.float32)
        v_s = gather(vh, sblk).astype(jnp.float32)
        k_o = lax.dynamic_index_in_dim(kh, own, axis=1, keepdims=False).astype(jnp.float32)
        v_o = lax.dynamic_index_in_dim(vh, own, axis=1, keepdims=False).astype(jnp.float32)
        qf = qblk.astype(jnp.float32) * scale
        s_sel = jnp.einsum('hqd,hqjkd->hqjk', qf, k_s)
        kpos_sel = sblk[..., None] * MOBA_BLOCK + off
        dist_sel = (tpos[None, :, None, None] - kpos_sel).astype(jnp.float32)
        s_sel = s_sel - slopes[:, None, None, None] * dist_sel
        s_sel = jnp.where((sblk < own)[..., None], s_sel, -jnp.inf)
        s_own = jnp.einsum('hqd,hkd->hqk', qf, k_o)
        kpos_own = own * MOBA_BLOCK + off
        dist_own = (tpos[:, None] - kpos_own[None, :]).astype(jnp.float32)
        s_own = s_own - slopes[:, None, None] * dist_own[None]
        s_own = jnp.where((kpos_own[None, :] <= tpos[:, None])[None], s_own, -jnp.inf)
        logits = jnp.concatenate([s_sel.reshape(H, Q_BLOCK, ksel * MOBA_BLOCK), s_own], axis=-1)
        p = jax.nn.softmax(logits, axis=-1)
        p_sel = p[..., :ksel * MOBA_BLOCK].reshape(H, Q_BLOCK, ksel, MOBA_BLOCK)
        p_own = p[..., ksel * MOBA_BLOCK:]
        o = jnp.einsum('hqjk,hqjkd->qhd', p_sel, v_s) + jnp.einsum('hqk,hkd->qhd', p_own, v_o)
        return o.astype(q.dtype)

    out = lax.map(one_block, (qq, ss, b_idx, qb_idx))
    return out.reshape(B, S, H * hd)

def hgrn2(q, f_pre, i, g, lb, norm_g):
    B, S, _ = q.shape
    nc = S // REC_CHUNK
    f = lb + (1.0 - lb) * jax.nn.sigmoid(f_pre.astype(jnp.float32))
    logf = jnp.log(f)
    kk = 1.0 - f
    qf = jax.nn.silu(q.astype(jnp.float32))
    vf = i.astype(jnp.float32)

    def heads(t, d):
        return t.reshape(B, nc, REC_CHUNK, REC_HEADS, d).transpose(1, 0, 3, 2, 4)

    causal = jnp.tril(jnp.ones((REC_CHUNK, REC_CHUNK), dtype=bool))

    def step(state, inp):
        qc, lfc, kc, vc = inp
        cum = jnp.cumsum(lfc, axis=2)
        diff = cum[:, :, :, None, :] - cum[:, :, None, :, :]
        decay = jnp.where(causal[None, None, :, :, None], jnp.exp(jnp.minimum(diff, 0.0)), 0.0)
        scores = jnp.einsum('bhtd,bhtsd,bhsd->bhts', qc, decay, kc)
        o = jnp.einsum('bhts,bhsv->bhtv', scores, vc) + jnp.einsum('bhtd,bhdv->bhtv', qc * jnp.exp(cum), state)
        last = cum[:, :, -1:, :]
        state = jnp.exp(last[:, :, 0, :])[..., None] * state + jnp.einsum('bhsd,bhsv->bhdv', kc * jnp.exp(last - cum), vc)
        return state, o

    state0 = jnp.zeros((B, REC_HEADS, REC_DK, REC_DV), jnp.float32)
    _, o = lax.scan(step, state0, (heads(qf, REC_DK), heads(logf, REC_DK), heads(kk, REC_DK), heads(vf, REC_DV)))
    o = o.transpose(1, 0, 3, 2, 4).reshape(B, S, REC_HEADS, REC_DV)
    o = rmsnorm(o, norm_g.reshape(REC_HEADS, REC_DV))
    o = o * jax.nn.silu(g.astype(jnp.float32)).reshape(B, S, REC_HEADS, REC_DV)
    return o.reshape(B, S, REC_VW).astype(q.dtype)

def peer(x, wq, subkeys, u, v):
    B, S, D = x.shape
    T = B * S
    xt = x.reshape(T // PEER_TOKEN_BLOCK, PEER_TOKEN_BLOCK, D)

    def one(xb):
        qp = (xb @ wq).reshape(PEER_TOKEN_BLOCK, PEER_HEADS, 2, PEER_DKEY // 2)
        s = jnp.einsum('thcd,hcnd->thcn', qp.astype(jnp.float32), subkeys.astype(jnp.float32))
        v1, i1 = lax.top_k(s[:, :, 0], PEER_TOPK)
        v2, i2 = lax.top_k(s[:, :, 1], PEER_TOPK)
        cand = (v1[..., :, None] + v2[..., None, :]).reshape(PEER_TOKEN_BLOCK, PEER_HEADS, PEER_TOPK * PEER_TOPK)
        cidx = (i1[..., :, None] * PEER_NKEYS + i2[..., None, :]).reshape(PEER_TOKEN_BLOCK, PEER_HEADS, PEER_TOPK * PEER_TOPK)
        sc, p = lax.top_k(cand, PEER_TOPK)
        eidx = jnp.take_along_axis(cidx, p, axis=-1)
        gates = jax.nn.softmax(sc, axis=-1)
        ue = u[eidx]
        ve = v[eidx]
        act = jax.nn.gelu(jnp.einsum('td,thkd->thk', xb, ue).astype(jnp.float32), approximate=False)
        return jnp.einsum('thk,thkd->td', (gates * act).astype(x.dtype), ve)

    return lax.map(one, xt).reshape(B, S, D)

def second_inputs(seed: int = 0) -> dict:
    key = jax.random.key(seed)
    ks = jax.random.split(key, 12)
    nrm = jax.random.normal
    x = nrm(ks[0], (BATCH, SEQ, D_MODEL), jnp.float32)
    norm1_g = 1.0 + 0.05 * nrm(ks[1], (DEPTH, D_MODEL), jnp.float32)
    w_in = nrm(ks[2], (DEPTH, D_MODEL, IN_COLS_2), jnp.float32) * D_MODEL ** -0.5
    rec_lb_logits = 0.5 * nrm(ks[3], (DEPTH + 1, REC_W), jnp.float32)
    rec_norm_g = 1.0 + 0.05 * nrm(ks[4], (DEPTH, REC_VW), jnp.float32)
    w_out = nrm(ks[5], (DEPTH, D_MIX, D_MODEL), jnp.float32) * D_MIX ** -0.5
    norm2_g = 1.0 + 0.05 * nrm(ks[6], (DEPTH, D_MODEL), jnp.float32)
    peer_wq = nrm(ks[7], (DEPTH, D_MODEL, PEER_HEADS * PEER_DKEY), jnp.float32) * D_MODEL ** -0.5
    peer_subkeys = nrm(ks[8], (DEPTH, PEER_HEADS, 2, PEER_NKEYS, PEER_DKEY // 2), jnp.float32) * (PEER_DKEY // 2) ** -0.5
    peer_u = nrm(ks[9], (DEPTH, PEER_N, D_MODEL), jnp.float32) * D_MODEL ** -0.5
    peer_v = 0.1 * nrm(ks[10], (DEPTH, PEER_N, D_MODEL), jnp.float32)
    normf_g = 1.0 + 0.05 * nrm(ks[11], (D_MODEL,), jnp.float32)
    return {'x': x, 'norm1_g': norm1_g, 'w_in': w_in, 'rec_lb_logits': rec_lb_logits,
            'rec_norm_g': rec_norm_g, 'w_out': w_out, 'norm2_g': norm2_g, 'peer_wq': peer_wq,
            'peer_subkeys': peer_subkeys, 'peer_u': peer_u, 'peer_v': peer_v, 'normf_g': normf_g}

def second_block(x, norm1_g, w_in, rec_lb_logits, rec_norm_g, w_out, norm2_g, peer_wq, peer_subkeys, peer_u, peer_v, normf_g):
    B, S, _ = x.shape
    lb_all = jnp.cumsum(jax.nn.softmax(rec_lb_logits.astype(jnp.float32), axis=0), axis=0)
    h = x
    for layer in range(DEPTH):
        xn = rmsnorm(h, norm1_g[layer])
        proj = xn @ w_in[layer]
        q_a, k_a, v_a, q_r, f_r, i_r, g_r = jnp.split(proj, IN_SPLITS, axis=-1)
        attn = moba_attention(q_a.reshape(B, S, ATTN_HEADS, ATTN_HD),
                              k_a.reshape(B, S, ATTN_HEADS, ATTN_HD),
                              v_a.reshape(B, S, ATTN_HEADS, ATTN_HD))
        rec = hgrn2(q_r, f_r, i_r, g_r, lb_all[layer], rec_norm_g[layer])
        h = h + jnp.concatenate([attn, rec], axis=-1) @ w_out[layer]
        hn = rmsnorm(h, norm2_g[layer])
        h = h + peer(hn, peer_wq[layer], peer_subkeys[layer], peer_u[layer], peer_v[layer])
    return rmsnorm(h, normf_g)


def setup_inputs(seed=0):
    out = dict(first_inputs(seed))
    for name, value in second_inputs(seed + 1).items():
        if name != "x":
            out[name + "_2"] = value
    return out


def reference(
    x, mem, norm1_g, w_in, shift_mu, decay_w0, decay_w2, iclr_a0, iclr_a2, gate_g2, k_k, k_a,
    r_k, lnx_g, lnx_b, vres_v0, vres_v1, vres_v2, sb_q_norm_g, sb_k_norm_g, mem_norm_g,
    w_mem_kv, mem_q_norm_g, mem_k_norm_g, w_branch, w_out, norm2_g, w_up, conv_w, conv_b,
    w_down, norm1_g_2, w_in_2, rec_lb_logits_2, rec_norm_g_2, w_out_2, norm2_g_2, peer_wq_2,
    peer_subkeys_2, peer_u_2, peer_v_2, normf_g_2,
):
    x = first_block(
        x, mem, norm1_g, w_in, shift_mu, decay_w0, decay_w2, iclr_a0, iclr_a2, gate_g2, k_k,
        k_a, r_k, lnx_g, lnx_b, vres_v0, vres_v1, vres_v2, sb_q_norm_g, sb_k_norm_g, mem_norm_g,
        w_mem_kv, mem_q_norm_g, mem_k_norm_g, w_branch, w_out, norm2_g, w_up, conv_w, conv_b,
        w_down,
    )
    return second_block(
        x, norm1_g_2, w_in_2, rec_lb_logits_2, rec_norm_g_2, w_out_2, norm2_g_2, peer_wq_2,
        peer_subkeys_2, peer_u_2, peer_v_2, normf_g_2,
    )


_drawn_inputs = setup_inputs


def setup_inputs(seed=0):
    import zlib

    import numpy as np

    out = dict(_drawn_inputs(seed))
    spreads = {}
    factors = {'decay_w2': 6.478,
     'iclr_a0': 4.214,
     'k_k': 29.915,
     'k_a': 2.948,
     'lnx_g': 13.854,
     'lnx_b': 30.951,
     'sb_q_norm_g': 18.298,
     'sb_k_norm_g': 15.928,
     'mem_norm_g': 8.0,
     'mem_q_norm_g': 8.0,
     'mem_k_norm_g': 8.0,
     'conv_b': 11.8,
     'rec_lb_logits_2': 3.026,
     'rec_norm_g_2': 46.088,
     'norm2_g_2': 47.09,
     'norm2_g': 4.732,
     'norm1_g_2': 2.788}
    for name, (base, spread) in spreads.items():
        noise = np.random.default_rng([zlib.crc32(name.encode()), seed]).standard_normal(out[name].shape)
        drawn = base * np.exp(spread * noise) if base else spread * noise
        out[name] = __import__('jax').numpy.asarray(drawn.astype(out[name].dtype))
    for name, factor in factors.items():
        out[name] = (out[name] * factor).astype(out[name].dtype)
    return out
```

```python
import numpy as np
import concourse.bass as bass
from concourse import mybir

F32 = mybir.dt.float32
U32 = mybir.dt.uint32
ALU = mybir.AluOpType
ACT = mybir.ActivationFunctionType
AX = mybir.AxisListType

P = 128
T = 256
D = 1024
KT = D // P
RH, RHD = 8, 64
SH, SHD = 8, 64
MH, MHD = 4, 128
MEM = 256
FF = 2816
FT = FF // P
BH, BHD = 8, 64
GH = 4
NK, TOPK, PH = 128, 16, 8
SLOTS = 4
PAGE = 8 * P
BIG = 3.0e38
DECAY_SCALE = -float(np.exp(-0.5))

N_IN_A, N_SBV, N_MK, N_MV, N_GATE = 26, 4, 4, 4, 24
N_BR, N_OUT, N_UP, N_DOWN = 12, 8, 2 * FT, FT
N_IN2, N_TOK2, N_OUT2, N_WQ = 20, 8, 8, 16
STAGES = ["in_a", "sbv", "mk", "mv", "gate", "branch", "out", "up", "down", "in2", "tok2", "out2", "wq"]
COUNTS = [N_IN_A, N_SBV, N_MK, N_MV, N_GATE, N_BR, N_OUT, N_UP, N_DOWN, N_IN2, N_TOK2, N_OUT2, N_WQ]
PAGE0 = {s: sum(COUNTS[:i]) for i, s in enumerate(STAGES)}
N_PAGES = sum(COUNTS)
TILED = [s for s in STAGES if s not in ("branch", "down")]
TILE0 = {s: sum(COUNTS[STAGES.index(x)] for x in TILED[:i]) for i, s in enumerate(TILED)}

VECS = [("mu", 14), ("norm1_g", 8), ("decay_w0", 4), ("iclr_a0", 4), ("k_k", 4), ("k_a", 4), ("r_k", 4),
        ("lnx_g", 4), ("lnx_b", 4), ("sb_q_g", 1), ("sb_k_g", 1), ("mem_g", 8), ("mem_q_g", 1), ("mem_k_g", 1),
        ("norm2_g", 8), ("conv_w0", 2 * FT), ("conv_w1", 2 * FT), ("conv_w2", 2 * FT), ("conv_b", 2 * FT),
        ("norm1_g_2", 8), ("lb0", 4), ("lb1", 4), ("rec_g", 4), ("norm2_g_2", 8), ("normf_g", 8)]
VCOL = {n: sum(c for _, c in VECS[:i]) for i, (n, _) in enumerate(VECS)}
N_VEC = sum(c for _, c in VECS)

LEVELS = [1, 2, 4, 8, 16, 32, 64]
C_IDENT, C_ONES, C_BLK64, C_INCL, C_STRICT, C_SUFFIX, C_LEVEL = [P * i for i in range(7)]
C_ALIBI = C_LEVEL + P * len(LEVELS)
C_IOTA = C_ALIBI + 2 * T
N_CONST = C_IOTA + TOPK


SQ = {n: i + 1 for i, n in enumerate(["kk", "bonus", "gn_var", "sbq", "sbk", "mq", "mk", "hn"])}
SUM = {n: i + 1 for i, n in enumerate(["kk", "bonus", "gn_mean", "gn_var", "sbq", "sbk", "mq", "mk", "hn"])}
ROOT = {n: i + 1 for i, n in enumerate(["kk", "gn_var", "sbq", "sbk", "mq", "mk", "hn"])}
HEAD0 = {"mem": 0, "moba": MH}


def constants():
    c = np.zeros((P, N_CONST), np.float32)
    p, f = np.arange(P)[:, None], np.arange(P)[None, :]
    c[:, C_IDENT:C_IDENT + P] = p == f
    c[:, C_ONES:C_ONES + P] = 1
    c[:, C_BLK64:C_BLK64 + P] = p // 64 == f // 64
    c[:, C_INCL:C_INCL + P] = f >= p
    c[:, C_STRICT:C_STRICT + P] = f > p
    c[:, C_SUFFIX:C_SUFFIX + P] = p >= f
    for i, h in enumerate(LEVELS):
        c[:, C_LEVEL + P * i:C_LEVEL + P * (i + 1)] = (p // (2 * h) == f // (2 * h)) & (p % (2 * h) < h) & (f % (2 * h) >= h)
    s = np.arange(T)[None, :]
    for tt in range(2):
        t = p + P * tt
        c[:, C_ALIBI + T * tt:C_ALIBI + T * (tt + 1)] = np.where(s <= t, s - t, -1e30)
    c[:, C_IOTA:C_IOTA + TOPK] = np.arange(TOPK)
    return c


def build(nc, A):
    sems = {}

    def S(name):
        if name not in sems:
            sems[name] = nc.semaphore(name).__enter__()
        return sems[name]

    def sb(name, shape, dt=F32):
        return nc.sbuf_tensor(name, shape, dt).__enter__()[tuple(slice(None) for _ in shape)]

    const = sb("const", [P, N_CONST])
    vec = sb("vec", [P, N_VEC])
    ring = sb("ring", [P, SLOTS, PAGE])
    x = sb("x_res", [P, KT, T])
    hn = sb("h_norm", [P, KT, T])
    ARENA = 41200
    arena = sb("arena", [P, ARENA])
    bank = [nc.psum_tensor(f"bank{i}", [P, 512], F32).__enter__() for i in range(8)]

    def at(off, *shape):
        n = int(np.prod(shape))
        assert off + n <= ARENA, (off, n)
        v = arena[:, off:off + n]
        if len(shape) == 2:
            v = v.rearrange("p (a b) -> p a b", b=shape[1])
        if len(shape) == 3:
            v = v.rearrange("p (a b c) -> p a b c", b=shape[1], c=shape[2])
        if len(shape) == 4:
            v = v.rearrange("p (a b c d) -> p a b c d", b=shape[1], c=shape[2], d=shape[3])
        return v

    def two(ap, b):
        return ap.rearrange("p (a b) -> p a b", b=b)

    def cst(c, n=P):
        return const[:, c:c + n]

    ident, ones, blk64 = cst(C_IDENT), cst(C_ONES), cst(C_BLK64)

    def many(ap, n):
        return ap.unsqueeze(1).broadcast_to([ap.shape[0], n, ap.shape[1]])

    def each(ap, n):
        return ap.unsqueeze(2).broadcast_to([ap.shape[0], ap.shape[1], n])

    def V(name, i=0):
        return vec[:, VCOL[name] + i:VCOL[name] + i + 1]

    memn = at(0, KT, T)
    proj = at(2048, N_IN_A, T)
    sbv = at(8704, 4, 2, P)
    mk = at(9728, 4, T)
    mv = at(10752, 4, 2, P)
    gates = at(11776, N_GATE, T)
    ys = at(17920, 12, T)
    W0 = 20992
    raw_r, raw_k, raw_v = proj[:, 0:4, :], proj[:, 4:8, :], proj[:, 8:12, :]
    tmp1, tmp2, tmp3 = at(W0, 4, T), at(W0 + 1024, 4, T), at(W0 + 2048, 4, T)
    logw, iclr, cc, kk = (at(W0 + 3072 + 1024 * i, 4, T) for i in range(4))
    shift_d = at(W0, 14, T)
    bT, kT, bonus, gT = (at(W0 + 7168 + 1024 * i, 4, T) for i in range(4))
    AR = at(W0 + 11264, 4, 2, 2, P)
    Vtok = at(W0 + 13312, 2, 512)
    Btok, Ktok = at(W0 + 14336, 512), at(W0 + 14848, 512)
    S1 = at(W0 + 15360, 4, 64)
    fac = at(W0 + 15616, 4, 1)
    mid = at(W0 + 15620, 8)
    lora_w = at(W0 + 15640, 2, 512)
    Y = at(W0 + 16664, 4, T)
    grp = []
    for g, o in enumerate((W0, W0 + 17688)):
        grp.append(o)
    MT = [at(W0, 4, P), at(W0 + 512, 4, P)]
    DD = [at(W0 + 1024, 4, P), at(W0 + 1536, 4, P)]
    DT = [at(W0 + 2048, 4, P), at(W0 + 2560, 4, P)]
    PP = [at(W0 + 3072, 4, P), at(W0 + 3584, 4, P)]
    CT = [at(W0 + 4096, 4, P), at(W0 + 4608, 4, P)]
    RB = [at(W0 + 5120, 4, P), at(W0 + 5632, 4, P)]
    KA = [at(W0 + 6144, 4, P), at(W0 + 6656, 4, P)]
    RK = [at(W0 + 17688, 4, P), at(W0 + 18200, 4, P)]
    Gs, Us = at(W0 + 18712, 512), at(W0 + 19224, 512)
    Vtok_sq = logw

    nsq, nroot, ninv = at(W0, KT, T), at(W0 + 2048, T), at(W0 + 2304, T)

    zc = 3 * P
    sbz, sba, sbb = at(W0, 8, zc), at(W0 + 3072, 8, zc), at(W0 + 6144, 8, zc)
    att_z = [at(W0 + 10000 + 512 * i, 2, T) for i in range(2)]
    att_p = [at(W0 + 11024 + 512 * i, 2, T) for i in range(2)]
    att_t = [at(W0 + 12048 + 512 * i, 2, T) for i in range(2)]
    att_m = [at(W0 + 13072 + 8 * i, 2) for i in range(2)]
    att_s = [at(W0 + 13090 + 8 * i, 2) for i in range(2)]
    att_r = [at(W0 + 13110 + 8 * i, 2) for i in range(2)]
    merged = at(W0, KT, T)
    gated = at(W0 + 2048, 2, T)

    ff = at(0, FT, T)
    conv_u = at(FT * T, 4, T)
    sig_u = at(FT * T + 1024, 2, T)

    pj = at(0, N_IN2, T)
    tok2 = at(5120, 8, 2, P)
    cat = at(7168, 8, T)
    bias_h = at(9216, 8, 2 * T)
    hw = 13312
    hq, hk, hcum, hE, hQ, hK, hf = (at(hw + 1024 * i, 4, T) for i in range(7))
    hacc = at(hw + 7168, 2, 4, P)
    hx = at(hw + 8192, 4, P)
    hmul = at(hw + 8704, 4, P)
    lbv = at(hw + 9216, 16)
    qp = at(0, N_WQ, T)
    subk = at(4096, N_WQ, NK)
    scores = at(6144, 2, N_WQ, NK)
    work = at(10240, T)
    htok = at(10496, 2, D)
    cand = at(12544, 8, T)
    top_v = at(14592, 2, N_WQ, TOPK)
    top_i = at(15104, 2, N_WQ, TOPK).bitcast(U32)
    top_f = at(15616, 2, N_WQ, TOPK)
    sel_v = at(16128, 2, PH, TOPK)
    pos_u = at(16384, PH, TOPK).bitcast(U32)
    a_u, b_u = at(16512, P).bitcast(U32), at(16640, P).bitcast(U32)
    a_f, b_f, i_a, i_b = (at(16768 + P * i, P) for i in range(4))
    gate_p = at(17280, 2, P)
    eidx = at(17536, 2, P).bitcast(U32)
    eqm = at(17792, P, TOPK)
    rsum = at(19840, 16)
    e_act = at(19860, 4)
    e_gelu = at(19864, 4)
    diag = at(19872, 4, P)
    junk = at(20384, 1024)
    UVS = 4
    uv = at(21408, UVS, 2 * D)
    yt = at(29600, 2, D)

    def done(eng, ins, sem, n):
        ins.then_inc(S(sem), 1)
        eng.wait_ge(S(sem), n)

    def chain(eng, name):
        n = [0]

        def step(ins):
            n[0] += 1
            done(eng, ins, name, n[0])
        return step

    def barrier(eng, k):
        eng.drain().then_inc(S("phase_done"), 1)
        eng.wait_ge(S("phase_done"), 3 * k)

    block = nc.Block().__enter__()

    @block.sync
    def _(sp):
        sp.dma_start(const[:, :], A["const"]).then_inc(S("const_in"), 16)
        sp.dma_start(vec[:, :], A["vec"]).then_inc(S("vec_in"), 16)
        sp.dma_start(x[:, :, :], A["xT"]).then_inc(S("x_in"), 16)

        def load(slot, page, n):
            sp.dma_start(ring[:, slot, :], page).then_inc(S(f"page_in{slot}"), 16)

        for s in range(SLOTS):
            load(s, A["pages"][s], 1)
        with sp.Fori(0, N_PAGES // SLOTS - 1) as i:
            for s in range(SLOTS):
                sp.wait_ge(S("page_done"), i * SLOTS + s + 1)
                load(s, A["pages"][bass.ds(i * SLOTS + s + SLOTS, 1)].rearrange("o p c -> (o p) c"), 1)
        sp.wait_ge(S("final_out"), 1)
        sp.dma_start(A["out"], hn[:, :, :]).then_inc(S("out_stored"), 16)
        sp.wait_ge(S("out_stored"), 16)

    @block.tensor
    def _(pe):
        mm = nc.tensor.matmul

        def page_ready(page, i=None):
            n = page // SLOTS + 1
            pe.wait_ge(S(f"page_in{page % SLOTS}"), 16 * n if i is None else i * 16 + 16 * n)

        def linear(stage, src, by_token=False):
            page0, tile0, n = PAGE0[stage], TILE0[stage], COUNTS[STAGES.index(stage)]

            def one(b, i=None):
                page, tile = page0 + b, tile0 + b
                page_ready(page, i)
                pe.wait_ge(S("tile_taken"), tile + 1 if i is None else i * SLOTS + tile + 1)
                w, out = ring[:, page % SLOTS, :], bank[page % SLOTS]
                if by_token:
                    for tt in range(2):
                        for k in range(KT):
                            last = mm(out[:, tt * P:(tt + 1) * P], src[:, k, tt * P:(tt + 1) * P], w[:, k * P:(k + 1) * P],
                                      start=k == 0, stop=k == KT - 1)
                else:
                    for k in range(KT):
                        last = mm(out[:, 0:T], w[:, k * P:(k + 1) * P], src[:, k, :], start=k == 0, stop=k == KT - 1)
                last.then_inc(S("page_done"), 1)

            groups = n // SLOTS
            if groups > 1:
                with pe.Fori(0, groups) as i:
                    for b in range(SLOTS):
                        one(b, i)
            else:
                for b in range(groups * SLOTS):
                    one(b)
            for b in range(groups * SLOTS, n):
                one(b)

        def wide(page0, rhs, n, first, last_page):
            for k in range(n):
                page_ready(page0 + k)
                w = ring[:, (page0 + k) % SLOTS, :]
                for j in range(KT):
                    last = mm(bank[j][:, 0:T], w[:, j * P:(j + 1) * P], rhs(k), start=first and k == 0,
                              stop=last_page and k == n - 1)
                last.then_inc(S("page_done"), 1)

        def norm_sum(i):
            pe.wait_ge(S("norm_sq"), i + 1)
            for k in range(KT):
                last = mm(bank[4][:, 0:T], ones, nsq[:, k, :], start=k == 0, stop=k == KT - 1)
            last.then_inc(S("norm_sum"), 1)

        def head_sum(name, mat, src, b0, wait=True):
            if wait:
                pe.wait_ge(S("head_sq"), SQ[name])
            for j in range(2):
                last = mm(bank[b0 + j][:, :], mat, src[:, 2 * j:2 * j + 2, :], start=True, stop=True)
            last.then_inc(S("head_sum"), 1)

        pe.wait_ge(S("const_in"), 16)
        norm_sum(0)
        norm_sum(1)
        pe.wait_ge(S("norm_out"), 2)
        linear("in_a", hn)
        linear("sbv", hn, by_token=True)
        linear("mk", memn)
        pe.wait_ge(S("lora_w_in"), 48)
        pe.wait_ge(S("lora_act"), 1)
        for ft in range(4):
            mm(bank[4 + ft // 2][:, (ft % 2) * T:(ft % 2) * T + T], lora_w[0:64, 0, ft * P:(ft + 1) * P], proj[0:64, 12, :],
               start=True, stop=True)
            last = mm(bank[6 + ft // 2][:, (ft % 2) * T:(ft % 2) * T + T], lora_w[64:128, 0, ft * P:(ft + 1) * P],
                      proj[64:128, 12, :], start=True, stop=True)
        last.then_inc(S("lora_up"), 1)
        linear("mv", memn, by_token=True)
        pe.wait_ge(S("lora_taken"), 1)
        for ft in range(4):
            last = mm(bank[4 + ft // 2][:, (ft % 2) * T:(ft % 2) * T + T], lora_w[:, 1, ft * P:(ft + 1) * P], proj[:, 13, :],
                      start=True, stop=True)
        last.then_inc(S("gate_up"), 1)
        head_sum("kk", blk64, tmp2, 6)
        pe.wait_ge(S("gate_taken"), 1)
        head_sum("bonus", blk64, tmp3, 4)
        linear("gate", hn)
        pe.wait_ge(S("bonus_done"), 1)
        for tt in range(2):
            for ft in range(4):
                last = nc.tensor.transpose(bank[4 + tt][:, ft * P:(ft + 1) * P], raw_v[:, ft, tt * P:(tt + 1) * P], ident)
        last.then_inc(S("vtok"), 1)
        pe.wait_ge(S("scaled"), 1)
        for ft in range(4):
            nc.tensor.transpose(bank[6][:, ft * P:(ft + 1) * P], bT[:, ft, 0:P], ident)
            last = nc.tensor.transpose(bank[7][:, ft * P:(ft + 1) * P], kT[:, ft, 0:P], ident)
        last.then_inc(S("bktok"), 1)
        barrier(pe, 1)
        for c in range(2):
            for g in range(2):
                for hh in range(4):
                    h = 4 * g + hh
                    ft, o = h // 2, (h % 2) * 64
                    rhs = AR[o:o + 64, ft, c, :, :]
                    b, col = 4 * g + hh % 2, (hh // 2) * T
                    mm(bank[b][:, col:col + T], bT[o:o + 64, ft, c * P:(c + 1) * P], rhs, start=True, stop=True)
                    last = mm(bank[b + 2][:, col:col + T], kT[o:o + 64, ft, c * P:(c + 1) * P], rhs, start=True, stop=True)
                last.then_inc(S(f"pairs{g}"), 1)
            for g in range(2):
                pe.wait_ge(S(f"inv_start{g}"), c + 1)
                for hh in range(4):
                    last = nc.tensor.transpose(bank[4 * g][:, hh * P:(hh + 1) * P], DT[g][:, hh, :], ident)
                last.then_inc(S(f"inv_flip{g}"), 1)
            for lv in range(6):
                k = 6 * c + lv
                for g in range(2):
                    if lv == 0:
                        pe.wait_ge(S(f"inv_flip_copied{g}"), c + 1)
                    pe.wait_ge(S(f"cross{g}"), k + 1)
                    if lv:
                        pe.wait_ge(S(f"inv{g}"), k)
                    for hh in range(4):
                        last = mm(bank[4 * g + 1][:, hh * P:(hh + 1) * P], CT[g][:, hh, :], DD[g][:, hh, :], start=True, stop=True)
                    last.then_inc(S(f"cd{g}"), 1)
                for g in range(2):
                    pe.wait_ge(S(f"cd_copied{g}"), k + 1)
                    for hh in range(4):
                        mm(bank[4 * g + 2][:, hh * P:(hh + 1) * P], DT[g][:, hh, :], PP[g][:, hh, :], start=True, stop=True)
                        last = mm(bank[4 * g + 3][:, hh * P:(hh + 1) * P], PP[g][:, hh, :], DT[g][:, hh, :], start=True, stop=True)
                    last.then_inc(S(f"dcd{g}"), 1)
            for g in range(2):
                pe.wait_ge(S(f"inv{g}"), 6 * c + 6)
            for h in range(8):
                g, hh, ft, o = h // 4, h % 4, h // 2, (h % 2) * 64
                out = bank[4 * (h % 2)][:, ft * 64:ft * 64 + 64]
                last = mm(out, KA[g][:, hh, :], Vtok[:, c, h * 64:h * 64 + 64], start=True, stop=c == 0)
                if c:
                    last = mm(out, AR[o:o + 64, ft, 1, 0, :], S1[o:o + 64, ft, :], start=False, stop=True)
            last.then_inc(S("g_up"), 1)
            pe.wait_ge(S("g_copied"), c + 1)
            for h in range(8):
                last = mm(bank[1][:, h * 64:h * 64 + 64], DT[h // 4][:, h % 4, :], Gs[:, h * 64:h * 64 + 64], start=True, stop=True)
            last.then_inc(S("u_up"), 1)
            pe.wait_ge(S("u_copied"), c + 1)
            for h in range(8):
                g, hh, ft, o = h // 4, h % 4, h // 2, (h % 2) * 64
                out = bank[2][o:o + 64, ft * P:(ft + 1) * P]
                mm(out, Us[:, h * 64:h * 64 + 64], RB[g][:, hh, :], start=True, stop=False)
                last = mm(out, Vtok[:, c, h * 64:h * 64 + 64], RK[g][:, hh, :], start=False, stop=c == 0)
                if c:
                    last = mm(out, S1[o:o + 64, ft, :], AR[o:o + 64, ft, 1, 1, :], start=False, stop=True)
            last.then_inc(S("y_up"), 1)
            if c == 0:
                for h in range(8):
                    ft, o = h // 2, (h % 2) * 64
                    out = bank[3][o:o + 64, ft * 64:(ft + 1) * 64]
                    mm(out, Btok[:, h * 64:h * 64 + 64], Us[:, h * 64:h * 64 + 64], start=True, stop=False)
                    last = mm(out, Ktok[:, h * 64:h * 64 + 64], Vtok[:, 0, h * 64:h * 64 + 64], start=False, stop=True)
                last.then_inc(S("state_up"), 1)
                pe.wait_ge(S("state_done"), 1)
                pe.wait_ge(S("y_copied"), 1)
        pe.wait_ge(S("y_copied"), 2)
        head_sum("gn_mean", blk64, Y, 4, wait=False)
        head_sum("gn_var", blk64, Vtok_sq, 6)
        barrier(pe, 2)

        head_sum("sbq", blk64, at(W0, 4, T), 0)
        head_sum("sbk", blk64, at(W0 + 1024, 4, T), 2)
        for h in range(SH):
            if h == 0:
                pe.wait_ge(S("sb_normed"), 1)
            if h >= 4:
                pe.wait_ge(S("sbz_taken"), h - 3)
            ft, o, b = h // 2, (h % 2) * 64, 4 + h % 4
            q, k = proj[o:o + 64, 14 + ft, :], proj[o:o + 64, 18 + ft, :]
            mm(bank[b][:, 0:T], k[:, 0:P], q, start=True, stop=True)
            mm(bank[b][:, T:T + P], k[:, P:T], q[:, P:T], start=True, stop=True).then_inc(S("sbz_up"), 1)
        for h in range(SH):
            pe.wait_ge(S("sb_soft"), h // 4 + 1)
            if h >= 4:
                pe.wait_ge(S("sbc_taken"), h - 3)
            b = h % 4
            mm(bank[b][:, 0:P], cst(C_SUFFIX), sbb[:, h, 0:P], start=True, stop=True)
            mm(bank[b][:, P:T], cst(C_SUFFIX), sbb[:, h, P:T], start=True, stop=False)
            mm(bank[b][:, P:T], ones, sbb[:, h, T:zc], start=False, stop=True)
            mm(bank[b][:, T:zc], cst(C_SUFFIX), sbb[:, h, T:zc], start=True, stop=True).then_inc(S("sbc_up"), 1)
        pe.wait_ge(S("sb_attn"), 1)
        for h in range(SH):
            ft, o = h // 2, (h % 2) * 64
            out = bank[4 + ft][o:o + 64, :]
            v0, v1 = sbv[:, ft, 0, o:o + 64], sbv[:, ft, 1, o:o + 64]
            mm(out[:, 0:P], v0, sba[:, h, 0:P], start=True, stop=True)
            mm(out[:, P:T], v0, sba[:, h, P:T], start=True, stop=False)
            mm(out[:, P:T], v1, sba[:, h, T:zc], start=False, stop=True).then_inc(S("sbo_up"), 1)
        barrier(pe, 3)

        def attention(name, n, hd, q, k, v):
            per = P // hd

            def score(h):
                ft, o = h // per, (h % per) * hd
                for tt in range(2):
                    last = mm(bank[h % 2][:, tt * T:(tt + 1) * T], q[o:o + hd, ft, tt * P:(tt + 1) * P], k[o:o + hd, ft, :],
                              start=True, stop=True)
                last.then_inc(S("att_s"), 1)

            score(0)
            score(1)
            for h in range(n):
                ft, o = h // per, (h % per) * hd
                pe.wait_ge(S("att_p"), HEAD0[name] + h + 1)
                for tt in range(2):
                    for mt in range(2):
                        last = nc.tensor.transpose(bank[2 + h % 2][:, mt * T + tt * P:mt * T + (tt + 1) * P],
                                                   att_p[h % 2][:, tt, mt * P:(mt + 1) * P], ident)
                last.then_inc(S("att_t"), 1)
                if h + 2 < n:
                    score(h + 2)
                pe.wait_ge(S("att_tc"), HEAD0[name] + h + 1)
                if h >= 2:
                    pe.wait_ge(S("att_oc"), HEAD0[name] + h - 1)
                for mt in range(2):
                    last = mm(bank[4 + h % 2][o:o + hd, 0:T], v(ft, mt, o), att_t[h % 2][:, mt, :], start=mt == 0, stop=mt == 1)
                last.then_inc(S("att_o"), 1)

        head_sum("mq", ones, at(W0, 4, T), 0)
        head_sum("mk", ones, at(W0 + 1024, 4, T), 2)
        pe.wait_ge(S("mem_normed"), 1)
        attention("mem", MH, MHD, proj[:, 22:26, :], mk, lambda ft, mt, o: mv[:, ft, mt, :])
        barrier(pe, 4)

        for n in range(3):
            if n:
                pe.wait_ge(S("branch_taken"), n)
            wide(PAGE0["branch"] + 4 * n, lambda k, n=n: ys[:, 4 * n + k, :], 4, True, True)
        pe.wait_ge(S("branch_taken"), 3)
        linear("out", merged)
        barrier(pe, 5)
        norm_sum(2)
        pe.wait_ge(S("norm_out"), 3)
        linear("up", hn)
        barrier(pe, 6)
        wide(PAGE0["down"], lambda k: ff[:, k, :], FT, True, True)
        barrier(pe, 7)

        norm_sum(3)
        pe.wait_ge(S("norm_out"), 4)
        linear("in2", hn)
        linear("tok2", hn, by_token=True)
        barrier(pe, 8)
        attention("moba", BH, BHD, pj[:, 0:4, :], pj[:, 4:8, :], lambda ft, mt, o: tok2[:, ft, mt, o:o + 64])
        barrier(pe, 9)
        for lv in range(9):
            pe.wait_ge(S("h_sides"), lv + 1)
            if lv:
                pe.wait_ge(S("h_added"), lv)
            ql, kl = (hq, hk) if lv == 0 else (hQ, hK)
            for tt in range(2 if lv < 8 else 1):
                for h in range(GH):
                    s0, t0 = (tt * P, tt * P) if lv < 8 else (0, P)
                    last = mm(bank[tt][:, h * P:(h + 1) * P], kl[:, h, s0:s0 + P], ql[:, h, t0:t0 + P], start=True, stop=True)
            last.then_inc(S("h_pairs"), 1)
        pe.wait_ge(S("h_added"), 9)
        for h in range(GH):
            out = bank[2 + h // 2]
            c0 = (h % 2) * T
            mm(out[:, c0:c0 + P], tok2[:, 4 + h, 0, :], hacc[:, 0, h, :], start=True, stop=True)
            mm(out[:, c0 + P:c0 + T], tok2[:, 4 + h, 1, :], hacc[:, 1, h, :], start=True, stop=False)
            last = mm(out[:, c0 + P:c0 + T], tok2[:, 4 + h, 0, :], hx[:, h, :], start=False, stop=True)
        last.then_inc(S("h_out"), 1)
        head_sum("hn", ones, hE, 4)
        barrier(pe, 10)
        linear("out2", cat)
        barrier(pe, 11)
        norm_sum(4)
        pe.wait_ge(S("norm_out"), 5)
        linear("wq", hn)
        barrier(pe, 12)
        pe.wait_ge(S("subk_in"), 16)
        for tt in range(2):
            for hc in range(N_WQ):
                last = mm(bank[4 * tt + hc // 4][:, (hc % 4) * NK:(hc % 4 + 1) * NK], qp[:, hc, tt * P:(tt + 1) * P], subk[:, hc, :],
                          start=True, stop=True)
            last.then_inc(S("score_up"), 1)
        pe.wait_ge(S("score_taken"), 2)
        for tt in range(2):
            for k in range(KT):
                last = nc.tensor.transpose(bank[2 * tt + k // 4][:, (k % 4) * P:(k % 4 + 1) * P], hn[:, k, tt * P:(tt + 1) * P], ident)
        last.then_inc(S("htok_up"), 1)
        barrier(pe, 13)
        for tt in range(2):
            y = bank[2 * tt:2 * tt + 2]

            def add(slot, i, start, stop):
                pe.wait_ge(S("diag_ready"), i)
                for j in range(2):
                    last = mm(y[j][:, :], diag[:, slot, :], uv[:, slot, D + j * 512:D + (j + 1) * 512], start=start, stop=stop)
                last.then_inc(S("row_used"), 1)

            for s in range(UVS):
                add(s, tt * P + s + 1, s == 0, False)
            with pe.Fori(1, P // UVS - 1) as i:
                for s in range(UVS):
                    add(s, i * UVS + tt * P + s + 1, False, False)
            for s in range(UVS):
                add(s, tt * P + P - UVS + s + 1, False, s == UVS - 1)
        pe.wait_ge(S("y_tok"), 1)
        for tt in range(2):
            for k in range(KT):
                last = nc.tensor.transpose(bank[4 + k // 2][:, (k % 2) * T + tt * P:(k % 2) * T + (tt + 1) * P],
                                           yt[:, tt, k * P:(k + 1) * P], ident)
        last.then_inc(S("y_feat"), 1)
        norm_sum(5)

    @block.scalar
    def _(act):
        step = chain(act, "act_step")
        A_ = nc.scalar.activation
        act.dma_start(at(W0 + 4096, KT, T), A["memT"]).then_inc(S("mem_in"), 16)
        act.dma_start(lora_w[0:64, 0, :], A["decay_w2"]).then_inc(S("lora_w_in"), 16)
        act.dma_start(lora_w[64:128, 0, :], A["iclr_a2"]).then_inc(S("lora_w_in"), 16)
        act.dma_start(lora_w[:, 1, :], A["gate_g2"]).then_inc(S("lora_w_in"), 16)

        def norm_root(i):
            act.wait_ge(S("norm_mean"), i + 1)
            A_(nroot, nroot, ACT.Sqrt).then_inc(S("norm_root"), 1)

        def head_root(name, dst):
            act.wait_ge(S("head_mean"), ROOT[name])
            A_(dst, dst, ACT.Sqrt).then_inc(S("head_root"), 1)

        def take(stage, dst, func=ACT.Copy):
            page0, n = PAGE0[stage], COUNTS[STAGES.index(stage)]

            def one(b, i=None):
                page = page0 + b
                act.wait_ge(S("page_done"), page + 1 if i is None else i * SLOTS + page + 1)
                out = dst[:, b, :] if i is None else dst[:, bass.ds(i * SLOTS + b, 1), :]
                src = bank[page % SLOTS][:, 0:T]
                A_(out, src if i is None else src.unsqueeze(1), func).then_inc(S("tile_taken"), 1)

            groups = n // SLOTS
            if groups > 1:
                with act.Fori(0, groups) as i:
                    for b in range(SLOTS):
                        one(b, i)
            else:
                for b in range(groups * SLOTS):
                    one(b)
            for b in range(groups * SLOTS, n):
                one(b)

        def flat(v):
            return v.rearrange("p a b c -> p a (b c)")

        act.wait_ge(S("const_in"), 16)
        act.wait_ge(S("vec_in"), 16)
        for _ in range(SLOTS):
            act.drain().then_inc(S("tile_taken"), 1)
        norm_root(0)
        norm_root(1)
        take("in_a", proj)
        take("sbv", flat(sbv))
        act.wait_ge(S("shifted"), 1)
        step(A_(proj[0:64, 12, :], proj[0:64, 12, :], ACT.Tanh))
        A_(proj[:, 13, :], proj[:, 13, :], ACT.Sigmoid).then_inc(S("lora_act"), 1)
        take("mk", mk)
        act.wait_ge(S("lora_up"), 1)
        for ft in range(4):
            col = (ft % 2) * T
            A_(logw[:, ft, :], bank[4 + ft // 2][:, col:col + T], ACT.Sigmoid, bias=V("decay_w0", ft))
            last = A_(iclr[:, ft, :], bank[6 + ft // 2][:, col:col + T], ACT.Sigmoid, bias=V("iclr_a0", ft))
        last.then_inc(S("lora_taken"), 1)
        take("mv", flat(mv))
        act.wait_ge(S("gate_up"), 1)
        A_(gT[:, 0:2, :], two(bank[4][:, :], T), ACT.Copy)
        A_(gT[:, 2:4, :], two(bank[5][:, :], T), ACT.Copy).then_inc(S("gate_taken"), 1)
        head_root("kk", tmp2)
        act.wait_ge(S("cum_ready"), 1)
        A_(tmp1, cc, ACT.Exp).then_inc(S("exp_to"), 1)
        act.wait_ge(S("exp_to_used"), 1)
        A_(tmp2, cc, ACT.Exp, scale=-1.0).then_inc(S("exp_from"), 1)
        A_(tmp3, logw, ACT.Exp).then_inc(S("exp_before"), 1)
        act.wait_ge(S("fac_ready"), 1)
        A_(fac, fac, ACT.Exp).then_inc(S("fac_exp"), 1)
        take("gate", gates, ACT.Sigmoid)
        act.wait_ge(S("vtok"), 1)
        for tt in range(2):
            A_(Vtok[:, tt, :], bank[4 + tt][:, :], ACT.Copy)
        act.wait_ge(S("bktok"), 1)
        A_(Btok, bank[6][:, :], ACT.Copy)
        A_(Ktok, bank[7][:, :], ACT.Copy)
        barrier(act, 1)
        for c in range(2):
            for g in range(2):
                act.wait_ge(S(f"inv_flip{g}"), c + 1)
                A_(DD[g], two(bank[4 * g][:, :], P), ACT.Copy).then_inc(S(f"inv_flip_copied{g}"), 1)
            for lv in range(6):
                for g in range(2):
                    act.wait_ge(S(f"cd{g}"), 6 * c + lv + 1)
                    A_(PP[g], two(bank[4 * g + 1][:, :], P), ACT.Copy).then_inc(S(f"cd_copied{g}"), 1)
            act.wait_ge(S("g_up"), c + 1)
            gp = Gs.rearrange("p (f o i) -> p f o i", o=2, i=64)
            A_(gp[:, :, 0, :], two(bank[0][:, 0:T], 64), ACT.Copy, scale=-1.0)
            A_(gp[:, :, 1, :], two(bank[4][:, 0:T], 64), ACT.Copy, scale=-1.0).then_inc(S("g_copied"), 1)
            act.wait_ge(S("u_up"), c + 1)
            A_(Us, bank[1][:, :], ACT.Copy).then_inc(S("u_copied"), 1)
            act.wait_ge(S("y_up"), c + 1)
            A_(Y[:, :, c * P:(c + 1) * P], two(bank[2][:, :], P), ACT.Copy).then_inc(S("y_copied"), 1)
        head_root("gn_var", tmp2)
        barrier(act, 2)

        head_root("sbq", at(W0, 4, T))
        head_root("sbk", at(W0 + 1024, 4, T))
        for h in range(SH):
            act.wait_ge(S("sbz_up"), h + 1)
            A_(sbz[:, h, :], bank[4 + h % 4][:, 0:zc], ACT.Copy).then_inc(S("sbz_taken"), 1)
        for half in range(2):
            r = slice(4 * half, 4 * half + 4)
            act.wait_ge(S("sb_negabs"), half + 1)
            step(A_(sba[:, r, :], sba[:, r, :], ACT.Exp))
            A_(sba[:, r, :], sba[:, r, :], ACT.Ln, bias=1.0).then_inc(S("sb_log"), 1)
        act.wait_ge(S("sb_logit"), 1)
        A_(sba[:, :, :], sba[:, :, :], ACT.Exp).then_inc(S("sb_exp"), 1)
        for ft in range(4):
            act.wait_ge(S("sbo_up"), 2 * ft + 2)
            A_(ys[:, 4 + ft, :], bank[4 + ft][:, 0:T], ACT.Copy)
        barrier(act, 3)

        def attention(name, n, hd, dst):
            per = P // hd
            for h in range(n + 1):
                if h < n:
                    act.wait_ge(S("att_z"), HEAD0[name] + h + 1)
                    for tt in range(2):
                        last = A_(att_p[h % 2][:, tt, :], att_z[h % 2][:, tt, :], ACT.Exp, bias=att_m[h % 2][:, tt:tt + 1],
                                  accum_out=att_s[h % 2][:, tt:tt + 1])
                    last.then_inc(S("att_e"), 1)
                if h >= 1:
                    g = h - 1
                    ft, o = g // per, (g % per) * hd
                    act.wait_ge(S("att_t"), HEAD0[name] + g + 1)
                    A_(att_t[g % 2], two(bank[2 + g % 2][:, :], T), ACT.Copy).then_inc(S("att_tc"), 1)
                    act.wait_ge(S("att_o"), HEAD0[name] + g + 1)
                    A_(dst[o:o + hd, ft, :], bank[4 + g % 2][o:o + hd, 0:T], ACT.Copy).then_inc(S("att_oc"), 1)

        head_root("mq", at(W0, 4, T))
        head_root("mk", at(W0 + 1024, 4, T))
        attention("mem", MH, MHD, ys[:, 8:12, :])
        barrier(act, 4)
        barrier(act, 5)
        norm_root(2)
        page0 = PAGE0["up"]
        with act.Fori(0, N_UP // 4) as i:
            for b in range(4):
                if b == 0:
                    act.wait_ge(S("glu_done"), i * 2 + 2)
                act.wait_ge(S("page_done"), i * 4 + page0 + b + 1)
                cw = vec[:, bass.ds(i * 4 + VCOL["conv_w2"] + b, 1)]
                cb = vec[:, bass.ds(i * 4 + VCOL["conv_b"] + b, 1)]
                A_(conv_u[:, b, :], bank[(page0 + b) % SLOTS][:, 0:T], ACT.Identity, bias=cb, scale=cw)\
                    .then_inc(S("conv_centre"), 1)
            for pr in range(2):
                act.wait_ge(S("tile_taken"), i * 4 + SLOTS + TILE0["up"] + 2 * pr + 1)
                A_(sig_u[:, pr, :], conv_u[:, 2 * pr, :], ACT.Sigmoid).then_inc(S("glu_sig"), 1)
        barrier(act, 6)
        barrier(act, 7)
        norm_root(3)
        take("in2", pj)
        take("tok2", flat(tok2))
        barrier(act, 8)
        attention("moba", BH, BHD, cat[:, 0:4, :])
        barrier(act, 9)
        act.wait_ge(S("lb_diff"), 1)
        step(A_(lbv[:, 4:8], lbv[:, 0:4], ACT.Sigmoid))
        A_(hE, pj[:, 12:16, :], ACT.Sigmoid)
        A_(hQ, pj[:, 8:12, :], ACT.Sigmoid)
        A_(hK, pj[:, 16:20, :], ACT.Sigmoid).then_inc(S("h_sig"), 1)
        act.wait_ge(S("h_f"), 1)
        A_(hE, hf, ACT.Ln).then_inc(S("h_log"), 1)
        for lv in range(8):
            act.wait_ge(S("h_diff"), lv + 1)
            A_(hE, hE, ACT.Exp).then_inc(S("h_exp"), 1)
        head_root("hn", hE)
        barrier(act, 10)
        barrier(act, 11)
        norm_root(4)
        take("wq", qp)
        act.dma_start(subk, A["subkT"]).then_inc(S("subk_in"), 16)
        barrier(act, 12)
        for tt in range(2):
            act.wait_ge(S("score_up"), tt + 1)
            for b in range(4):
                last = A_(scores[:, tt, 4 * b:4 * b + 4, :], two(bank[4 * tt + b][:, :], NK), ACT.Copy)
            last.then_inc(S("score_taken"), 1)
        act.wait_ge(S("htok_up"), 1)
        for tt in range(2):
            for j in range(2):
                A_(htok[:, tt, j * 512:(j + 1) * 512], bank[2 * tt + j][:, :], ACT.Copy)
        for tt in range(2):
            act.wait_ge(S("soft_in"), tt + 1)
            A_(sel_v[:, tt, :, :], sel_v[:, tt, :, :], ACT.Exp).then_inc(S("soft_exp"), 1)
        barrier(act, 13)
        with act.Fori(0, 2 * P // UVS) as i:
            for s in range(UVS):
                act.wait_ge(S("dot_ready"), i * UVS + s + 1)
                A_(e_gelu[:, s:s + 1], e_act[:, s:s + 1], ACT.Gelu).then_inc(S("gelu_ready"), 1)
        act.wait_ge(S("row_used"), 2 * P)
        for tt in range(2):
            for j in range(2):
                last = A_(yt[:, tt, j * 512:(j + 1) * 512], bank[2 * tt + j][:, :], ACT.Copy)
        last.then_inc(S("y_tok"), 1)
        norm_root(5)

    @block.vector
    def _(dve):
        step = chain(dve, "dve_step")
        v = nc.vector
        tt_ = v.tensor_tensor
        stt = v.scalar_tensor_tensor
        ts = v.tensor_scalar

        def norm(i, src, gain, dst, out_sem="norm_out"):
            tt_(nsq, src, src, ALU.mult).then_inc(S("norm_sq"), 1)
            dve.wait_ge(S("norm_sum"), i + 1)
            ts(nroot, bank[4][:, 0:T], 1.0 / D, 1e-6, ALU.mult, ALU.add).then_inc(S("norm_mean"), 1)
            dve.wait_ge(S("norm_root"), i + 1)
            step(v.reciprocal(ninv, nroot))
            for k in range(KT):
                last = stt(dst[:, k, :], src[:, k, :], V(gain, k), ninv, ALU.mult, ALU.mult)
            last.then_inc(S(out_sem), 1)
            return last

        def head_inv(name, src, sq, root, b0, scale, eps):
            tt_(sq, src, src, ALU.mult).then_inc(S("head_sq"), 1)
            head_inv_rest(name, root, b0, scale, eps)

        def head_inv_rest(name, root, b0, scale, eps):
            dve.wait_ge(S("head_sum"), SUM[name])
            for j in range(2):
                last = ts(root[:, 2 * j:2 * j + 2, :], two(bank[b0 + j][:, :], T), scale, eps, ALU.mult, ALU.add)
            last.then_inc(S("head_mean"), 1)
            dve.wait_ge(S("head_root"), ROOT[name])
            step(v.reciprocal(root, root))

        dve.wait_ge(S("const_in"), 16)
        dve.wait_ge(S("vec_in"), 16)
        dve.wait_ge(S("x_in"), 16)
        norm(0, x, "norm1_g", hn)
        dve.wait_ge(S("norm_out"), 1)
        dve.wait_ge(S("mem_in"), 16)
        norm(1, at(W0 + 4096, KT, T), "mem_g", memn)

        dve.wait_ge(S("tile_taken"), SLOTS + 14)
        tt_(shift_d[:, :, 1:T], proj[:, 0:14, 0:T - 1], proj[:, 0:14, 1:T], ALU.subtract)
        step(ts(shift_d[:, :, 0:1], proj[:, 0:14, 0:1], -1.0, None, ALU.mult))
        for i in list(range(12, 14)) + list(range(12)):
            last = stt(proj[:, i, :], shift_d[:, i, :], V("mu", i), proj[:, i, :], ALU.mult, ALU.add)
        done(dve, last, "shifted", 1)
        for ft in range(4):
            last = ts(kk[:, ft, :], raw_k[:, ft, :], V("k_k", ft), None, ALU.mult)
        step(last)
        tt_(tmp2, kk, kk, ALU.mult).then_inc(S("head_sq"), 1)
        dve.wait_ge(S("lora_taken"), 1)
        for ft in range(4):
            last = ts(tmp1[:, ft, :], iclr[:, ft, :], -1.0, V("k_a", ft), ALU.add, ALU.mult)
        step(last)
        step(stt(raw_k, tmp1, 1.0, raw_k, ALU.add, ALU.mult))
        for ft in range(4):
            last = stt(tmp3[:, ft, :], raw_r[:, ft, :], V("r_k", ft), raw_k[:, ft, :], ALU.mult, ALU.mult)
        last.then_inc(S("head_sq"), 1)
        dve.wait_ge(S("head_sum"), SUM["kk"])
        for j in range(2):
            last = ts(tmp2[:, 2 * j:2 * j + 2, :], two(bank[6 + j][:, :], T), 1e-24, None, ALU.max)
        last.then_inc(S("head_mean"), 1)
        dve.wait_ge(S("head_root"), ROOT["kk"])
        step(v.reciprocal(tmp2, tmp2))
        step(tt_(kk, kk, tmp2, ALU.mult))
        dve.wait_ge(S("head_sum"), SUM["bonus"])
        for j in range(2):
            last = tt_(bonus[:, 2 * j:2 * j + 2, :], two(bank[4 + j][:, :], T), raw_v[:, 2 * j:2 * j + 2, :], ALU.mult)
        last.then_inc(S("bonus_done"), 1)
        step(ts(logw, logw, DECAY_SCALE, None, ALU.mult))
        step(v.memset(tmp1, 1.0))
        for ft in range(4):
            for c in range(2):
                r = slice(c * P, (c + 1) * P)
                last = v.tensor_tensor_scan(cc[:, ft, r], tmp1[:, ft, r], logw[:, ft, r], 0.0, ALU.mult, ALU.add)
        step(last)
        c8 = cc.rearrange("p a (c t) -> p (a c) t", t=P)
        step(v.tensor_copy(mid.unsqueeze(2), c8[:, :, 63:64]))
        step(tt_(c8, c8, each(mid, P), ALU.subtract))
        last = tt_(logw, cc, logw, ALU.subtract)
        done(dve, last, "cum_ready", 1)
        mid2 = mid.rearrange("p (a c) -> p a c", c=2)
        tt_(fac, cc[:, :, P - 1:P], mid2[:, :, 1:2], ALU.add).then_inc(S("fac_ready"), 1)
        dve.wait_ge(S("exp_to"), 1)
        c4 = lambda t_: t_.rearrange("p a (c t) -> p a c t", t=P)
        for ft in range(4):
            last = tt_(AR[:, ft, :, 1, :], c4(raw_r)[:, ft, :, :], c4(tmp1)[:, ft, :, :], ALU.mult)
        last.then_inc(S("exp_to_used"), 1)
        dve.wait_ge(S("exp_from"), 1)
        step(tt_(iclr, iclr, kk, ALU.mult))
        tt_(bT, iclr, tmp2, ALU.mult)
        tt_(kT, raw_k, tmp2, ALU.mult)
        dve.wait_ge(S("exp_before"), 1)
        for ft in range(4):
            last = tt_(AR[:, ft, :, 0, :], c4(kk)[:, ft, :, :], c4(tmp3)[:, ft, :, :], ALU.mult)
        last.then_inc(S("scaled"), 1)
        barrier(dve, 1)

        for c in range(2):
            for g in range(2):
                dve.wait_ge(S(f"pairs{g}"), c + 1)
                for q in range(2):
                    nb = bank[4 * g + q][:, :].rearrange("p (h s t) -> p h s t", h=2, s=2)
                    kb = bank[4 * g + 2 + q][:, :].rearrange("p (h s t) -> p h s t", h=2, s=2)
                    hs = slice(q, 4, 2)
                    stt(MT[g][:, hs, :], nb[:, :, 0, :], -1.0, many(cst(C_STRICT), 2), ALU.mult, ALU.mult)
                    tt_(RB[g][:, hs, :], nb[:, :, 1, :], many(cst(C_INCL), 2), ALU.mult)
                    tt_(KA[g][:, hs, :], kb[:, :, 0, :], many(cst(C_STRICT), 2), ALU.mult)
                    last = tt_(RK[g][:, hs, :], kb[:, :, 1, :], many(cst(C_INCL), 2), ALU.mult)
                step(last)
                step(tt_(DT[g], MT[g], many(cst(C_LEVEL), 4), ALU.mult))
                done(dve, tt_(DT[g], DT[g], many(ident, 4), ALU.add), f"inv_start{g}", c + 1)
                tt_(CT[g], MT[g], many(cst(C_LEVEL + P), 4), ALU.mult).then_inc(S(f"cross{g}"), 1)
            for lv in range(6):
                for g in range(2):
                    dve.wait_ge(S(f"dcd{g}"), 6 * c + lv + 1)
                    tt_(DD[g], DD[g], two(bank[4 * g + 2][:, :], P), ALU.add)
                    tt_(DT[g], DT[g], two(bank[4 * g + 3][:, :], P), ALU.add).then_inc(S(f"inv{g}"), 1)
                    if lv < 5:
                        dve.wait_ge(S(f"inv{g}"), 6 * c + lv + 1)
                        tt_(CT[g], MT[g], many(cst(C_LEVEL + P * (lv + 2)), 4), ALU.mult).then_inc(S(f"cross{g}"), 1)
            if c == 0:
                dve.wait_ge(S("state_up"), 1)
                dve.wait_ge(S("fac_exp"), 1)
                tt_(S1, two(bank[3][:, 0:T], 64), fac.broadcast_to([P, 4, 64]), ALU.mult).then_inc(S("state_done"), 1)
        dve.wait_ge(S("y_copied"), 2)
        dve.wait_ge(S("head_sum"), SUM["gn_mean"])
        for j in range(2):
            last = stt(Y[:, 2 * j:2 * j + 2, :], two(bank[4 + j][:, :], T), -1.0 / RHD, Y[:, 2 * j:2 * j + 2, :], ALU.mult, ALU.add)
        step(last)
        head_inv("gn_var", Y, Vtok_sq, tmp2, 6, 1.0 / RHD, 64e-5)
        step(tt_(Y, Y, tmp2, ALU.mult))
        for ft in range(4):
            last = ts(Y[:, ft, :], Y[:, ft, :], V("lnx_g", ft), V("lnx_b", ft), ALU.mult, ALU.add)
        step(last)
        step(tt_(Y, Y, bonus, ALU.add))
        tt_(ys[:, 0:4, :], Y, gT, ALU.mult)
        barrier(dve, 2)

        sq, sk = proj[:, 14:18, :], proj[:, 18:22, :]
        head_inv("sbq", sq, at(W0, 4, T), at(W0, 4, T), 0, 1.0 / SHD, 1e-6)
        step(stt(sq, sq, V("sb_q_g"), at(W0, 4, T), ALU.mult, ALU.mult))
        head_inv("sbk", sk, at(W0 + 1024, 4, T), at(W0 + 1024, 4, T), 2, 1.0 / SHD, 1e-6)
        stt(sk, sk, V("sb_k_g"), at(W0 + 1024, 4, T), ALU.mult, ALU.mult)
        ts(sq, sq, SHD ** -0.5, None, ALU.mult).then_inc(S("sb_normed"), 1)
        strict8 = lambda n: many(cst(C_STRICT), n)
        for half in range(2):
            r = slice(4 * half, 4 * half + 4)
            dve.wait_ge(S("sbz_taken"), 4 * half + 4)
            stt(sba[:, r, :], sbz[:, r, :], -1.0, sbz[:, r, :], ALU.mult, ALU.min).then_inc(S("sb_negabs"), 1)
            dve.wait_ge(S("sb_log"), half + 1)
            step(stt(sbb[:, r, :], sbz[:, r, :], 0.0, sba[:, r, :], ALU.max, ALU.add))
            tt_(sbb[:, r, 0:P], sbb[:, r, 0:P], strict8(4), ALU.mult)
            tt_(sbb[:, r, T:zc], sbb[:, r, T:zc], strict8(4), ALU.mult).then_inc(S("sb_soft"), 1)
        for h in range(SH):
            dve.wait_ge(S("sbc_up"), h + 1)
            tt_(sba[:, h, :], sbz[:, h, :], bank[h % 4][:, 0:zc], ALU.subtract).then_inc(S("sbc_taken"), 1)
        dve.wait_ge(S("sbc_taken"), SH)
        ts(sba[:, :, :], sba[:, :, :], 0.0, None, ALU.min).then_inc(S("sb_logit"), 1)
        dve.wait_ge(S("sb_exp"), 1)
        tt_(sba[:, :, 0:P], sba[:, :, 0:P], strict8(8), ALU.mult)
        tt_(sba[:, :, T:zc], sba[:, :, T:zc], strict8(8), ALU.mult).then_inc(S("sb_attn"), 1)
        barrier(dve, 3)

        def attention(name, n, scale, bias):
            def head(h):
                z, m = att_z[h % 2], att_m[h % 2]
                dve.wait_ge(S("att_s"), HEAD0[name] + h + 1)
                src = two(bank[h % 2][:, :], T)
                if bias is None:
                    step(ts(z, src, scale, None, ALU.mult))
                else:
                    step(stt(z, src, scale, two(bias[:, h, :], T), ALU.mult, ALU.add))
                step(v.reduce_max(m, z, AX.X))
                ts(m, m, -1.0, None, ALU.mult).then_inc(S("att_z"), 1)

            def share(h):
                dve.wait_ge(S("att_e"), HEAD0[name] + h + 1)
                step(v.reciprocal(att_r[h % 2], att_s[h % 2]))
                tt_(att_p[h % 2], att_p[h % 2], each(att_r[h % 2], T), ALU.mult).then_inc(S("att_p"), 1)

            head(0)
            for h in range(n):
                if h + 1 < n:
                    head(h + 1)
                share(h)

        mq = proj[:, 22:26, :]
        head_inv("mq", mq, at(W0, 4, T), at(W0, 4, T), 0, 1.0 / MHD, 1e-6)
        stt(mq, mq, V("mem_q_g"), at(W0, 4, T), ALU.mult, ALU.mult)
        head_inv("mk", mk, at(W0 + 1024, 4, T), at(W0 + 1024, 4, T), 2, 1.0 / MHD, 1e-6)
        stt(mk, mk, V("mem_k_g"), at(W0 + 1024, 4, T), ALU.mult, ALU.mult).then_inc(S("mem_normed"), 1)
        attention("mem", MH, MHD ** -0.5, None)
        barrier(dve, 4)

        for n in range(3):
            dve.wait_ge(S("page_done"), PAGE0["branch"] + 4 * (n + 1))
            for j in range(KT):
                if n == 0:
                    last = tt_(merged[:, j, :], bank[j][:, 0:T], gates[:, j, :], ALU.mult)
                else:
                    gj = gates[:, 8 * n + j, :]
                    last = tt_(gj, bank[j][:, 0:T], gj, ALU.mult)
            done(dve, last, "branch_read", n + 1)
            if n:
                last = tt_(merged, merged, gates[:, 8 * n:8 * n + 8, :], ALU.add)
            else:
                last = dve.drain()
            done(dve, last, "branch_taken", n + 1)

        def add_tiles(stage):
            for j in range(KT):
                page = PAGE0[stage] + j
                dve.wait_ge(S("page_done"), page + 1)
                tt_(x[:, j, :], bank[page % SLOTS][:, 0:T], x[:, j, :], ALU.add).then_inc(S("tile_taken"), 1)

        add_tiles("out")
        barrier(dve, 5)
        norm(2, x, "norm2_g", hn)
        for _ in range(2):
            dve.drain().then_inc(S("glu_done"), 1)
        with dve.Fori(0, N_UP // 4) as i:
            for b in range(4):
                src = bank[(PAGE0["up"] + b) % SLOTS]
                w1 = vec[:, bass.ds(i * 4 + VCOL["conv_w1"] + b, 1)]
                w0 = vec[:, bass.ds(i * 4 + VCOL["conv_w0"] + b, 1)]
                dve.wait_ge(S("conv_centre"), i * 4 + b + 1)
                stt(conv_u[:, b, 1:T], src[:, 0:T - 1], w1, conv_u[:, b, 1:T], ALU.mult, ALU.add).then_inc(S("conv_tap"), 1)
                dve.wait_ge(S("conv_tap"), i * 4 + b + 1)
                stt(conv_u[:, b, 2:T], src[:, 0:T - 2], w0, conv_u[:, b, 2:T], ALU.mult, ALU.add).then_inc(S("tile_taken"), 1)
            for pr in range(2):
                dve.wait_ge(S("glu_sig"), i * 2 + pr + 1)
                tt_(sig_u[:, pr, :], sig_u[:, pr, :], conv_u[:, 2 * pr, :], ALU.mult).then_inc(S("glu_silu"), 1)
                dve.wait_ge(S("glu_silu"), i * 2 + pr + 1)
                tt_(ff[:, bass.ds(i * 2 + pr, 1), :], sig_u[:, pr:pr + 1, :], conv_u[:, 2 * pr + 1:2 * pr + 2, :], ALU.mult)\
                    .then_inc(S("glu_done"), 1)
        barrier(dve, 6)
        dve.wait_ge(S("page_done"), PAGE0["down"] + N_DOWN)
        for j in range(KT):
            tt_(x[:, j, :], bank[j][:, 0:T], x[:, j, :], ALU.add)
        barrier(dve, 7)

        norm(3, x, "norm1_g_2", hn)
        for h in range(BH):
            ts(bias_h[:, h, :], cst(C_ALIBI, 2 * T), 2.0 ** (-8.0 * (h + 1) / BH), None, ALU.mult)
        barrier(dve, 8)
        attention("moba", BH, BHD ** -0.5, bias_h)
        barrier(dve, 9)
        tt_(lbv[:, 0:4], vec[:, VCOL["lb0"]:VCOL["lb0"] + 4], vec[:, VCOL["lb1"]:VCOL["lb1"] + 4], ALU.subtract)\
            .then_inc(S("lb_diff"), 1)
        dve.wait_ge(S("h_sig"), 1)
        step(ts(lbv[:, 8:12], lbv[:, 4:8], -1.0, 1.0, ALU.mult, ALU.add))
        for h in range(GH):
            last = ts(hf[:, h, :], hE[:, h, :], lbv[:, 8 + h:9 + h], lbv[:, 4 + h:5 + h], ALU.mult, ALU.add)
        done(dve, last, "h_f", 1)
        ts(hk, hf, -1.0, 1.0, ALU.mult, ALU.add)
        tt_(hq, hQ, pj[:, 8:12, :], ALU.mult)
        tt_(pj[:, 16:20, :], hK, pj[:, 16:20, :], ALU.mult).then_inc(S("h_sides"), 1)
        dve.wait_ge(S("h_sides"), 1)
        step(v.memset(hQ, 1.0))
        dve.wait_ge(S("h_log"), 1)
        for h in range(GH):
            last = v.tensor_tensor_scan(hcum[:, h, :], hQ[:, h, :], hE[:, h, :], 0.0, ALU.mult, ALU.add)
        step(last)
        n_exp = 0
        for lv in range(9):
            if lv:
                half = (LEVELS + [P])[lv - 1]
                cb = hcum.rearrange("p h (b c) -> p (h b) c", c=2 * half)
                eb = hE.rearrange("p h (b c) -> p (h b) c", c=2 * half)
                step(tt_(eb, cb, cb[:, :, half - 1:half].broadcast_to([P, cb.shape[1], 2 * half]), ALU.subtract))
                stt(hE, hE, -1.0, hE, ALU.mult, ALU.min).then_inc(S("h_diff"), 1)
                n_exp += 1
                dve.wait_ge(S("h_exp"), n_exp)
                tt_(hQ, hq, hE, ALU.mult)
                done(dve, tt_(hK, hk, hE, ALU.mult), "h_sides", lv + 1)
            dve.wait_ge(S("h_pairs"), lv + 1)
            if lv == 0:
                for tt in range(2):
                    last = tt_(hacc[:, tt, :, :], two(bank[tt][:, :], P), many(ident, 4), ALU.mult)
            elif lv < 8:
                for tt in range(2):
                    step(tt_(hmul, two(bank[tt][:, :], P), many(cst(C_LEVEL + P * (lv - 1)), 4), ALU.mult))
                    last = tt_(hacc[:, tt, :, :], hacc[:, tt, :, :], hmul, ALU.add)
                    if tt == 0:
                        step(last)
            else:
                last = v.tensor_copy(hx, two(bank[0][:, :], P))
            done(dve, last, "h_added", lv + 1)
        dve.wait_ge(S("h_out"), 1)
        for j in range(2):
            last = v.tensor_copy(hf[:, 2 * j:2 * j + 2, :], two(bank[2 + j][:, :], T))
        step(last)
        head_inv("hn", hf, hE, hE, 4, 1.0 / P, 1e-6)
        for h in range(GH):
            last = stt(hf[:, h, :], hf[:, h, :], V("rec_g", h), hE[:, h, :], ALU.mult, ALU.mult)
        step(last)
        tt_(cat[:, 4:8, :], hf, pj[:, 16:20, :], ALU.mult)
        barrier(dve, 10)
        add_tiles("out2")
        barrier(dve, 11)
        norm(4, x, "norm2_g_2", hn)
        barrier(dve, 12)

        for tt in range(2):
            dve.wait_ge(S("score_taken"), tt + 1)
            for hc in range(N_WQ):
                s, tv, ti = scores[:, tt, hc, :], top_v[:, tt, hc, :], top_i[:, tt, hc, :]
                wk = work[:, 0:NK]
                step(v.max(tv[:, 0:8], s))
                v.max_index(ti[:, 0:8], tv[:, 0:8], s)
                step(v.match_replace(wk, tv[:, 0:8], s, -BIG))
                step(v.max(tv[:, 8:16], wk))
                step(v.max_index(ti[:, 8:16], tv[:, 8:16], wk))
            step(v.tensor_copy(top_f[:, tt, :, :], top_i[:, tt, :, :]))
            for h in range(PH):
                c3 = cand[:, h, :].rearrange("p (a b) -> p a b", b=TOPK)
                step(tt_(c3, each(top_v[:, tt, 2 * h, :], TOPK), many(top_v[:, tt, 2 * h + 1, :], TOPK), ALU.add))
                sv, pu = sel_v[:, tt, h, :], pos_u[:, h, :]
                step(v.max(sv[:, 0:8], cand[:, h, :]))
                v.max_index(pu[:, 0:8], sv[:, 0:8], cand[:, h, :])
                step(v.match_replace(work, sv[:, 0:8], cand[:, h, :], -BIG))
                step(v.max(sv[:, 8:16], work))
                step(v.max_index(pu[:, 8:16], sv[:, 8:16], work))
            pf = pos_u.rearrange("p h k -> p (h k)")
            ts(a_u, pf, 4, None, ALU.logical_shift_right)
            step(ts(b_u, pf, 15, None, ALU.bitwise_and))
            v.tensor_copy(a_f, a_u)
            step(v.tensor_copy(b_f, b_u))
            for side, (want, got) in enumerate(((a_f, i_a), (b_f, i_b))):
                step(tt_(eqm, each(want, TOPK), many(cst(C_IOTA, TOPK), P), ALU.is_equal))
                for h in range(PH):
                    eh = eqm[:, h * TOPK:(h + 1) * TOPK, :]
                    last = tt_(eh, eh, many(top_f[:, tt, 2 * h + side, :], TOPK), ALU.mult)
                step(last)
                step(v.reduce_sum(got, eqm, AX.X))
            step(stt(i_a, i_a, float(NK), i_b, ALU.mult, ALU.add))
            step(v.tensor_copy(eidx[:, tt, :], i_a))
            v.tensor_copy(rsum[:, 0:8].unsqueeze(2), sel_v[:, tt, :, 0:1])
            dve.drain().then_inc(S("max_kept"), 1)
            dve.wait_ge(S("max_kept"), tt + 1)
            tt_(sel_v[:, tt, :, :], sel_v[:, tt, :, :], each(rsum[:, 0:8], TOPK), ALU.subtract).then_inc(S("soft_in"), 1)
            dve.wait_ge(S("soft_exp"), tt + 1)
            step(v.reduce_sum(rsum[:, 8:16], sel_v[:, tt, :, :], AX.X))
            step(v.reciprocal(rsum[:, 8:16], rsum[:, 8:16]))
            step(tt_(two(gate_p[:, tt, :], TOPK), sel_v[:, tt, :, :], each(rsum[:, 8:16], TOPK), ALU.mult))
        barrier(dve, 13)

        for tt in range(2):
            with dve.Fori(0, P // UVS) as i:
                for s in range(UVS):
                    n = i * UVS + tt * P + s
                    dve.wait_ge(S(f"row_in{s}"), i * 16 + (tt * (P // UVS) + 1) * 16)
                    stt(junk, uv[:, s, 0:D], 1.0, htok[:, tt, :], ALU.mult, ALU.mult, accum_out=e_act[:, s:s + 1])\
                        .then_inc(S("dot_ready"), 1)
                    dve.wait_ge(S("gelu_ready"), n + 1)
                    ts(diag[:, s, :], ident, e_gelu[:, s:s + 1], gate_p[:, tt, bass.ds(i * UVS + s, 1)], ALU.mult, ALU.mult)\
                        .then_inc(S("diag_ready"), 1)
        dve.wait_ge(S("y_feat"), 1)
        for k in range(4):
            last = tt_(x[:, 2 * k:2 * k + 2, :], two(bank[4 + k][:, :], T), x[:, 2 * k:2 * k + 2, :], ALU.add)
        step(last)
        norm(5, x, "normf_g", hn, "final_out")

    @block.gpsimd
    def _(pool):
        pool.wait_ge(S("phase_done"), 3 * 13)

        def gather(slot, tt, col):
            nc.gpsimd.indirect_dma_start(out=uv[:, slot, :], out_offset=None, in_=A["experts"],
                                         in_offset=bass.IndirectOffsetOnAxis(ap=eidx[:, tt, col], axis=0))\
                .then_inc(S(f"row_in{slot}"), 16)

        for n in range(2 * P):
            s, tt, m = n % UVS, n // P, n % P
            if n >= UVS:
                pool.wait_ge(S("row_used"), n - UVS + 1)
            gather(s, tt, slice(m, m + 1))

    block.__exit__(None, None, None)


def kernel(**inputs):
    import concourse.bacc as _bacc
    from concourse.bass_utils import run_bass_kernel_spmd as _run

    a = {k: np.asarray(v) for k, v in inputs.items()}

    def feat(m):
        r, f = m.shape
        return np.ascontiguousarray(m.reshape(r, f // P, P).transpose(2, 1, 0))

    def cols(m):
        i, o = m.shape
        return m.reshape(i // P, P, o // P, P).transpose(2, 1, 0, 3).reshape(o // P, P, i)

    def rows(m):
        return m.reshape(m.shape[0] // P, P, m.shape[1])

    w_in, w_up, kv, w2 = a["w_in"][0], a["w_up"][0], a["w_mem_kv"][0], a["w_in_2"][0]
    up = cols(w_up)
    up = np.stack([up[:FT], up[FT:]], axis=1).reshape(2 * FT, P, D)
    pages = np.concatenate([
        cols(w_in[:, 0:1792]), cols(w_in[:, 1792:2816]), cols(w_in[:, 3328:3840]),
        cols(w_in[:, 2816:3328]), cols(kv[:, 0:512]), cols(kv[:, 512:1024]), cols(w_in[:, 3840:6912]),
        rows(a["w_branch"][0].reshape(1536, D)), cols(a["w_out"][0]), up, rows(a["w_down"][0]),
        cols(w2[:, 0:1024]), cols(w2[:, 1536:2560]), cols(w2[:, 3072:3584]),
        cols(w2[:, 1024:1536]), cols(w2[:, 2560:3072]), cols(a["w_out_2"][0]), cols(a["peer_wq_2"][0])], axis=0)
    assert pages.shape == (N_PAGES, P, PAGE), pages.shape

    def vcol(m):
        return m.reshape(-1, P).T

    def pairs(m):
        t = m.reshape(2, FT, P).transpose(1, 0, 2).reshape(2 * FT, P)
        return t.T

    lb = a["rec_lb_logits_2"]
    vec = np.concatenate([
        vcol(a["shift_mu"]), vcol(a["norm1_g"]), vcol(a["decay_w0"]), vcol(a["iclr_a0"]), vcol(a["k_k"]), vcol(a["k_a"]),
        vcol(a["r_k"]), vcol(a["lnx_g"]), vcol(a["lnx_b"]), vcol(np.tile(a["sb_q_norm_g"][0], 2)),
        vcol(np.tile(a["sb_k_norm_g"][0], 2)), vcol(a["mem_norm_g"]), vcol(a["mem_q_norm_g"]), vcol(a["mem_k_norm_g"]),
        vcol(a["norm2_g"]), pairs(a["conv_w"][0, 0]), pairs(a["conv_w"][0, 1]), pairs(a["conv_w"][0, 2]), pairs(a["conv_b"][0]),
        vcol(a["norm1_g_2"]), vcol(lb[0]), vcol(lb[1]), vcol(a["rec_norm_g_2"]), vcol(a["norm2_g_2"]), vcol(a["normf_g_2"])],
        axis=1)
    sub = a["peer_subkeys_2"][0].reshape(N_WQ, NK, P).transpose(2, 0, 1)
    dram = {
        "const": constants(), "vec": vec, "xT": feat(a["x"][0]), "memT": feat(a["mem"][0]), "pages": pages,
        "decay_w2": a["decay_w2"][0], "iclr_a2": a["iclr_a2"][0], "gate_g2": a["gate_g2"][0], "subkT": sub,
        "experts": np.concatenate([a["peer_u_2"][0], a["peer_v_2"][0]], axis=1),
    }
    nc = _bacc.Bacc("TRN2", target_bir_lowering=False, num_devices=1)
    arrays, args = {}, {}
    for name, arr in dram.items():
        arr = np.ascontiguousarray(arr)
        arrays[f"in_{name}"] = arr
        args[name] = nc.dram_tensor(f"in_{name}", arr.shape, mybir.dt.from_np(arr.dtype), kind="ExternalInput").ap()
    args["out"] = nc.dram_tensor("out_T", (P, KT, T), F32, kind="ExternalOutput").ap()
    build(nc, args)
    r = _run(nc, [arrays], core_ids=[0])
    out = r.results[0]["out_T"]
    return np.ascontiguousarray(out.transpose(2, 1, 0).reshape(1, T, D))
```

```python
import numpy as np
import concourse.bass as bass
from concourse import mybir

F32 = mybir.dt.float32
U32 = mybir.dt.uint32
ALU = mybir.AluOpType
ACT = mybir.ActivationFunctionType
AX = mybir.AxisListType

P = 128
T = 256
D = 1024
KT = D // P
RH, RHD = 8, 64
SH, SHD = 8, 64
MH, MHD = 4, 128
MEM = 256
FF = 2816
FT = FF // P
BH, BHD = 8, 64
GH = 4
NK, TOPK, PH = 128, 16, 8
SLOTS = 4
PAGE = 8 * P
BIG = 3.0e38
DECAY_SCALE = -float(np.exp(-0.5))

N_IN_A, N_SBV, N_MK, N_MV, N_GATE = 26, 4, 4, 4, 24
N_BR, N_OUT, N_UP, N_DOWN = 12, 8, 2 * FT, FT
N_IN2, N_TOK2, N_OUT2, N_WQ = 20, 8, 8, 16
STAGES = ["in_a", "sbv", "mk", "mv", "gate", "branch", "out", "up", "down", "in2", "tok2", "out2", "wq"]
COUNTS = [N_IN_A, N_SBV, N_MK, N_MV, N_GATE, N_BR, N_OUT, N_UP, N_DOWN, N_IN2, N_TOK2, N_OUT2, N_WQ]
PAGE0 = {s: sum(COUNTS[:i]) for i, s in enumerate(STAGES)}
N_PAGES = sum(COUNTS)
TILED = [s for s in STAGES if s not in ("branch", "down")]
TILE0 = {s: sum(COUNTS[STAGES.index(x)] for x in TILED[:i]) for i, s in enumerate(TILED)}

VECS = [("mu", 14), ("norm1_g", 8), ("decay_w0", 4), ("iclr_a0", 4), ("k_k", 4), ("k_a", 4), ("r_k", 4),
        ("lnx_g", 4), ("lnx_b", 4), ("sb_q_g", 1), ("sb_k_g", 1), ("mem_g", 8), ("mem_q_g", 1), ("mem_k_g", 1),
        ("norm2_g", 8), ("conv_w0", 2 * FT), ("conv_w1", 2 * FT), ("conv_w2", 2 * FT), ("conv_b", 2 * FT),
        ("norm1_g_2", 8), ("lb0", 4), ("lb1", 4), ("rec_g", 4), ("norm2_g_2", 8), ("normf_g", 8)]
VCOL = {n: sum(c for _, c in VECS[:i]) for i, (n, _) in enumerate(VECS)}
N_VEC = sum(c for _, c in VECS)

LEVELS = [1, 2, 4, 8, 16, 32, 64]
C_IDENT, C_ONES, C_BLK64, C_INCL, C_STRICT, C_SUFFIX, C_LEVEL = [P * i for i in range(7)]
C_ALIBI = C_LEVEL + P * len(LEVELS)
C_IOTA = C_ALIBI + 2 * T
N_CONST = C_IOTA + TOPK


SQ = {n: i + 1 for i, n in enumerate(["kk", "bonus", "gn_var", "sbq", "sbk", "mq", "mk", "hn"])}
SUM = {n: i + 1 for i, n in enumerate(["kk", "bonus", "gn_mean", "gn_var", "sbq", "sbk", "mq", "mk", "hn"])}
ROOT = {n: i + 1 for i, n in enumerate(["kk", "gn_var", "sbq", "sbk", "mq", "mk", "hn"])}
HEAD0 = {"mem": 0, "moba": MH}


def constants():
    c = np.zeros((P, N_CONST), np.float32)
    p, f = np.arange(P)[:, None], np.arange(P)[None, :]
    c[:, C_IDENT:C_IDENT + P] = p == f
    c[:, C_ONES:C_ONES + P] = 1
    c[:, C_BLK64:C_BLK64 + P] = p // 64 == f // 64
    c[:, C_INCL:C_INCL + P] = f >= p
    c[:, C_STRICT:C_STRICT + P] = f > p
    c[:, C_SUFFIX:C_SUFFIX + P] = p >= f
    for i, h in enumerate(LEVELS):
        c[:, C_LEVEL + P * i:C_LEVEL + P * (i + 1)] = (p // (2 * h) == f // (2 * h)) & (p % (2 * h) < h) & (f % (2 * h) >= h)
    s = np.arange(T)[None, :]
    for tt in range(2):
        t = p + P * tt
        c[:, C_ALIBI + T * tt:C_ALIBI + T * (tt + 1)] = np.where(s <= t, s - t, -1e30)
    c[:, C_IOTA:C_IOTA + TOPK] = np.arange(TOPK)
    return c


def build(nc, A):
    sems = {}

    def S(name):
        if name not in sems:
            sems[name] = nc.semaphore(name).__enter__()
        return sems[name]

    def sb(name, shape, dt=F32):
        return nc.sbuf_tensor(name, shape, dt).__enter__()[tuple(slice(None) for _ in shape)]

    const = sb("const", [P, N_CONST])
    vec = sb("vec", [P, N_VEC])
    ring = sb("ring", [P, SLOTS, PAGE])
    x = sb("x_res", [P, KT, T])
    hn = sb("h_norm", [P, KT, T])
    ARENA = 41200
    arena = sb("arena", [P, ARENA])
    bank = [nc.psum_tensor(f"bank{i}", [P, 512], F32).__enter__() for i in range(8)]

    def at(off, *shape):
        n = int(np.prod(shape))
        assert off + n <= ARENA, (off, n)
        v = arena[:, off:off + n]
        if len(shape) == 2:
            v = v.rearrange("p (a b) -> p a b", b=shape[1])
        if len(shape) == 3:
            v = v.rearrange("p (a b c) -> p a b c", b=shape[1], c=shape[2])
        if len(shape) == 4:
            v = v.rearrange("p (a b c d) -> p a b c d", b=shape[1], c=shape[2], d=shape[3])
        return v

    def two(ap, b):
        return ap.rearrange("p (a b) -> p a b", b=b)

    def cst(c, n=P):
        return const[:, c:c + n]

    ident, ones, blk64 = cst(C_IDENT), cst(C_ONES), cst(C_BLK64)

    def many(ap, n):
        return ap.unsqueeze(1).broadcast_to([ap.shape[0], n, ap.shape[1]])

    def each(ap, n):
        return ap.unsqueeze(2).broadcast_to([ap.shape[0], ap.shape[1], n])

    def V(name, i=0):
        return vec[:, VCOL[name] + i:VCOL[name] + i + 1]

    memn = at(0, KT, T)
    proj = at(2048, N_IN_A, T)
    sbv = at(8704, 4, 2, P)
    mk = at(9728, 4, T)
    mv = at(10752, 4, 2, P)
    gates = at(11776, N_GATE, T)
    ys = at(17920, 12, T)
    W0 = 20992
    raw_r, raw_k, raw_v = proj[:, 0:4, :], proj[:, 4:8, :], proj[:, 8:12, :]
    tmp1, tmp2, tmp3 = at(W0, 4, T), at(W0 + 1024, 4, T), at(W0 + 2048, 4, T)
    logw, iclr, cc, kk = (at(W0 + 3072 + 1024 * i, 4, T) for i in range(4))
    shift_d = at(W0, 14, T)
    bT, kT, bonus, gT = (at(W0 + 7168 + 1024 * i, 4, T) for i in range(4))
    AR = at(W0 + 11264, 4, 2, 2, P)
    Vtok = at(W0 + 13312, 2, 512)
    Btok, Ktok = at(W0 + 14336, 512), at(W0 + 14848, 512)
    S1 = at(W0 + 15360, 4, 64)
    fac = at(W0 + 15616, 4, 1)
    mid = at(W0 + 15620, 8)
    lora_w = at(W0 + 15640, 2, 512)
    Y = at(W0 + 16664, 4, T)
    free = [W0 + 512 * i for i in range(14)] + [W0 + 17688, W0 + 18200] + [2048 + 512 * i for i in range(6)] \
        + [512 * i for i in range(4)] + [11776 + 8 * T + 512 * i for i in range(6)]
    MT, DD, DT, PP, CT, RB, KA, RK = ([at(free[4 * b + g], 4, P) for g in range(4)] for b in range(8))
    Gs, Us = at(W0 + 18712, 512), at(W0 + 19224, 512)
    Vtok_sq = logw

    nsq, nroot, ninv = at(W0, KT, T), at(W0 + 2048, T), at(W0 + 2304, T)

    zc = 3 * P
    sbz, sba, sbb = at(W0, 8, zc), at(W0 + 3072, 8, zc), at(W0 + 6144, 8, zc)
    att_z = [at(W0 + 10000 + 512 * i, 2, T) for i in range(2)]
    att_p = [at(W0 + 11024 + 512 * i, 2, T) for i in range(2)]
    att_t = [at(W0 + 12048 + 512 * i, 2, T) for i in range(2)]
    att_m = [at(W0 + 13072 + 8 * i, 2) for i in range(2)]
    att_s = [at(W0 + 13090 + 8 * i, 2) for i in range(2)]
    att_r = [at(W0 + 13110 + 8 * i, 2) for i in range(2)]
    merged = at(W0, KT, T)
    gated = at(W0 + 2048, 2, T)

    ff = at(0, FT, T)
    conv_u = at(FT * T, 4, T)
    sig_u = at(FT * T + 1024, 2, T)

    pj = at(0, N_IN2, T)
    tok2 = at(5120, 8, 2, P)
    cat = at(7168, 8, T)
    bias_h = at(9216, 8, 2 * T)
    hw = 13312
    hq, hk, hcum, hE, hQ, hK, hf = (at(hw + 1024 * i, 4, T) for i in range(7))
    hacc = at(hw + 7168, 2, 4, P)
    hx = at(hw + 8192, 4, P)
    hmul = at(hw + 8704, 8, P)
    lbv = at(hw + 9728, 16)
    qp = at(0, N_WQ, T)
    subk = at(4096, N_WQ, NK)
    scores = at(6144, 2, N_WQ, NK)
    work = at(10240, T)
    htok = at(10496, 2, D)
    cand = at(12544, T)
    top_v, top_f = at(12800, 2, TOPK), at(12832, 2, TOPK)
    top_i = at(12864, 2, TOPK).bitcast(U32)
    sel_v, pos_u = at(12896, TOPK), at(12912, TOPK).bitcast(U32)
    place_u, place_f = at(12928, 2, TOPK).bitcast(U32), at(12960, 2, TOPK)
    key_f = at(12992, 2 * TOPK)
    eqm = at(13024, 2, TOPK, TOPK)
    soft = at(13536, 2 * PH, TOPK)
    rsum, rinv = at(13792, 2 * PH), at(13808, 1)
    UVS = 8
    e_act, e_gelu = at(13812, UVS), at(13820, UVS)
    gate_p = at(17280, 2, P)
    eidx = at(17536, 2, P).bitcast(U32)
    junk = at(20384, 1024)
    uv = at(21408, UVS, 2 * D)
    yt = at(37792, 2, D)
    diag = at(39840, UVS, P)

    def done(eng, ins, sem, n):
        ins.then_inc(S(sem), 1)
        eng.wait_ge(S(sem), n)

    def chain(eng, name):
        n = [0]

        def step(ins):
            n[0] += 1
            done(eng, ins, name, n[0])
        return step

    def barrier(eng, k):
        eng.drain().then_inc(S("phase_done"), 1)
        eng.wait_ge(S("phase_done"), 3 * k)

    block = nc.Block().__enter__()

    @block.sync
    def _(sp):
        sp.dma_start(const[:, :], A["const"]).then_inc(S("const_in"), 16)
        sp.dma_start(vec[:, :], A["vec"]).then_inc(S("vec_in"), 16)
        sp.dma_start(x[:, :, :], A["xT"]).then_inc(S("x_in"), 16)

        def load(slot, page, n):
            sp.dma_start(ring[:, slot, :], page).then_inc(S(f"page_in{slot}"), 16)

        for s in range(SLOTS):
            load(s, A["pages"][s], 1)
        with sp.Fori(0, N_PAGES // SLOTS - 1) as i:
            for s in range(SLOTS):
                sp.wait_ge(S("page_done"), i * SLOTS + s + 1)
                load(s, A["pages"][bass.ds(i * SLOTS + s + SLOTS, 1)].rearrange("o p c -> (o p) c"), 1)
        sp.wait_ge(S("final_out"), 1)
        sp.dma_start(A["out"], hn[:, :, :]).then_inc(S("out_stored"), 16)
        sp.wait_ge(S("out_stored"), 16)

    @block.tensor
    def _(pe):
        mm = nc.tensor.matmul

        def page_ready(page, i=None):
            n = page // SLOTS + 1
            pe.wait_ge(S(f"page_in{page % SLOTS}"), 16 * n if i is None else i * 16 + 16 * n)

        def linear(stage, src, by_token=False, part=None):
            first, n = part or (0, COUNTS[STAGES.index(stage)])
            page0, tile0 = PAGE0[stage] + first, TILE0[stage] + first

            def one(b, i=None):
                page, tile = page0 + b, tile0 + b
                page_ready(page, i)
                pe.wait_ge(S("tile_taken"), tile + 1 if i is None else i * SLOTS + tile + 1)
                w, out = ring[:, page % SLOTS, :], bank[page % SLOTS]
                if by_token:
                    for tt in range(2):
                        for k in range(KT):
                            last = mm(out[:, tt * P:(tt + 1) * P], src[:, k, tt * P:(tt + 1) * P], w[:, k * P:(k + 1) * P],
                                      start=k == 0, stop=k == KT - 1)
                else:
                    for k in range(KT):
                        last = mm(out[:, 0:T], w[:, k * P:(k + 1) * P], src[:, k, :], start=k == 0, stop=k == KT - 1)
                last.then_inc(S("page_done"), 1)

            groups = n // SLOTS
            if groups > 1:
                with pe.Fori(0, groups) as i:
                    for b in range(SLOTS):
                        one(b, i)
            else:
                for b in range(groups * SLOTS):
                    one(b)
            for b in range(groups * SLOTS, n):
                one(b)

        def wide(page0, rhs, n, first, last_page):
            for k in range(n):
                page_ready(page0 + k)
                w = ring[:, (page0 + k) % SLOTS, :]
                for j in range(KT):
                    last = mm(bank[j][:, 0:T], w[:, j * P:(j + 1) * P], rhs(k), start=first and k == 0,
                              stop=last_page and k == n - 1)
                last.then_inc(S("page_done"), 1)

        def norm_sum(i):
            pe.wait_ge(S("norm_sq"), i + 1)
            for k in range(KT):
                last = mm(bank[4][:, 0:T], ones, nsq[:, k, :], start=k == 0, stop=k == KT - 1)
            last.then_inc(S("norm_sum"), 1)

        def head_sum(name, mat, src, b0, wait=True):
            if wait:
                pe.wait_ge(S("head_sq"), SQ[name])
            for j in range(2):
                last = mm(bank[b0 + j][:, :], mat, src[:, 2 * j:2 * j + 2, :], start=True, stop=True)
            last.then_inc(S("head_sum"), 1)

        pe.wait_ge(S("const_in"), 16)
        norm_sum(0)
        norm_sum(1)
        pe.wait_ge(S("norm_out"), 2)
        linear("in_a", hn)
        pe.wait_ge(S("lora_w_in"), 48)
        pe.wait_ge(S("lora_act"), 1)
        for ft in range(4):
            mm(bank[4 + ft // 2][:, (ft % 2) * T:(ft % 2) * T + T], lora_w[0:64, 0, ft * P:(ft + 1) * P], proj[0:64, 12, :],
               start=True, stop=True)
            last = mm(bank[6 + ft // 2][:, (ft % 2) * T:(ft % 2) * T + T], lora_w[64:128, 0, ft * P:(ft + 1) * P],
                      proj[64:128, 12, :], start=True, stop=True)
        last.then_inc(S("lora_up"), 1)
        linear("sbv", hn, by_token=True)
        linear("mk", memn)
        pe.wait_ge(S("lora_taken"), 1)
        for ft in range(4):
            last = mm(bank[4 + ft // 2][:, (ft % 2) * T:(ft % 2) * T + T], lora_w[:, 1, ft * P:(ft + 1) * P], proj[:, 13, :],
                      start=True, stop=True)
        last.then_inc(S("gate_up"), 1)
        head_sum("kk", blk64, tmp2, 6)
        pe.wait_ge(S("gate_taken"), 1)
        head_sum("bonus", blk64, tmp3, 4)
        linear("mv", memn, by_token=True)
        linear("gate", hn, part=(0, 8))
        pe.wait_ge(S("bonus_done"), 1)
        for tt in range(2):
            for ft in range(4):
                last = nc.tensor.transpose(bank[4 + tt][:, ft * P:(ft + 1) * P], raw_v[:, ft, tt * P:(tt + 1) * P], ident)
        last.then_inc(S("vtok"), 1)
        pe.wait_ge(S("scaled"), 1)
        for ft in range(4):
            nc.tensor.transpose(bank[6][:, ft * P:(ft + 1) * P], bT[:, ft, 0:P], ident)
            last = nc.tensor.transpose(bank[7][:, ft * P:(ft + 1) * P], kT[:, ft, 0:P], ident)
        last.then_inc(S("bktok"), 1)
        barrier(pe, 1)
        for side, src in enumerate((bT, kT)):
            for G in range(4):
                if side:
                    pe.wait_ge(S("pairs_read"), G + 1)
                for hh in range(4):
                    h, c = 4 * (G % 2) + hh, G // 2
                    ft, o = h // 2, (h % 2) * 64
                    last = mm(bank[2 * G + hh % 2][:, (hh // 2) * T:(hh // 2 + 1) * T], src[o:o + 64, ft, c * P:(c + 1) * P],
                              AR[o:o + 64, ft, c, :, :], start=True, stop=True)
                last.then_inc(S("pairs"), 1)
        for G in range(4):
            pe.wait_ge(S("inv_start"), G + 1)
            pe.wait_ge(S("pairs_read"), 4 + G + 1)
            for hh in range(4):
                last = nc.tensor.transpose(bank[2 * G][:, hh * P:(hh + 1) * P], DT[G][:, hh, :], ident)
            last.then_inc(S("inv_flip"), 1)
        for lv in range(6):
            for G in range(4):
                if lv == 0:
                    pe.wait_ge(S("inv_flip_copied"), G + 1)
                else:
                    pe.wait_ge(S("inv"), 4 * (lv - 1) + G + 1)
                pe.wait_ge(S("cross"), 4 * lv + G + 1)
                for hh in range(4):
                    last = mm(bank[2 * G][:, hh * P:(hh + 1) * P], CT[G][:, hh, :], DD[G][:, hh, :], start=True, stop=True)
                last.then_inc(S("cd"), 1)
            for G in range(4):
                pe.wait_ge(S("cd_copied"), 4 * lv + G + 1)
                if lv < 5:
                    for hh in range(4):
                        mm(bank[2 * G + 1][:, hh * P:(hh + 1) * P], DT[G][:, hh, :], PP[G][:, hh, :], start=True, stop=True)
                for hh in range(4):
                    last = mm(bank[2 * G][:, hh * P:(hh + 1) * P], PP[G][:, hh, :], DT[G][:, hh, :], start=True, stop=True)
                last.then_inc(S("dcd"), 1)
        pe.wait_ge(S("inv"), 24)
        for c in range(2):
            for h in range(8):
                g, hh, ft, o = 2 * c + h // 4, h % 4, h // 2, (h % 2) * 64
                out = bank[4 * (h % 2)][:, ft * 64:ft * 64 + 64]
                last = mm(out, KA[g][:, hh, :], Vtok[:, c, h * 64:h * 64 + 64], start=True, stop=c == 0)
                if c:
                    last = mm(out, AR[o:o + 64, ft, 1, 0, :], S1[o:o + 64, ft, :], start=False, stop=True)
            last.then_inc(S("g_up"), 1)
            pe.wait_ge(S("g_copied"), c + 1)
            for h in range(8):
                last = mm(bank[1][:, h * 64:h * 64 + 64], DT[2 * c + h // 4][:, h % 4, :], Gs[:, h * 64:h * 64 + 64], start=True, stop=True)
            last.then_inc(S("u_up"), 1)
            pe.wait_ge(S("u_copied"), c + 1)
            for h in range(8):
                g, hh, ft, o = 2 * c + h // 4, h % 4, h // 2, (h % 2) * 64
                out = bank[2][o:o + 64, ft * P:(ft + 1) * P]
                mm(out, Us[:, h * 64:h * 64 + 64], RB[g][:, hh, :], start=True, stop=False)
                last = mm(out, Vtok[:, c, h * 64:h * 64 + 64], RK[g][:, hh, :], start=False, stop=c == 0)
                if c:
                    last = mm(out, S1[o:o + 64, ft, :], AR[o:o + 64, ft, 1, 1, :], start=False, stop=True)
            last.then_inc(S("y_up"), 1)
            if c == 0:
                for h in range(8):
                    ft, o = h // 2, (h % 2) * 64
                    out = bank[3][o:o + 64, ft * 64:(ft + 1) * 64]
                    mm(out, Btok[:, h * 64:h * 64 + 64], Us[:, h * 64:h * 64 + 64], start=True, stop=False)
                    last = mm(out, Ktok[:, h * 64:h * 64 + 64], Vtok[:, 0, h * 64:h * 64 + 64], start=False, stop=True)
                last.then_inc(S("state_up"), 1)
                pe.wait_ge(S("state_done"), 1)
                pe.wait_ge(S("y_copied"), 1)
        pe.wait_ge(S("y_copied"), 2)
        head_sum("gn_mean", blk64, Y, 4, wait=False)
        head_sum("gn_var", blk64, Vtok_sq, 6)
        barrier(pe, 2)

        head_sum("sbq", blk64, at(W0, 4, T), 4)
        head_sum("sbk", blk64, at(W0 + 1024, 4, T), 6)
        linear("gate", hn, part=(8, 4))
        pe.wait_ge(S("sb_normed"), 1)
        for h in range(SH):
            if h >= 4:
                pe.wait_ge(S("sbz_taken"), h - 3)
            ft, o, b = h // 2, (h % 2) * 64, 4 + h % 4
            q, k = proj[o:o + 64, 14 + ft, :], proj[o:o + 64, 18 + ft, :]
            mm(bank[b][:, 0:T], k[:, 0:P], q, start=True, stop=True)
            mm(bank[b][:, T:T + P], k[:, P:T], q[:, P:T], start=True, stop=True).then_inc(S("sbz_up"), 1)
        linear("gate", hn, part=(12, 4))
        for h in range(SH):
            pe.wait_ge(S("sb_soft"), h // 4 + 1)
            if h >= 4:
                pe.wait_ge(S("sbc_taken"), h - 3)
            b = 4 + h % 4
            mm(bank[b][:, 0:P], cst(C_SUFFIX), sbb[:, h, 0:P], start=True, stop=True)
            mm(bank[b][:, P:T], cst(C_SUFFIX), sbb[:, h, P:T], start=True, stop=False)
            mm(bank[b][:, P:T], ones, sbb[:, h, T:zc], start=False, stop=True)
            mm(bank[b][:, T:zc], cst(C_SUFFIX), sbb[:, h, T:zc], start=True, stop=True).then_inc(S("sbc_up"), 1)
        linear("gate", hn, part=(16, 4))
        pe.wait_ge(S("sb_attn"), 1)
        for h in range(SH):
            ft, o = h // 2, (h % 2) * 64
            out = bank[4 + ft][o:o + 64, :]
            v0, v1 = sbv[:, ft, 0, o:o + 64], sbv[:, ft, 1, o:o + 64]
            mm(out[:, 0:P], v0, sba[:, h, 0:P], start=True, stop=True)
            mm(out[:, P:T], v0, sba[:, h, P:T], start=True, stop=False)
            mm(out[:, P:T], v1, sba[:, h, T:zc], start=False, stop=True).then_inc(S("sbo_up"), 1)
        pe.wait_ge(S("sbo_taken"), 1)
        head_sum("mq", ones, at(W0 + 9216, 4, T), 4)
        head_sum("mk", ones, at(W0 + 10240, 4, T), 6)
        linear("gate", hn, part=(20, 4))

        def att_score(name, n, hd, q, k, h):
            ft, o = h // (P // hd), (h % (P // hd)) * hd
            for tt in range(2):
                last = mm(bank[4 + h % 2][:, tt * T:(tt + 1) * T], q[o:o + hd, ft, tt * P:(tt + 1) * P], k[o:o + hd, ft, :],
                          start=True, stop=True)
            last.then_inc(S("att_s"), 1)

        def att_out(name, n, hd, q, k, v, h):
            ft, o = h // (P // hd), (h % (P // hd)) * hd
            pe.wait_ge(S("att_p"), HEAD0[name] + h + 1)
            for tt in range(2):
                for mt in range(2):
                    last = nc.tensor.transpose(bank[6][:, mt * T + tt * P:mt * T + (tt + 1) * P],
                                               att_p[h % 2][:, tt, mt * P:(mt + 1) * P], ident)
            last.then_inc(S("att_t"), 1)
            if h + 2 < n:
                att_score(name, n, hd, q, k, h + 2)
            pe.wait_ge(S("att_tc"), HEAD0[name] + h + 1)
            if h >= 1:
                pe.wait_ge(S("att_oc"), HEAD0[name] + h)
            for mt in range(2):
                last = mm(bank[7][o:o + hd, 0:T], v(ft, mt, o), att_t[h % 2][:, mt, :], start=mt == 0, stop=mt == 1)
            last.then_inc(S("att_o"), 1)

        mem = ("mem", MH, MHD, proj[:, 22:26, :], mk)
        pe.wait_ge(S("mem_normed"), 1)
        att_score(*mem, 0)
        att_score(*mem, 1)
        for h in range(MH):
            att_out(*mem, lambda ft, mt, o: mv[:, ft, mt, :], h)
        barrier(pe, 3)

        for n in range(3):
            if n:
                pe.wait_ge(S("branch_taken"), n)
            wide(PAGE0["branch"] + 4 * n, lambda k, n=n: ys[:, 4 * n + k, :], 4, True, True)
        pe.wait_ge(S("branch_taken"), 3)
        linear("out", merged)
        barrier(pe, 4)
        norm_sum(2)
        pe.wait_ge(S("norm_out"), 3)
        linear("up", hn)
        barrier(pe, 5)
        wide(PAGE0["down"], lambda k: ff[:, k, :], FT, True, True)
        barrier(pe, 6)

        norm_sum(3)
        pe.wait_ge(S("norm_out"), 4)
        linear("in2", hn)
        linear("tok2", hn, by_token=True)
        barrier(pe, 7)
        moba = ("moba", BH, BHD, pj[:, 0:4, :], pj[:, 4:8, :])
        att_score(*moba, 0)
        att_score(*moba, 1)
        for lv in range(9):
            pe.wait_ge(S("h_sides"), lv + 1)
            if lv:
                pe.wait_ge(S("h_added"), lv)
            ql, kl = (hq, hk) if lv == 0 else (hQ, hK)
            for tt in range(2 if lv < 8 else 1):
                for h in range(GH):
                    s0, t0 = (tt * P, tt * P) if lv < 8 else (0, P)
                    last = mm(bank[tt][:, h * P:(h + 1) * P], kl[:, h, s0:s0 + P], ql[:, h, t0:t0 + P], start=True, stop=True)
            last.then_inc(S("h_pairs"), 1)
            if lv < BH:
                att_out(*moba, lambda ft, mt, o: tok2[:, ft, mt, o:o + 64], lv)
        pe.wait_ge(S("h_added"), 9)
        for h in range(GH):
            out = bank[2 + h // 2]
            c0 = (h % 2) * T
            mm(out[:, c0:c0 + P], tok2[:, 4 + h, 0, :], hacc[:, 0, h, :], start=True, stop=True)
            mm(out[:, c0 + P:c0 + T], tok2[:, 4 + h, 1, :], hacc[:, 1, h, :], start=True, stop=False)
            last = mm(out[:, c0 + P:c0 + T], tok2[:, 4 + h, 0, :], hx[:, h, :], start=False, stop=True)
        last.then_inc(S("h_out"), 1)
        head_sum("hn", ones, hE, 0)
        barrier(pe, 8)
        linear("out2", cat)
        barrier(pe, 9)
        norm_sum(4)
        pe.wait_ge(S("norm_out"), 5)
        linear("wq", hn)
        barrier(pe, 10)
        pe.wait_ge(S("subk_in"), 16)
        for tt in range(2):
            for hc in range(N_WQ):
                last = mm(bank[4 * tt + hc // 4][:, (hc % 4) * NK:(hc % 4 + 1) * NK], qp[:, hc, tt * P:(tt + 1) * P], subk[:, hc, :],
                          start=True, stop=True)
                if hc % 4 == 3:
                    last.then_inc(S("score_up"), 1)
        pe.wait_ge(S("score_taken"), 8)
        for tt in range(2):
            for k in range(KT):
                last = nc.tensor.transpose(bank[2 * tt + k // 4][:, (k % 4) * P:(k % 4 + 1) * P], hn[:, k, tt * P:(tt + 1) * P], ident)
        last.then_inc(S("htok_up"), 1)
        for tt in range(2):
            y = bank[2 * tt:2 * tt + 2]

            def add(slot, i, start, stop):
                pe.wait_ge(S("diag_ready"), i)
                for j in range(2):
                    last = mm(y[j][:, :], diag[:, slot, :], uv[:, slot, D + j * 512:D + (j + 1) * 512], start=start, stop=stop)
                last.then_inc(S("row_used"), 1)

            for s in range(UVS):
                add(s, tt * P + s + 1, s == 0, False)
            with pe.Fori(1, P // UVS - 1) as i:
                for s in range(UVS):
                    add(s, i * UVS + tt * P + s + 1, False, False)
            for s in range(UVS):
                add(s, tt * P + P - UVS + s + 1, False, s == UVS - 1)
        pe.wait_ge(S("y_tok"), 1)
        for tt in range(2):
            for k in range(KT):
                last = nc.tensor.transpose(bank[4 + k // 2][:, (k % 2) * T + tt * P:(k % 2) * T + (tt + 1) * P],
                                           yt[:, tt, k * P:(k + 1) * P], ident)
        last.then_inc(S("y_feat"), 1)
        norm_sum(5)

    @block.scalar
    def _(act):
        step = chain(act, "act_step")
        A_ = nc.scalar.activation
        act.dma_start(at(W0 + 4096, KT, T), A["memT"]).then_inc(S("mem_in"), 16)
        act.dma_start(lora_w[0:64, 0, :], A["decay_w2"]).then_inc(S("lora_w_in"), 16)
        act.dma_start(lora_w[64:128, 0, :], A["iclr_a2"]).then_inc(S("lora_w_in"), 16)
        act.dma_start(lora_w[:, 1, :], A["gate_g2"]).then_inc(S("lora_w_in"), 16)

        def norm_root(i):
            act.wait_ge(S("norm_mean"), i + 1)
            A_(nroot, nroot, ACT.Sqrt).then_inc(S("norm_root"), 1)

        def head_root(name, dst):
            act.wait_ge(S("head_mean"), ROOT[name])
            A_(dst, dst, ACT.Sqrt).then_inc(S("head_root"), 1)

        def take(stage, dst, func=ACT.Copy, part=None):
            first, n = part or (0, COUNTS[STAGES.index(stage)])
            page0 = PAGE0[stage] + first
            dst = dst[:, first:first + n, :]

            def one(b, i=None):
                page = page0 + b
                act.wait_ge(S("page_done"), page + 1 if i is None else i * SLOTS + page + 1)
                out = dst[:, b, :] if i is None else dst[:, bass.ds(i * SLOTS + b, 1), :]
                src = bank[page % SLOTS][:, 0:T]
                A_(out, src if i is None else src.unsqueeze(1), func).then_inc(S("tile_taken"), 1)

            groups = n // SLOTS
            if groups > 1:
                with act.Fori(0, groups) as i:
                    for b in range(SLOTS):
                        one(b, i)
            else:
                for b in range(groups * SLOTS):
                    one(b)
            for b in range(groups * SLOTS, n):
                one(b)

        def flat(v):
            return v.rearrange("p a b c -> p a (b c)")

        act.wait_ge(S("const_in"), 16)
        act.wait_ge(S("vec_in"), 16)
        for _ in range(SLOTS):
            act.drain().then_inc(S("tile_taken"), 1)
        norm_root(0)
        norm_root(1)
        take("in_a", proj)
        act.wait_ge(S("shifted"), 1)
        step(A_(proj[0:64, 12, :], proj[0:64, 12, :], ACT.Tanh))
        A_(proj[:, 13, :], proj[:, 13, :], ACT.Sigmoid).then_inc(S("lora_act"), 1)
        act.wait_ge(S("lora_up"), 1)
        for ft in range(4):
            col = (ft % 2) * T
            A_(logw[:, ft, :], bank[4 + ft // 2][:, col:col + T], ACT.Sigmoid, bias=V("decay_w0", ft))
            last = A_(iclr[:, ft, :], bank[6 + ft // 2][:, col:col + T], ACT.Sigmoid, bias=V("iclr_a0", ft))
        last.then_inc(S("lora_taken"), 1)
        take("sbv", flat(sbv))
        take("mk", mk)
        act.wait_ge(S("gate_up"), 1)
        A_(gT[:, 0:2, :], two(bank[4][:, :], T), ACT.Copy)
        A_(gT[:, 2:4, :], two(bank[5][:, :], T), ACT.Copy).then_inc(S("gate_taken"), 1)
        head_root("kk", tmp2)
        take("mv", flat(mv))
        act.wait_ge(S("cum_ready"), 1)
        A_(tmp1, cc, ACT.Exp).then_inc(S("exp_to"), 1)
        act.wait_ge(S("exp_to_used"), 1)
        A_(tmp2, cc, ACT.Exp, scale=-1.0).then_inc(S("exp_from"), 1)
        A_(tmp3, logw, ACT.Exp).then_inc(S("exp_before"), 1)
        act.wait_ge(S("fac_ready"), 1)
        A_(fac, fac, ACT.Exp).then_inc(S("fac_exp"), 1)
        take("gate", gates, ACT.Sigmoid, part=(0, 8))
        act.wait_ge(S("vtok"), 1)
        for tt in range(2):
            A_(Vtok[:, tt, :], bank[4 + tt][:, :], ACT.Copy)
        act.wait_ge(S("bktok"), 1)
        A_(Btok, bank[6][:, :], ACT.Copy)
        A_(Ktok, bank[7][:, :], ACT.Copy)
        barrier(act, 1)
        for G in range(4):
            act.wait_ge(S("inv_flip"), G + 1)
            A_(DD[G], two(bank[2 * G][:, :], P), ACT.Copy).then_inc(S("inv_flip_copied"), 1)
        for lv in range(6):
            for G in range(4):
                act.wait_ge(S("cd"), 4 * lv + G + 1)
                A_(PP[G], two(bank[2 * G][:, :], P), ACT.Copy).then_inc(S("cd_copied"), 1)
        for c in range(2):
            act.wait_ge(S("g_up"), c + 1)
            gp = Gs.rearrange("p (f o i) -> p f o i", o=2, i=64)
            A_(gp[:, :, 0, :], two(bank[0][:, 0:T], 64), ACT.Copy, scale=-1.0)
            A_(gp[:, :, 1, :], two(bank[4][:, 0:T], 64), ACT.Copy, scale=-1.0).then_inc(S("g_copied"), 1)
            act.wait_ge(S("u_up"), c + 1)
            A_(Us, bank[1][:, :], ACT.Copy).then_inc(S("u_copied"), 1)
            act.wait_ge(S("y_up"), c + 1)
            A_(Y[:, :, c * P:(c + 1) * P], two(bank[2][:, :], P), ACT.Copy).then_inc(S("y_copied"), 1)
        head_root("gn_var", tmp2)
        barrier(act, 2)

        head_root("sbq", at(W0, 4, T))
        head_root("sbk", at(W0 + 1024, 4, T))
        take("gate", gates, ACT.Sigmoid, part=(8, 4))
        for h in range(SH):
            act.wait_ge(S("sbz_up"), h + 1)
            A_(sbz[:, h, :], bank[4 + h % 4][:, 0:zc], ACT.Copy).then_inc(S("sbz_taken"), 1)
        for half in range(2):
            r = slice(4 * half, 4 * half + 4)
            act.wait_ge(S("sb_negabs"), half + 1)
            step(A_(sba[:, r, :], sba[:, r, :], ACT.Exp))
            A_(sba[:, r, :], sba[:, r, :], ACT.Ln, bias=1.0).then_inc(S("sb_log"), 1)
        take("gate", gates, ACT.Sigmoid, part=(12, 4))
        act.wait_ge(S("sb_logit"), 1)
        A_(sba[:, :, :], sba[:, :, :], ACT.Exp).then_inc(S("sb_exp"), 1)
        take("gate", gates, ACT.Sigmoid, part=(16, 4))
        for ft in range(4):
            act.wait_ge(S("sbo_up"), 2 * ft + 2)
            last = A_(ys[:, 4 + ft, :], bank[4 + ft][:, 0:T], ACT.Copy)
        last.then_inc(S("sbo_taken"), 1)

        def att_exp(name, h):
            act.wait_ge(S("att_z"), HEAD0[name] + h + 1)
            for tt in range(2):
                last = A_(att_p[h % 2][:, tt, :], att_z[h % 2][:, tt, :], ACT.Exp, bias=att_m[h % 2][:, tt:tt + 1],
                          accum_out=att_s[h % 2][:, tt:tt + 1])
            last.then_inc(S("att_e"), 1)

        def att_take(name, hd, dst, h):
            ft, o = h // (P // hd), (h % (P // hd)) * hd
            act.wait_ge(S("att_t"), HEAD0[name] + h + 1)
            A_(att_t[h % 2], two(bank[6][:, :], T), ACT.Copy).then_inc(S("att_tc"), 1)
            act.wait_ge(S("att_o"), HEAD0[name] + h + 1)
            A_(dst[o:o + hd, ft, :], bank[7][o:o + hd, 0:T], ACT.Copy).then_inc(S("att_oc"), 1)

        head_root("mq", at(W0 + 9216, 4, T))
        head_root("mk", at(W0 + 10240, 4, T))
        take("gate", gates, ACT.Sigmoid, part=(20, 4))
        att_exp("mem", 0)
        for h in range(MH):
            if h + 1 < MH:
                att_exp("mem", h + 1)
            att_take("mem", MHD, ys[:, 8:12, :], h)
        barrier(act, 3)
        barrier(act, 4)
        norm_root(2)
        page0 = PAGE0["up"]
        with act.Fori(0, N_UP // 4) as i:
            for b in range(4):
                if b == 0:
                    act.wait_ge(S("glu_done"), i * 2 + 2)
                act.wait_ge(S("page_done"), i * 4 + page0 + b + 1)
                cw = vec[:, bass.ds(i * 4 + VCOL["conv_w2"] + b, 1)]
                cb = vec[:, bass.ds(i * 4 + VCOL["conv_b"] + b, 1)]
                A_(conv_u[:, b, :], bank[(page0 + b) % SLOTS][:, 0:T], ACT.Identity, bias=cb, scale=cw)\
                    .then_inc(S("conv_centre"), 1)
            for pr in range(2):
                act.wait_ge(S("tile_taken"), i * 4 + SLOTS + TILE0["up"] + 2 * pr + 1)
                A_(sig_u[:, pr, :], conv_u[:, 2 * pr, :], ACT.Sigmoid).then_inc(S("glu_sig"), 1)
        barrier(act, 5)
        barrier(act, 6)
        norm_root(3)
        take("in2", pj)
        act.wait_ge(S("tile_taken"), SLOTS + TILE0["in2"] + N_IN2)
        act.wait_ge(S("lb_diff"), 1)
        A_(hE, pj[:, 12:16, :], ACT.Sigmoid)
        A_(hQ, pj[:, 8:12, :], ACT.Sigmoid)
        A_(hK, pj[:, 16:20, :], ACT.Sigmoid)
        A_(lbv[:, 4:8], lbv[:, 0:4], ACT.Sigmoid).then_inc(S("h_sig"), 1)
        take("tok2", flat(tok2))
        act.wait_ge(S("h_f"), 1)
        A_(hE, hf, ACT.Ln).then_inc(S("h_log"), 1)
        barrier(act, 7)
        att_exp("moba", 0)
        for lv in range(9):
            if lv < 8:
                act.wait_ge(S("h_diff"), lv + 1)
                A_(hE, hE, ACT.Exp).then_inc(S("h_exp"), 1)
                if lv + 1 < BH:
                    att_exp("moba", lv + 1)
                att_take("moba", BHD, cat[:, 0:4, :], lv)
        head_root("hn", hE)
        barrier(act, 8)
        barrier(act, 9)
        norm_root(4)
        take("wq", qp)
        act.dma_start(subk, A["subkT"]).then_inc(S("subk_in"), 16)
        barrier(act, 10)
        for q in range(8):
            act.wait_ge(S("score_up"), q + 1)
            A_(scores[:, q // 4, 4 * (q % 4):4 * (q % 4) + 4, :], two(bank[q][:, :], NK), ACT.Copy).then_inc(S("score_taken"), 1)
        act.wait_ge(S("htok_up"), 1)
        for tt in range(2):
            for j in range(2):
                last = A_(htok[:, tt, j * 512:(j + 1) * 512], bank[2 * tt + j][:, :], ACT.Copy)
        last.then_inc(S("htok_in"), 1)

        def soft_exp(j):
            act.wait_ge(S("soft_in"), j + 1)
            A_(soft[:, j, :], soft[:, j, :], ACT.Exp, accum_out=rsum[:, j:j + 1]).then_inc(S("soft_exp"), 1)

        soft_exp(0)
        soft_exp(1)
        for j in range(2 * PH):
            with act.Fori(0, TOPK // UVS) as i:
                for s in range(UVS):
                    act.wait_ge(S("dot_ready"), i * UVS + j * TOPK + s + 1)
                    A_(e_gelu[:, s:s + 1], e_act[:, s:s + 1], ACT.Gelu).then_inc(S("gelu_ready"), 1)
            if j + 2 < 2 * PH:
                soft_exp(j + 2)
        act.wait_ge(S("row_used"), 2 * P)
        for tt in range(2):
            for j in range(2):
                last = A_(yt[:, tt, j * 512:(j + 1) * 512], bank[2 * tt + j][:, :], ACT.Copy)
        last.then_inc(S("y_tok"), 1)
        norm_root(5)

    @block.vector
    def _(dve):
        step = chain(dve, "dve_step")
        v = nc.vector
        tt_ = v.tensor_tensor
        stt = v.scalar_tensor_tensor
        ts = v.tensor_scalar

        def norm(i, src, gain, dst, out_sem="norm_out"):
            tt_(nsq, src, src, ALU.mult).then_inc(S("norm_sq"), 1)
            dve.wait_ge(S("norm_sum"), i + 1)
            ts(nroot, bank[4][:, 0:T], 1.0 / D, 1e-6, ALU.mult, ALU.add).then_inc(S("norm_mean"), 1)
            dve.wait_ge(S("norm_root"), i + 1)
            step(v.reciprocal(ninv, nroot))
            for k in range(KT):
                last = stt(dst[:, k, :], src[:, k, :], V(gain, k), ninv, ALU.mult, ALU.mult)
            last.then_inc(S(out_sem), 1)
            return last

        def head_inv(name, src, sq, root, b0, scale, eps):
            tt_(sq, src, src, ALU.mult).then_inc(S("head_sq"), 1)
            head_inv_rest(name, root, b0, scale, eps)

        def head_inv_rest(name, root, b0, scale, eps):
            dve.wait_ge(S("head_sum"), SUM[name])
            for j in range(2):
                last = ts(root[:, 2 * j:2 * j + 2, :], two(bank[b0 + j][:, :], T), scale, eps, ALU.mult, ALU.add)
            last.then_inc(S("head_mean"), 1)
            dve.wait_ge(S("head_root"), ROOT[name])
            step(v.reciprocal(root, root))

        dve.wait_ge(S("const_in"), 16)
        dve.wait_ge(S("vec_in"), 16)
        dve.wait_ge(S("x_in"), 16)
        norm(0, x, "norm1_g", hn)
        dve.wait_ge(S("norm_out"), 1)
        dve.wait_ge(S("mem_in"), 16)
        norm(1, at(W0 + 4096, KT, T), "mem_g", memn)

        dve.wait_ge(S("tile_taken"), SLOTS + 14)
        tt_(shift_d[:, :, 1:T], proj[:, 0:14, 0:T - 1], proj[:, 0:14, 1:T], ALU.subtract)
        step(ts(shift_d[:, :, 0:1], proj[:, 0:14, 0:1], -1.0, None, ALU.mult))
        for i in list(range(12, 14)) + list(range(12)):
            last = stt(proj[:, i, :], shift_d[:, i, :], V("mu", i), proj[:, i, :], ALU.mult, ALU.add)
        done(dve, last, "shifted", 1)
        for ft in range(4):
            last = ts(kk[:, ft, :], raw_k[:, ft, :], V("k_k", ft), None, ALU.mult)
        step(last)
        tt_(tmp2, kk, kk, ALU.mult).then_inc(S("head_sq"), 1)
        dve.wait_ge(S("lora_taken"), 1)
        for ft in range(4):
            last = ts(tmp1[:, ft, :], iclr[:, ft, :], -1.0, V("k_a", ft), ALU.add, ALU.mult)
        step(last)
        step(stt(raw_k, tmp1, 1.0, raw_k, ALU.add, ALU.mult))
        for ft in range(4):
            last = stt(tmp3[:, ft, :], raw_r[:, ft, :], V("r_k", ft), raw_k[:, ft, :], ALU.mult, ALU.mult)
        last.then_inc(S("head_sq"), 1)
        dve.wait_ge(S("head_sum"), SUM["kk"])
        for j in range(2):
            last = ts(tmp2[:, 2 * j:2 * j + 2, :], two(bank[6 + j][:, :], T), 1e-24, None, ALU.max)
        last.then_inc(S("head_mean"), 1)
        dve.wait_ge(S("head_root"), ROOT["kk"])
        step(v.reciprocal(tmp2, tmp2))
        step(tt_(kk, kk, tmp2, ALU.mult))
        dve.wait_ge(S("head_sum"), SUM["bonus"])
        for j in range(2):
            last = tt_(bonus[:, 2 * j:2 * j + 2, :], two(bank[4 + j][:, :], T), raw_v[:, 2 * j:2 * j + 2, :], ALU.mult)
        last.then_inc(S("bonus_done"), 1)
        step(ts(logw, logw, DECAY_SCALE, None, ALU.mult))
        step(v.memset(tmp1, 1.0))
        for ft in range(4):
            for c in range(2):
                r = slice(c * P, (c + 1) * P)
                last = v.tensor_tensor_scan(cc[:, ft, r], tmp1[:, ft, r], logw[:, ft, r], 0.0, ALU.mult, ALU.add)
        step(last)
        c8 = cc.rearrange("p a (c t) -> p (a c) t", t=P)
        step(v.tensor_copy(mid.unsqueeze(2), c8[:, :, 63:64]))
        step(tt_(c8, c8, each(mid, P), ALU.subtract))
        last = tt_(logw, cc, logw, ALU.subtract)
        done(dve, last, "cum_ready", 1)
        mid2 = mid.rearrange("p (a c) -> p a c", c=2)
        tt_(fac, cc[:, :, P - 1:P], mid2[:, :, 1:2], ALU.add).then_inc(S("fac_ready"), 1)
        dve.wait_ge(S("exp_to"), 1)
        c4 = lambda t_: t_.rearrange("p a (c t) -> p a c t", t=P)
        for ft in range(4):
            last = tt_(AR[:, ft, :, 1, :], c4(raw_r)[:, ft, :, :], c4(tmp1)[:, ft, :, :], ALU.mult)
        last.then_inc(S("exp_to_used"), 1)
        dve.wait_ge(S("exp_from"), 1)
        step(tt_(iclr, iclr, kk, ALU.mult))
        tt_(bT, iclr, tmp2, ALU.mult)
        tt_(kT, raw_k, tmp2, ALU.mult)
        dve.wait_ge(S("exp_before"), 1)
        for ft in range(4):
            last = tt_(AR[:, ft, :, 0, :], c4(kk)[:, ft, :, :], c4(tmp3)[:, ft, :, :], ALU.mult)
        last.then_inc(S("scaled"), 1)
        barrier(dve, 1)

        strict, incl = many(cst(C_STRICT), 2), many(cst(C_INCL), 2)
        for side in range(2):
            for G in range(4):
                dve.wait_ge(S("pairs"), 4 * side + G + 1)
                for q in range(2):
                    pb = bank[2 * G + q][:, :].rearrange("p (h s t) -> p h s t", h=2, s=2)
                    hs = slice(q, 4, 2)
                    if side == 0:
                        stt(MT[G][:, hs, :], pb[:, :, 0, :], -1.0, strict, ALU.mult, ALU.mult)
                        last = tt_(RB[G][:, hs, :], pb[:, :, 1, :], incl, ALU.mult)
                    else:
                        tt_(KA[G][:, hs, :], pb[:, :, 0, :], strict, ALU.mult)
                        last = tt_(RK[G][:, hs, :], pb[:, :, 1, :], incl, ALU.mult)
                done(dve, last, "pairs_read", 4 * side + G + 1)
                if side == 0:
                    step(tt_(DT[G], MT[G], many(cst(C_LEVEL), 4), ALU.mult))
                    tt_(DT[G], DT[G], many(ident, 4), ALU.add).then_inc(S("inv_start"), 1)
                    tt_(CT[G], MT[G], many(cst(C_LEVEL + P), 4), ALU.mult).then_inc(S("cross"), 1)
        for lv in range(6):
            for G in range(4):
                dve.wait_ge(S("dcd"), 4 * lv + G + 1)
                if lv < 5:
                    tt_(DD[G], DD[G], two(bank[2 * G + 1][:, :], P), ALU.add)
                tt_(DT[G], DT[G], two(bank[2 * G][:, :], P), ALU.add).then_inc(S("inv"), 1)
                if lv < 5:
                    tt_(CT[G], MT[G], many(cst(C_LEVEL + P * (lv + 2)), 4), ALU.mult).then_inc(S("cross"), 1)
        dve.wait_ge(S("state_up"), 1)
        dve.wait_ge(S("fac_exp"), 1)
        tt_(S1, two(bank[3][:, 0:T], 64), fac.broadcast_to([P, 4, 64]), ALU.mult).then_inc(S("state_done"), 1)
        dve.wait_ge(S("y_copied"), 2)
        dve.wait_ge(S("head_sum"), SUM["gn_mean"])
        for j in range(2):
            last = stt(Y[:, 2 * j:2 * j + 2, :], two(bank[4 + j][:, :], T), -1.0 / RHD, Y[:, 2 * j:2 * j + 2, :], ALU.mult, ALU.add)
        step(last)
        head_inv("gn_var", Y, Vtok_sq, tmp2, 6, 1.0 / RHD, 64e-5)
        step(tt_(Y, Y, tmp2, ALU.mult))
        for ft in range(4):
            last = ts(Y[:, ft, :], Y[:, ft, :], V("lnx_g", ft), V("lnx_b", ft), ALU.mult, ALU.add)
        step(last)
        step(tt_(Y, Y, bonus, ALU.add))
        tt_(ys[:, 0:4, :], Y, gT, ALU.mult)
        barrier(dve, 2)

        sq, sk = proj[:, 14:18, :], proj[:, 18:22, :]
        head_inv("sbq", sq, at(W0, 4, T), at(W0, 4, T), 4, 1.0 / SHD, 1e-6)
        step(stt(sq, sq, V("sb_q_g"), at(W0, 4, T), ALU.mult, ALU.mult))
        head_inv("sbk", sk, at(W0 + 1024, 4, T), at(W0 + 1024, 4, T), 6, 1.0 / SHD, 1e-6)
        stt(sk, sk, V("sb_k_g"), at(W0 + 1024, 4, T), ALU.mult, ALU.mult)
        ts(sq, sq, SHD ** -0.5, None, ALU.mult).then_inc(S("sb_normed"), 1)
        strict8 = lambda n: many(cst(C_STRICT), n)
        for half in range(2):
            r = slice(4 * half, 4 * half + 4)
            dve.wait_ge(S("sbz_taken"), 4 * half + 4)
            stt(sba[:, r, :], sbz[:, r, :], -1.0, sbz[:, r, :], ALU.mult, ALU.min).then_inc(S("sb_negabs"), 1)
            dve.wait_ge(S("sb_log"), half + 1)
            step(stt(sbb[:, r, :], sbz[:, r, :], 0.0, sba[:, r, :], ALU.max, ALU.add))
            tt_(sbb[:, r, 0:P], sbb[:, r, 0:P], strict8(4), ALU.mult)
            tt_(sbb[:, r, T:zc], sbb[:, r, T:zc], strict8(4), ALU.mult).then_inc(S("sb_soft"), 1)
        for h in range(SH):
            dve.wait_ge(S("sbc_up"), h + 1)
            tt_(sba[:, h, :], sbz[:, h, :], bank[4 + h % 4][:, 0:zc], ALU.subtract).then_inc(S("sbc_taken"), 1)
        dve.wait_ge(S("sbc_taken"), SH)
        ts(sba[:, :, :], sba[:, :, :], 0.0, None, ALU.min).then_inc(S("sb_logit"), 1)
        dve.wait_ge(S("sb_exp"), 1)
        tt_(sba[:, :, 0:P], sba[:, :, 0:P], strict8(8), ALU.mult)
        tt_(sba[:, :, T:zc], sba[:, :, T:zc], strict8(8), ALU.mult).then_inc(S("sb_attn"), 1)

        def att_logits(name, scale, bias, h):
            z, m = att_z[h % 2], att_m[h % 2]
            dve.wait_ge(S("att_s"), HEAD0[name] + h + 1)
            src = two(bank[4 + h % 2][:, :], T)
            if bias is None:
                step(ts(z, src, scale, None, ALU.mult))
            else:
                step(stt(z, src, scale, two(bias[:, h, :], T), ALU.mult, ALU.add))
            step(v.reduce_max(m, z, AX.X))
            ts(m, m, -1.0, None, ALU.mult).then_inc(S("att_z"), 1)

        def att_share(name, h):
            dve.wait_ge(S("att_e"), HEAD0[name] + h + 1)
            step(v.reciprocal(att_r[h % 2], att_s[h % 2]))
            tt_(att_p[h % 2], att_p[h % 2], each(att_r[h % 2], T), ALU.mult).then_inc(S("att_p"), 1)

        mq = proj[:, 22:26, :]
        head_inv("mq", mq, at(W0 + 9216, 4, T), at(W0 + 9216, 4, T), 4, 1.0 / MHD, 1e-6)
        stt(mq, mq, V("mem_q_g"), at(W0 + 9216, 4, T), ALU.mult, ALU.mult)
        head_inv("mk", mk, at(W0 + 10240, 4, T), at(W0 + 10240, 4, T), 6, 1.0 / MHD, 1e-6)
        stt(mk, mk, V("mem_k_g"), at(W0 + 10240, 4, T), ALU.mult, ALU.mult).then_inc(S("mem_normed"), 1)
        att_logits("mem", MHD ** -0.5, None, 0)
        for h in range(MH):
            if h + 1 < MH:
                att_logits("mem", MHD ** -0.5, None, h + 1)
            att_share("mem", h)
        barrier(dve, 3)

        for n in range(3):
            dve.wait_ge(S("page_done"), PAGE0["branch"] + 4 * (n + 1))
            for j in range(KT):
                if n == 0:
                    last = tt_(merged[:, j, :], bank[j][:, 0:T], gates[:, j, :], ALU.mult)
                else:
                    gj = gates[:, 8 * n + j, :]
                    last = tt_(gj, bank[j][:, 0:T], gj, ALU.mult)
            done(dve, last, "branch_read", n + 1)
            if n:
                last = tt_(merged, merged, gates[:, 8 * n:8 * n + 8, :], ALU.add)
            else:
                last = dve.drain()
            done(dve, last, "branch_taken", n + 1)

        def add_tiles(stage):
            for j in range(KT):
                page = PAGE0[stage] + j
                dve.wait_ge(S("page_done"), page + 1)
                tt_(x[:, j, :], bank[page % SLOTS][:, 0:T], x[:, j, :], ALU.add).then_inc(S("tile_taken"), 1)

        add_tiles("out")
        barrier(dve, 4)
        norm(2, x, "norm2_g", hn)
        for _ in range(2):
            dve.drain().then_inc(S("glu_done"), 1)
        with dve.Fori(0, N_UP // 4) as i:
            for b in range(4):
                src = bank[(PAGE0["up"] + b) % SLOTS]
                w1 = vec[:, bass.ds(i * 4 + VCOL["conv_w1"] + b, 1)]
                w0 = vec[:, bass.ds(i * 4 + VCOL["conv_w0"] + b, 1)]
                dve.wait_ge(S("conv_centre"), i * 4 + b + 1)
                stt(conv_u[:, b, 1:T], src[:, 0:T - 1], w1, conv_u[:, b, 1:T], ALU.mult, ALU.add).then_inc(S("conv_tap"), 1)
                dve.wait_ge(S("conv_tap"), i * 4 + b + 1)
                stt(conv_u[:, b, 2:T], src[:, 0:T - 2], w0, conv_u[:, b, 2:T], ALU.mult, ALU.add).then_inc(S("tile_taken"), 1)
            for pr in range(2):
                dve.wait_ge(S("glu_sig"), i * 2 + pr + 1)
                tt_(sig_u[:, pr, :], sig_u[:, pr, :], conv_u[:, 2 * pr, :], ALU.mult).then_inc(S("glu_silu"), 1)
                dve.wait_ge(S("glu_silu"), i * 2 + pr + 1)
                tt_(ff[:, bass.ds(i * 2 + pr, 1), :], sig_u[:, pr:pr + 1, :], conv_u[:, 2 * pr + 1:2 * pr + 2, :], ALU.mult)\
                    .then_inc(S("glu_done"), 1)
        barrier(dve, 5)
        dve.wait_ge(S("page_done"), PAGE0["down"] + N_DOWN)
        for j in range(KT):
            tt_(x[:, j, :], bank[j][:, 0:T], x[:, j, :], ALU.add)
        barrier(dve, 6)

        norm(3, x, "norm1_g_2", hn)
        for h in range(BH):
            ts(bias_h[:, h, :], cst(C_ALIBI, 2 * T), 2.0 ** (-8.0 * (h + 1) / BH), None, ALU.mult)
        tt_(lbv[:, 0:4], vec[:, VCOL["lb0"]:VCOL["lb0"] + 4], vec[:, VCOL["lb1"]:VCOL["lb1"] + 4], ALU.subtract)\
            .then_inc(S("lb_diff"), 1)
        dve.wait_ge(S("h_sig"), 1)
        step(ts(lbv[:, 8:12], lbv[:, 4:8], -1.0, 1.0, ALU.mult, ALU.add))
        for h in range(GH):
            last = ts(hf[:, h, :], hE[:, h, :], lbv[:, 8 + h:9 + h], lbv[:, 4 + h:5 + h], ALU.mult, ALU.add)
        done(dve, last, "h_f", 1)
        ts(hk, hf, -1.0, 1.0, ALU.mult, ALU.add)
        tt_(hq, hQ, pj[:, 8:12, :], ALU.mult)
        tt_(pj[:, 16:20, :], hK, pj[:, 16:20, :], ALU.mult).then_inc(S("h_sides"), 1)
        dve.wait_ge(S("h_sides"), 1)
        step(v.memset(hQ, 1.0))
        dve.wait_ge(S("h_log"), 1)
        for h in range(GH):
            last = v.tensor_tensor_scan(hcum[:, h, :], hQ[:, h, :], hE[:, h, :], 0.0, ALU.mult, ALU.add)
        step(last)
        barrier(dve, 7)

        def level_diff(lv):
            half = (LEVELS + [P])[lv - 1]
            cb = hcum.rearrange("p h (b c) -> p (h b) c", c=2 * half)
            eb = hE.rearrange("p h (b c) -> p (h b) c", c=2 * half)
            step(tt_(eb, cb, cb[:, :, half - 1:half].broadcast_to([P, cb.shape[1], 2 * half]), ALU.subtract))
            stt(hE, hE, -1.0, hE, ALU.mult, ALU.min).then_inc(S("h_diff"), 1)

        def level_add(lv):
            dve.wait_ge(S("h_pairs"), lv + 1)
            if lv == 0:
                for tt in range(2):
                    last = tt_(hacc[:, tt, :, :], two(bank[tt][:, :], P), many(ident, 4), ALU.mult)
            elif lv < 8:
                for tt in range(2):
                    last = tt_(hmul[:, 4 * tt:4 * tt + 4, :], two(bank[tt][:, :], P), many(cst(C_LEVEL + P * (lv - 1)), 4),
                               ALU.mult)
                step(last)
                for tt in range(2):
                    last = tt_(hacc[:, tt, :, :], hacc[:, tt, :, :], hmul[:, 4 * tt:4 * tt + 4, :], ALU.add)
            else:
                last = v.tensor_copy(hx, two(bank[0][:, :], P))
            done(dve, last, "h_added", lv + 1)

        att_logits("moba", BHD ** -0.5, bias_h, 0)
        for lv in range(9):
            if lv < 8:
                level_diff(lv + 1)
                if lv + 1 < BH:
                    att_logits("moba", BHD ** -0.5, bias_h, lv + 1)
                dve.wait_ge(S("h_exp"), lv + 1)
                dve.wait_ge(S("h_pairs"), lv + 1)
                tt_(hQ, hq, hE, ALU.mult)
                done(dve, tt_(hK, hk, hE, ALU.mult), "h_sides", lv + 2)
                att_share("moba", lv)
            level_add(lv)
        dve.wait_ge(S("h_out"), 1)
        for j in range(2):
            last = v.tensor_copy(hf[:, 2 * j:2 * j + 2, :], two(bank[2 + j][:, :], T))
        step(last)
        head_inv("hn", hf, hE, hE, 0, 1.0 / P, 1e-6)
        for h in range(GH):
            last = stt(hf[:, h, :], hf[:, h, :], V("rec_g", h), hE[:, h, :], ALU.mult, ALU.mult)
        step(last)
        tt_(cat[:, 4:8, :], hf, pj[:, 16:20, :], ALU.mult)
        barrier(dve, 8)
        add_tiles("out2")
        barrier(dve, 9)
        norm(4, x, "norm2_g_2", hn)
        barrier(dve, 10)

        def rank(j):
            tt, h = j // PH, j % PH
            dve.wait_ge(S("score_taken"), j // 2 + 1)
            hs = (2 * h, 2 * h + 1)
            sc = [scores[:, tt, hc, :] for hc in hs]
            wk = [work[:, i * NK:(i + 1) * NK] for i in range(2)]
            for i in range(2):
                last = v.max(top_v[:, i, 0:8], sc[i])
            step(last)
            for i in range(2):
                v.max_index(top_i[:, i, 0:8], top_v[:, i, 0:8], sc[i])
            for i in range(2):
                last = v.match_replace(wk[i], top_v[:, i, 0:8], sc[i], -BIG)
            step(last)
            for i in range(2):
                last = v.max(top_v[:, i, 8:16], wk[i])
            step(last)
            for i in range(2):
                v.max_index(top_i[:, i, 8:16], top_v[:, i, 8:16], wk[i])
            step(tt_(two(cand, TOPK), each(top_v[:, 0, :], TOPK), many(top_v[:, 1, :], TOPK), ALU.add))
            v.tensor_copy(top_f, top_i)
            step(v.max(sel_v[:, 0:8], cand))
            v.max_index(pos_u[:, 0:8], sel_v[:, 0:8], cand)
            step(v.match_replace(work, sel_v[:, 0:8], cand, -BIG))
            step(v.max(sel_v[:, 8:16], work))
            step(v.max_index(pos_u[:, 8:16], sel_v[:, 8:16], work))
            ts(soft[:, j, :], sel_v, sel_v[:, 0:1], None, ALU.subtract).then_inc(S("soft_in"), 1)
            ts(place_u[:, 0, :], pos_u, 4, None, ALU.logical_shift_right)
            step(ts(place_u[:, 1, :], pos_u, 15, None, ALU.bitwise_and))
            step(v.tensor_copy(place_f, place_u))
            for i in range(2):
                last = tt_(eqm[:, i, :, :], each(place_f[:, i, :], TOPK), many(cst(C_IOTA, TOPK), TOPK), ALU.is_equal)
            step(last)
            for i in range(2):
                last = tt_(eqm[:, i, :, :], eqm[:, i, :, :], many(top_f[:, i, :], TOPK), ALU.mult)
            step(last)
            step(v.reduce_sum(key_f, eqm.rearrange("p i a b -> p (i a) b"), AX.X))
            step(stt(key_f[:, 0:TOPK], key_f[:, 0:TOPK], float(NK), key_f[:, TOPK:2 * TOPK], ALU.mult, ALU.add))
            done(dve, v.tensor_copy(eidx[:, tt, h * TOPK:(h + 1) * TOPK], key_f[:, 0:TOPK]), "rows_ready", j + 1)

        def experts(j):
            tt, h = j // PH, j % PH
            dve.wait_ge(S("soft_exp"), j + 1)
            step(v.reciprocal(rinv, rsum[:, j:j + 1]))
            step(ts(gate_p[:, tt, h * TOPK:(h + 1) * TOPK], soft[:, j, :], rinv, None, ALU.mult))
            with dve.Fori(0, TOPK // UVS) as i:
                for s in range(UVS):
                    n = j * TOPK + s
                    dve.wait_ge(S(f"row_in{s}"), i * 16 + ((n // UVS) + 1) * 16)
                    stt(junk, uv[:, s, 0:D], 1.0, htok[:, tt, :], ALU.mult, ALU.mult, accum_out=e_act[:, s:s + 1])\
                        .then_inc(S("dot_ready"), 1)
                    dve.wait_ge(S("gelu_ready"), i * UVS + n + 1)
                    ts(diag[:, s, :], ident, e_gelu[:, s:s + 1], gate_p[:, tt, bass.ds(i * UVS + h * TOPK + s, 1)],
                       ALU.mult, ALU.mult).then_inc(S("diag_ready"), 1)

        rank(0)
        rank(1)
        dve.wait_ge(S("htok_in"), 1)
        for j in range(2 * PH):
            experts(j)
            if j + 2 < 2 * PH:
                rank(j + 2)
        dve.wait_ge(S("y_feat"), 1)
        for k in range(4):
            last = tt_(x[:, 2 * k:2 * k + 2, :], two(bank[4 + k][:, :], T), x[:, 2 * k:2 * k + 2, :], ALU.add)
        step(last)
        norm(5, x, "normf_g", hn, "final_out")

    @block.gpsimd
    def _(pool):
        def gather(slot, tt, col):
            nc.gpsimd.indirect_dma_start(out=uv[:, slot, :], out_offset=None, in_=A["experts"],
                                         in_offset=bass.IndirectOffsetOnAxis(ap=eidx[:, tt, col], axis=0))\
                .then_inc(S(f"row_in{slot}"), 16)

        for n in range(2 * P):
            s, tt, m = n % UVS, n // P, n % P
            if n % TOPK == 0:
                pool.wait_ge(S("rows_ready"), n // TOPK + 1)
            if n >= UVS:
                pool.wait_ge(S("row_used"), n - UVS + 1)
            gather(s, tt, slice(m, m + 1))

    block.__exit__(None, None, None)


def kernel(**inputs):
    import concourse.bacc as _bacc
    from concourse.bass_utils import run_bass_kernel_spmd as _run

    a = {k: np.asarray(v) for k, v in inputs.items()}

    def feat(m):
        r, f = m.shape
        return np.ascontiguousarray(m.reshape(r, f // P, P).transpose(2, 1, 0))

    def cols(m):
        i, o = m.shape
        return m.reshape(i // P, P, o // P, P).transpose(2, 1, 0, 3).reshape(o // P, P, i)

    def rows(m):
        return m.reshape(m.shape[0] // P, P, m.shape[1])

    w_in, w_up, kv, w2 = a["w_in"][0], a["w_up"][0], a["w_mem_kv"][0], a["w_in_2"][0]
    up = cols(w_up)
    up = np.stack([up[:FT], up[FT:]], axis=1).reshape(2 * FT, P, D)
    pages = np.concatenate([
        cols(w_in[:, 0:1792]), cols(w_in[:, 1792:2816]), cols(w_in[:, 3328:3840]),
        cols(w_in[:, 2816:3328]), cols(kv[:, 0:512]), cols(kv[:, 512:1024]), cols(w_in[:, 3840:6912]),
        rows(a["w_branch"][0].reshape(1536, D)), cols(a["w_out"][0]), up, rows(a["w_down"][0]),
        cols(w2[:, 0:1024]), cols(w2[:, 1536:2560]), cols(w2[:, 3072:3584]),
        cols(w2[:, 1024:1536]), cols(w2[:, 2560:3072]), cols(a["w_out_2"][0]), cols(a["peer_wq_2"][0])], axis=0)
    assert pages.shape == (N_PAGES, P, PAGE), pages.shape

    def vcol(m):
        return m.reshape(-1, P).T

    def pairs(m):
        t = m.reshape(2, FT, P).transpose(1, 0, 2).reshape(2 * FT, P)
        return t.T

    lb = a["rec_lb_logits_2"]
    vec = np.concatenate([
        vcol(a["shift_mu"]), vcol(a["norm1_g"]), vcol(a["decay_w0"]), vcol(a["iclr_a0"]), vcol(a["k_k"]), vcol(a["k_a"]),
        vcol(a["r_k"]), vcol(a["lnx_g"]), vcol(a["lnx_b"]), vcol(np.tile(a["sb_q_norm_g"][0], 2)),
        vcol(np.tile(a["sb_k_norm_g"][0], 2)), vcol(a["mem_norm_g"]), vcol(a["mem_q_norm_g"]), vcol(a["mem_k_norm_g"]),
        vcol(a["norm2_g"]), pairs(a["conv_w"][0, 0]), pairs(a["conv_w"][0, 1]), pairs(a["conv_w"][0, 2]), pairs(a["conv_b"][0]),
        vcol(a["norm1_g_2"]), vcol(lb[0]), vcol(lb[1]), vcol(a["rec_norm_g_2"]), vcol(a["norm2_g_2"]), vcol(a["normf_g_2"])],
        axis=1)
    sub = a["peer_subkeys_2"][0].reshape(N_WQ, NK, P).transpose(2, 0, 1)
    dram = {
        "const": constants(), "vec": vec, "xT": feat(a["x"][0]), "memT": feat(a["mem"][0]), "pages": pages,
        "decay_w2": a["decay_w2"][0], "iclr_a2": a["iclr_a2"][0], "gate_g2": a["gate_g2"][0], "subkT": sub,
        "experts": np.concatenate([a["peer_u_2"][0], a["peer_v_2"][0]], axis=1),
    }
    nc = _bacc.Bacc("TRN2", target_bir_lowering=False, num_devices=1)
    arrays, args = {}, {}
    for name, arr in dram.items():
        arr = np.ascontiguousarray(arr)
        arrays[f"in_{name}"] = arr
        args[name] = nc.dram_tensor(f"in_{name}", arr.shape, mybir.dt.from_np(arr.dtype), kind="ExternalInput").ap()
    args["out"] = nc.dram_tensor("out_T", (P, KT, T), F32, kind="ExternalOutput").ap()
    build(nc, args)
    r = _run(nc, [arrays], core_ids=[0])
    out = r.results[0]["out_T"]
    return np.ascontiguousarray(out.transpose(2, 1, 0).reshape(1, T, D))
```

```python
import numpy as np
import concourse.bass as bass
from concourse import mybir

F32 = mybir.dt.float32
U32 = mybir.dt.uint32
F32R = mybir.dt.float32r
ALU = mybir.AluOpType
ACT = mybir.ActivationFunctionType
AX = mybir.AxisListType

P = 128
T = 256
D = 1024
KT = D // P
RH, RHD = 8, 64
SH, SHD = 8, 64
MH, MHD = 4, 128
MEM = 256
FF = 2816
FT = FF // P
BH, BHD = 8, 64
GH = 4
NK, TOPK, PH = 128, 16, 8
SLOTS = 4
PAGE = 8 * P
BIG = 3.0e38
DECAY_SCALE = -float(np.exp(-0.5))

N_IN_A, N_SBV, N_MK, N_MV, N_GATE = 26, 4, 4, 4, 24
N_BR, N_OUT, N_UP, N_DOWN = 12, 8, 2 * FT, FT
N_IN2, N_TOK2, N_OUT2, N_WQ = 20, 8, 8, 16
STAGES = ["in_a", "sbv", "mk", "mv", "gate", "branch", "out", "up", "down", "in2", "tok2", "out2", "wq"]
COUNTS = [N_IN_A, N_SBV, N_MK, N_MV, N_GATE, N_BR, N_OUT, N_UP, N_DOWN, N_IN2, N_TOK2, N_OUT2, N_WQ]
PAGE0 = {s: sum(COUNTS[:i]) for i, s in enumerate(STAGES)}
N_PAGES = sum(COUNTS)
SPLIT0 = PAGE0["up"]
TILED = [s for s in STAGES if s not in ("branch", "down")]
TILE0 = {s: sum(COUNTS[STAGES.index(x)] for x in TILED[:i]) for i, s in enumerate(TILED)}

VECS = [("mu", 14), ("norm1_g", 8), ("decay_w0", 4), ("iclr_a0", 4), ("k_k", 4), ("k_a", 4), ("r_k", 4),
        ("lnx_g", 4), ("lnx_b", 4), ("sb_q_g", 1), ("sb_k_g", 1), ("mem_g", 8), ("mem_q_g", 1), ("mem_k_g", 1),
        ("norm2_g", 8), ("conv_w0", 2 * FT), ("conv_w1", 2 * FT), ("conv_w2", 2 * FT), ("conv_b", 2 * FT),
        ("norm1_g_2", 8), ("lb0", 4), ("lb1", 4), ("rec_g", 4), ("norm2_g_2", 8), ("normf_g", 8)]
VCOL = {n: sum(c for _, c in VECS[:i]) for i, (n, _) in enumerate(VECS)}
N_VEC = sum(c for _, c in VECS)

LEVELS = [1, 2, 4, 8, 16, 32, 64]
C_IDENT, C_ONES, C_BLK64, C_INCL, C_STRICT, C_SUFFIX, C_LEVEL = [P * i for i in range(7)]
C_ALIBI = C_LEVEL + P * len(LEVELS)
C_IOTA = C_ALIBI + 2 * T
N_CONST = C_IOTA + TOPK


SQ = {n: i + 1 for i, n in enumerate(["kk", "bonus", "sbq", "sbk", "mq", "mk", "gn_var", "hn"])}
SUM = {n: i + 1 for i, n in enumerate(["kk", "bonus", "sbq", "sbk", "mq", "mk", "gn_mean", "gn_var", "hn"])}
ROOT = {n: i + 1 for i, n in enumerate(["kk", "sbq", "sbk", "mq", "mk", "gn_var", "hn"])}
HEAD0 = {"mem": 0, "moba": MH}


def constants():
    c = np.zeros((P, N_CONST), np.float32)
    p, f = np.arange(P)[:, None], np.arange(P)[None, :]
    c[:, C_IDENT:C_IDENT + P] = p == f
    c[:, C_ONES:C_ONES + P] = 1
    c[:, C_BLK64:C_BLK64 + P] = p // 64 == f // 64
    c[:, C_INCL:C_INCL + P] = f >= p
    c[:, C_STRICT:C_STRICT + P] = f > p
    c[:, C_SUFFIX:C_SUFFIX + P] = p >= f
    for i, h in enumerate(LEVELS):
        c[:, C_LEVEL + P * i:C_LEVEL + P * (i + 1)] = (p // (2 * h) == f // (2 * h)) & (p % (2 * h) < h) & (f % (2 * h) >= h)
    s = np.arange(T)[None, :]
    for tt in range(2):
        t = p + P * tt
        c[:, C_ALIBI + T * tt:C_ALIBI + T * (tt + 1)] = np.where(s <= t, s - t, -1e30)
    c[:, C_IOTA:C_IOTA + TOPK] = np.arange(TOPK)
    return c


def build(nc, A):
    sems = {}

    def S(name):
        if name not in sems:
            sems[name] = nc.semaphore(name).__enter__()
        return sems[name]

    def sb(name, shape, dt=F32):
        return nc.sbuf_tensor(name, shape, dt).__enter__()[tuple(slice(None) for _ in shape)]

    const = sb("const", [P, N_CONST])
    vec = sb("vec", [P, N_VEC])
    ring = sb("ring", [P, SLOTS, PAGE])
    x = sb("x_res", [P, KT, T])
    hn = sb("h_norm", [P, KT, T])
    ARENA = 41200
    bank = [nc.psum_tensor(f"bank{i}", [P, 512], F32).__enter__() for i in range(8)]

    def room(name, size):
        space = nc.sbuf_tensor(name, [P, size], F32)
        whole = space.__enter__()

        def at(off, *shape):
            n = int(np.prod(shape))
            assert off + n <= size, (name, off, n)
            v = whole[:, off:off + n]
            if len(shape) == 2:
                v = v.rearrange("p (a b) -> p a b", b=shape[1])
            if len(shape) == 3:
                v = v.rearrange("p (a b c) -> p a b c", b=shape[1], c=shape[2])
            if len(shape) == 4:
                v = v.rearrange("p (a b c d) -> p a b c d", b=shape[1], c=shape[2], d=shape[3])
            return v
        return space, at

    space1, at = room("arena_mix", ARENA)

    def two(ap, b):
        return ap.rearrange("p (a b) -> p a b", b=b)

    def cst(c, n=P):
        return const[:, c:c + n]

    ident, ones, blk64 = cst(C_IDENT), cst(C_ONES), cst(C_BLK64)

    def many(ap, n):
        return ap.unsqueeze(1).broadcast_to([ap.shape[0], n, ap.shape[1]])

    def each(ap, n):
        return ap.unsqueeze(2).broadcast_to([ap.shape[0], ap.shape[1], n])

    def V(name, i=0):
        return vec[:, VCOL[name] + i:VCOL[name] + i + 1]

    memn = at(0, KT, T)
    proj = at(2048, N_IN_A, T)
    sbv = at(8704, 4, 2, P)
    mk = at(9728, 4, T)
    mv = at(10752, 4, 2, P)
    gates = at(11776, N_GATE, T)
    ys = at(17920, 12, T)
    W0 = 20992
    raw_r, raw_k, raw_v = proj[:, 0:4, :], proj[:, 4:8, :], proj[:, 8:12, :]
    tmp1, tmp2, tmp3 = at(W0, 4, T), at(W0 + 1024, 4, T), at(W0 + 2048, 4, T)
    logw, iclr, cc, kk = (at(W0 + 3072 + 1024 * i, 4, T) for i in range(4))
    shift_d = at(W0, 14, T)
    bT, kT, bonus, gT = (at(W0 + 7168 + 1024 * i, 4, T) for i in range(4))
    AR = at(W0 + 11264, 4, 2, 2, P)
    Vtok = at(W0 + 13312, 2, 512)
    Btok, Ktok = at(W0 + 14336, 512), at(W0 + 14848, 512)
    S1 = at(W0 + 15360, 4, 64)
    fac = at(W0 + 15616, 4, 1)
    mid = at(W0 + 15620, 8)
    lora_w = at(W0 + 15640, 2, 512)
    Y = at(W0 + 16664, 4, T)
    free = [W0 + 512 * i for i in range(14)] + [W0 + 17688, W0 + 18200] + [2048 + 512 * i for i in range(6)] \
        + [512 * i for i in range(4)] + [11776 + 8 * T + 512 * i for i in range(6)]
    MT, DD, DT, PP, CT, RB, KA, RK = ([at(free[4 * b + g], 4, P) for g in range(4)] for b in range(8))
    Gs, Us = at(W0 + 18712, 512), at(W0 + 19224, 512)
    Vtok_sq = logw

    norm_at = [(at(W0, KT, T), at(W0 + 2048, T), at(W0 + 2304, T))] * 2

    zc = 3 * P
    sbz, sba, sbb = at(W0, 8, zc), at(W0 + 3072, 8, zc), at(W0 + 6144, 8, zc)
    att_z = [at(W0 + 10000 + 512 * i, 2, T) for i in range(2)]
    att_p = [at(W0 + 11024 + 512 * i, 2, T) for i in range(2)]
    att_t = [at(W0 + 12048 + 512 * i, 2, T) for i in range(2)]
    att_m = [at(W0 + 13072 + 8 * i, 2) for i in range(2)]
    att_s = [at(W0 + 13090 + 8 * i, 2) for i in range(2)]
    att_r = [at(W0 + 13110 + 8 * i, 2) for i in range(2)]
    merged = at(W0, KT, T)
    gated = at(W0 + 2048, 2, T)

    inv_at = {"sbq": at(17920, 4, T), "sbk": at(18944, 4, T), "mq": at(19968, 4, T), "mk": Y}
    space1.__exit__(None, None, None)

    w_hi, w_lo = (sb(n, [P, SLOTS, PAGE], F32R) for n in ("w_hi", "w_lo"))
    x_hi, x_lo = (sb(n, [P, KT, T], F32R) for n in ("x_hi", "x_lo"))
    ff_space = [nc.sbuf_tensor(n, [P, FT, T], F32R) for n in ("ff_hi", "ff_lo")]
    ff_hi, ff_lo = (m.__enter__()[:, :, :] for m in ff_space)
    space2, at2 = room("arena_ffn", 4864)
    conv_u, sig_u, glu = at2(0, 4, T), at2(1024, 2, T), at2(1536, 2, T)
    norm_at += [(at2(2048, KT, T), at2(4096, T), at2(4352, T))]
    space2.__exit__(None, None, None)
    for m in reversed(ff_space):
        m.__exit__(None, None, None)

    _, at3 = room("arena_block2", ARENA - 2 * SLOTS * PAGE - 2 * KT * T)
    pj = at3(0, N_IN2, T)
    tok2 = at3(5120, 8, 2, P)
    cat = at3(7168, 8, T)
    bias_h = at3(9216, 8, 2 * T)
    hw = 13312
    hq, hk, hcum, hE, hQ, hK, hf = (at3(hw + 1024 * i, 4, T) for i in range(7))
    hacc = at3(hw + 7168, 2, 4, P)
    hx = at3(hw + 8192, 4, P)
    hmul = at3(hw + 8704, 8, P)
    lbv = at3(hw + 9728, 16)
    AT2 = hw + 9744
    att_z = [att_z, [at3(AT2 + 512 * i, 2, T) for i in range(2)]]
    att_p = [att_p, [at3(AT2 + 1024 + 512 * i, 2, T) for i in range(2)]]
    att_t = [att_t, [at3(AT2 + 2048 + 512 * i, 2, T) for i in range(2)]]
    att_m = [att_m, [at3(AT2 + 3072 + 2 * i, 2) for i in range(2)]]
    att_s = [att_s, [at3(AT2 + 3076 + 2 * i, 2) for i in range(2)]]
    att_r = [att_r, [at3(AT2 + 3080 + 2 * i, 2) for i in range(2)]]
    ATT = {"mem": 0, "moba": 1}
    norm_at += [(at3(20992, KT, T), at3(23040, T), at3(23296, T))] * 3
    qp = at3(0, N_WQ, T)
    subk = at3(4096, N_WQ, NK)
    scores = at3(6144, 2, N_WQ, NK)
    work = at3(10240, T)
    htok = at3(10496, 2, D)
    cand = at3(12544, T)
    top_v, top_f = at3(12800, 2, TOPK), at3(12832, 2, TOPK)
    top_i = at3(12864, 2, TOPK).bitcast(U32)
    sel_v, pos_u = at3(12896, TOPK), at3(12912, TOPK).bitcast(U32)
    place_u, place_f = at3(12928, 2, TOPK).bitcast(U32), at3(12960, 2, TOPK)
    key_f = at3(12992, 2 * TOPK)
    eqm = at3(13024, 2, TOPK, TOPK)
    soft = at3(13536, 2 * PH, TOPK)
    rsum, rinv = at3(13792, 2 * PH), at3(13808, 1)
    UVS = 8
    e_act, e_gelu = at3(13812, UVS), at3(13820, UVS)
    gate_p = at3(13828, 2, P)
    eidx = at3(14084, 2, P).bitcast(U32)
    uv = [at3(14340 + 2 * D * i, 2 * D) for i in range(UVS - 3)] + [at3(2 * D * i, 2 * D) for i in range(3)]
    yt = at3(24580, 2, D)
    junk = at3(26628, D)
    diag = at3(27652, UVS, P)

    def done(eng, ins, sem, n):
        ins.then_inc(S(sem), 1)
        eng.wait_ge(S(sem), n)

    def chain(eng, name):
        n = [0]

        def step(ins):
            n[0] += 1
            done(eng, ins, name, n[0])
        return step

    def barrier(eng, k):
        eng.drain().then_inc(S("phase_done"), 1)
        eng.wait_ge(S("phase_done"), 3 * k)

    block = nc.Block().__enter__()

    @block.sync
    def _(sp):
        sp.dma_start(const[:, :], A["const"]).then_inc(S("const_in"), 16)
        sp.dma_start(vec[:, :], A["vec"]).then_inc(S("vec_in"), 16)
        sp.dma_start(x[:, :, :], A["xT"]).then_inc(S("x_in"), 16)

        def load(slot, page, n):
            sp.dma_start(ring[:, slot, :], page).then_inc(S(f"page_in{slot}"), 16)

        def reload(sem, first, at, n, i=None):
            page = first + n
            sp.wait_ge(S(sem), at + n + 1 if i is None else i * SLOTS + at + n + 1)
            src = A["pages"][page] if i is None else A["pages"][bass.ds(i * SLOTS + page, 1)].rearrange("o p c -> (o p) c")
            load(page % SLOTS, src, 1)

        for s in range(SLOTS):
            load(s, A["pages"][s], 1)
        for sem, first, end, at in (("page_done", SLOTS, SPLIT0 + SLOTS, 0), ("lo_ready", SPLIT0 + SLOTS, N_PAGES, 0)):
            rounds = (end - first) // SLOTS
            with sp.Fori(0, rounds) as i:
                for n in range(SLOTS):
                    reload(sem, first, at, n, i)
            for n in range(rounds * SLOTS, end - first):
                reload(sem, first, at, n)
        sp.wait_ge(S("final_out"), 1)
        sp.dma_start(A["out"], hn[:, :, :]).then_inc(S("out_stored"), 16)
        sp.wait_ge(S("out_stored"), 16)

    @block.tensor
    def _(pe):
        mm = nc.tensor.matmul

        def page_ready(page, i=None):
            if page >= SPLIT0:
                n = page - SPLIT0 + 1
                pe.wait_ge(S("lo_ready"), n if i is None else i * SLOTS + n)
                return
            n = page // SLOTS + 1
            pe.wait_ge(S(f"page_in{page % SLOTS}"), 16 * n if i is None else i * 16 + 16 * n)

        def products(page, hi, lo):
            slot = page % SLOTS
            if page < SPLIT0:
                return [(ring[:, slot, :], hi)]
            return [(w_hi[:, slot, :], hi), (w_hi[:, slot, :], lo), (w_lo[:, slot, :], hi)]

        def linear(stage, src, by_token=False, part=None):
            first, n = part or (0, COUNTS[STAGES.index(stage)])
            page0, tile0 = PAGE0[stage] + first, TILE0[stage] + first

            def one(b, i=None):
                page, tile = page0 + b, tile0 + b
                page_ready(page, i)
                pe.wait_ge(S("tile_taken"), tile + 1 if i is None else i * SLOTS + tile + 1)
                out, ways = bank[page % SLOTS], products(page, src, x_lo)
                for tt in range(2 if by_token else 1):
                    for k in range(KT):
                        for n_, (w, y) in enumerate(ways):
                            w, y = w[:, k * P:(k + 1) * P], y[:, k, :]
                            flags = dict(start=k == 0 and n_ == 0, stop=k == KT - 1 and n_ == len(ways) - 1)
                            if by_token:
                                last = mm(out[:, tt * P:(tt + 1) * P], y[:, tt * P:(tt + 1) * P], w, **flags)
                            else:
                                last = mm(out[:, 0:T], w, y, **flags)
                last.then_inc(S("page_done"), 1)

            groups = n // SLOTS
            if groups > 1:
                with pe.Fori(0, groups) as i:
                    for b in range(SLOTS):
                        one(b, i)
            else:
                for b in range(groups * SLOTS):
                    one(b)
            for b in range(groups * SLOTS, n):
                one(b)

        def wide(page0, n, hi, lo=None):
            for k in range(n):
                page_ready(page0 + k)
                ways = products(page0 + k, hi, lo)
                for j in range(KT):
                    for n_, (w, y) in enumerate(ways):
                        last = mm(bank[j][:, 0:T], w[:, j * P:(j + 1) * P], y[:, k, :], start=k == 0 and n_ == 0,
                                  stop=k == n - 1 and n_ == len(ways) - 1)
                last.then_inc(S("page_done"), 1)

        def norm_sum(i):
            pe.wait_ge(S("norm_sq"), i + 1)
            for k in range(KT):
                last = mm(bank[4][:, 0:T], ones, norm_at[i][0][:, k, :], start=k == 0, stop=k == KT - 1)
            last.then_inc(S("norm_sum"), 1)

        def head_sum(name, mat, src, b0, wait=True):
            if wait:
                pe.wait_ge(S("head_sq"), SQ[name])
            for j in range(2):
                last = mm(bank[b0 + j][:, :], mat, src[:, 2 * j:2 * j + 2, :], start=True, stop=True)
            last.then_inc(S("head_sum"), 1)

        pe.wait_ge(S("const_in"), 16)
        norm_sum(0)
        norm_sum(1)
        pe.wait_ge(S("norm_out"), 2)
        linear("in_a", hn)
        pe.wait_ge(S("lora_w_in"), 48)
        pe.wait_ge(S("lora_act"), 1)
        for ft in range(4):
            mm(bank[4 + ft // 2][:, (ft % 2) * T:(ft % 2) * T + T], lora_w[0:64, 0, ft * P:(ft + 1) * P], proj[0:64, 12, :],
               start=True, stop=True)
            last = mm(bank[6 + ft // 2][:, (ft % 2) * T:(ft % 2) * T + T], lora_w[64:128, 0, ft * P:(ft + 1) * P],
                      proj[64:128, 12, :], start=True, stop=True)
        last.then_inc(S("lora_up"), 1)
        linear("sbv", hn, by_token=True)
        linear("mk", memn)
        pe.wait_ge(S("lora_taken"), 1)
        for ft in range(4):
            last = mm(bank[4 + ft // 2][:, (ft % 2) * T:(ft % 2) * T + T], lora_w[:, 1, ft * P:(ft + 1) * P], proj[:, 13, :],
                      start=True, stop=True)
        last.then_inc(S("gate_up"), 1)
        head_sum("kk", blk64, tmp2, 6)
        pe.wait_ge(S("gate_taken"), 1)
        head_sum("bonus", blk64, tmp3, 4)
        linear("mv", memn, by_token=True)
        pe.wait_ge(S("head_mean"), ROOT["kk"])
        head_sum("sbq", blk64, inv_at["sbq"], 6)
        pe.wait_ge(S("bonus_done"), 1)
        head_sum("sbk", blk64, inv_at["sbk"], 4)
        linear("gate", hn, part=(0, 4))
        pe.wait_ge(S("head_mean"), ROOT["sbk"])
        head_sum("mq", ones, inv_at["mq"], 6)
        head_sum("mk", ones, inv_at["mk"], 4)
        linear("gate", hn, part=(4, 4))
        pe.wait_ge(S("head_mean"), ROOT["mk"])
        for tt in range(2):
            for ft in range(4):
                last = nc.tensor.transpose(bank[4 + tt][:, ft * P:(ft + 1) * P], raw_v[:, ft, tt * P:(tt + 1) * P], ident)
        last.then_inc(S("vtok"), 1)
        pe.wait_ge(S("scaled"), 1)
        for ft in range(4):
            nc.tensor.transpose(bank[6][:, ft * P:(ft + 1) * P], bT[:, ft, 0:P], ident)
            last = nc.tensor.transpose(bank[7][:, ft * P:(ft + 1) * P], kT[:, ft, 0:P], ident)
        last.then_inc(S("bktok"), 1)
        barrier(pe, 1)
        for side, src in enumerate((bT, kT)):
            for G in range(4):
                if side:
                    pe.wait_ge(S("pairs_read"), G + 1)
                for hh in range(4):
                    h, c = 4 * (G % 2) + hh, G // 2
                    ft, o = h // 2, (h % 2) * 64
                    last = mm(bank[2 * G + hh % 2][:, (hh // 2) * T:(hh // 2 + 1) * T], src[o:o + 64, ft, c * P:(c + 1) * P],
                              AR[o:o + 64, ft, c, :, :], start=True, stop=True)
                last.then_inc(S("pairs"), 1)
        for G in range(4):
            pe.wait_ge(S("inv_start"), G + 1)
            pe.wait_ge(S("pairs_read"), 4 + G + 1)
            for hh in range(4):
                last = nc.tensor.transpose(bank[2 * G][:, hh * P:(hh + 1) * P], DT[G][:, hh, :], ident)
            last.then_inc(S("inv_flip"), 1)
        for lv in range(6):
            for G in range(4):
                if lv == 0:
                    pe.wait_ge(S("inv_flip_copied"), G + 1)
                else:
                    pe.wait_ge(S("inv"), 4 * (lv - 1) + G + 1)
                pe.wait_ge(S("cross"), 4 * lv + G + 1)
                for hh in range(4):
                    last = mm(bank[2 * G][:, hh * P:(hh + 1) * P], CT[G][:, hh, :], DD[G][:, hh, :], start=True, stop=True)
                last.then_inc(S("cd"), 1)
            for G in range(4):
                pe.wait_ge(S("cd_copied"), 4 * lv + G + 1)
                if lv < 5:
                    for hh in range(4):
                        mm(bank[2 * G + 1][:, hh * P:(hh + 1) * P], DT[G][:, hh, :], PP[G][:, hh, :], start=True, stop=True)
                for hh in range(4):
                    last = mm(bank[2 * G][:, hh * P:(hh + 1) * P], PP[G][:, hh, :], DT[G][:, hh, :], start=True, stop=True)
                last.then_inc(S("dcd"), 1)
        pe.wait_ge(S("inv"), 24)
        for c in range(2):
            for h in range(8):
                g, hh, ft, o = 2 * c + h // 4, h % 4, h // 2, (h % 2) * 64
                out = bank[4 * (h % 2)][:, ft * 64:ft * 64 + 64]
                last = mm(out, KA[g][:, hh, :], Vtok[:, c, h * 64:h * 64 + 64], start=True, stop=c == 0)
                if c:
                    last = mm(out, AR[o:o + 64, ft, 1, 0, :], S1[o:o + 64, ft, :], start=False, stop=True)
            last.then_inc(S("g_up"), 1)
            pe.wait_ge(S("g_copied"), c + 1)
            for h in range(8):
                last = mm(bank[1][:, h * 64:h * 64 + 64], DT[2 * c + h // 4][:, h % 4, :], Gs[:, h * 64:h * 64 + 64], start=True, stop=True)
            last.then_inc(S("u_up"), 1)
            pe.wait_ge(S("u_copied"), c + 1)
            for h in range(8):
                g, hh, ft, o = 2 * c + h // 4, h % 4, h // 2, (h % 2) * 64
                out = bank[2][o:o + 64, ft * P:(ft + 1) * P]
                mm(out, Us[:, h * 64:h * 64 + 64], RB[g][:, hh, :], start=True, stop=False)
                last = mm(out, Vtok[:, c, h * 64:h * 64 + 64], RK[g][:, hh, :], start=False, stop=c == 0)
                if c:
                    last = mm(out, S1[o:o + 64, ft, :], AR[o:o + 64, ft, 1, 1, :], start=False, stop=True)
            last.then_inc(S("y_up"), 1)
            if c == 0:
                for h in range(8):
                    ft, o = h // 2, (h % 2) * 64
                    out = bank[3][o:o + 64, ft * 64:(ft + 1) * 64]
                    mm(out, Btok[:, h * 64:h * 64 + 64], Us[:, h * 64:h * 64 + 64], start=True, stop=False)
                    last = mm(out, Ktok[:, h * 64:h * 64 + 64], Vtok[:, 0, h * 64:h * 64 + 64], start=False, stop=True)
                last.then_inc(S("state_up"), 1)
                pe.wait_ge(S("state_done"), 1)
                pe.wait_ge(S("y_copied"), 1)
        pe.wait_ge(S("y_copied"), 2)
        head_sum("gn_mean", blk64, Y, 4, wait=False)
        head_sum("gn_var", blk64, Vtok_sq, 6)
        barrier(pe, 2)

        for h in range(SH):
            if h >= 4:
                pe.wait_ge(S("sbz_taken"), h - 3)
            ft, o, b = h // 2, (h % 2) * 64, 4 + h % 4
            q, k = proj[o:o + 64, 14 + ft, :], proj[o:o + 64, 18 + ft, :]
            mm(bank[b][:, 0:T], k[:, 0:P], q, start=True, stop=True)
            mm(bank[b][:, T:T + P], k[:, P:T], q[:, P:T], start=True, stop=True).then_inc(S("sbz_up"), 1)
        linear("gate", hn, part=(8, 4))
        linear("gate", hn, part=(12, 4))
        for h in range(SH):
            pe.wait_ge(S("sb_soft"), h // 4 + 1)
            if h >= 4:
                pe.wait_ge(S("sbc_taken"), h - 3)
            b = 4 + h % 4
            mm(bank[b][:, 0:P], cst(C_SUFFIX), sbb[:, h, 0:P], start=True, stop=True)
            mm(bank[b][:, P:T], cst(C_SUFFIX), sbb[:, h, P:T], start=True, stop=False)
            mm(bank[b][:, P:T], ones, sbb[:, h, T:zc], start=False, stop=True)
            mm(bank[b][:, T:zc], cst(C_SUFFIX), sbb[:, h, T:zc], start=True, stop=True).then_inc(S("sbc_up"), 1)
        linear("gate", hn, part=(16, 4))
        pe.wait_ge(S("sb_attn"), 1)
        for h in range(SH):
            ft, o = h // 2, (h % 2) * 64
            out = bank[4 + ft][o:o + 64, :]
            v0, v1 = sbv[:, ft, 0, o:o + 64], sbv[:, ft, 1, o:o + 64]
            mm(out[:, 0:P], v0, sba[:, h, 0:P], start=True, stop=True)
            mm(out[:, P:T], v0, sba[:, h, P:T], start=True, stop=False)
            mm(out[:, P:T], v1, sba[:, h, T:zc], start=False, stop=True).then_inc(S("sbo_up"), 1)
        pe.wait_ge(S("sbo_taken"), 1)

        def att_score(name, n, hd, q, k, h):
            ft, o = h // (P // hd), (h % (P // hd)) * hd
            for tt in range(2):
                last = mm(bank[4 + h % 2][:, tt * T:(tt + 1) * T], q[o:o + hd, ft, tt * P:(tt + 1) * P], k[o:o + hd, ft, :],
                          start=True, stop=True)
            last.then_inc(S("att_s"), 1)

        def att_out(name, n, hd, q, k, v, h):
            ft, o = h // (P // hd), (h % (P // hd)) * hd
            pe.wait_ge(S("att_p"), HEAD0[name] + h + 1)
            for tt in range(2):
                for mt in range(2):
                    last = nc.tensor.transpose(bank[6][:, mt * T + tt * P:mt * T + (tt + 1) * P],
                                               att_p[ATT[name]][h % 2][:, tt, mt * P:(mt + 1) * P], ident)
            last.then_inc(S("att_t"), 1)
            if h + 2 < n:
                att_score(name, n, hd, q, k, h + 2)
            pe.wait_ge(S("att_tc"), HEAD0[name] + h + 1)
            if h >= 1:
                pe.wait_ge(S("att_oc"), HEAD0[name] + h)
            for mt in range(2):
                last = mm(bank[7][o:o + hd, 0:T], v(ft, mt, o), att_t[ATT[name]][h % 2][:, mt, :], start=mt == 0, stop=mt == 1)
            last.then_inc(S("att_o"), 1)

        mem = ("mem", MH, MHD, proj[:, 22:26, :], mk)
        att_score(*mem, 0)
        att_score(*mem, 1)
        linear("gate", hn, part=(20, 4))
        for h in range(MH):
            att_out(*mem, lambda ft, mt, o: mv[:, ft, mt, :], h)
        barrier(pe, 3)

        for n in range(3):
            if n:
                pe.wait_ge(S("branch_taken"), n)
            wide(PAGE0["branch"] + 4 * n, 4, ys[:, 4 * n:4 * n + 4, :])
        pe.wait_ge(S("branch_taken"), 3)
        linear("out", merged)
        barrier(pe, 4)
        norm_sum(2)
        pe.wait_ge(S("norm_out"), 3)
        linear("up", x_hi)
        barrier(pe, 5)
        wide(PAGE0["down"], FT, ff_hi, ff_lo)
        barrier(pe, 6)

        norm_sum(3)
        pe.wait_ge(S("norm_out"), 4)
        linear("in2", x_hi)
        linear("tok2", x_hi, by_token=True)
        barrier(pe, 7)
        moba = ("moba", BH, BHD, pj[:, 12:16, :], pj[:, 16:20, :])
        att_score(*moba, 0)
        att_score(*moba, 1)
        for lv in range(9):
            pe.wait_ge(S("h_sides"), lv + 1)
            if lv:
                pe.wait_ge(S("h_added"), lv)
            ql, kl = (hq, hk) if lv == 0 else (hQ, hK)
            for tt in range(2 if lv < 8 else 1):
                for h in range(GH):
                    s0, t0 = (tt * P, tt * P) if lv < 8 else (0, P)
                    last = mm(bank[tt][:, h * P:(h + 1) * P], kl[:, h, s0:s0 + P], ql[:, h, t0:t0 + P], start=True, stop=True)
            last.then_inc(S("h_pairs"), 1)
            if lv < BH:
                att_out(*moba, lambda ft, mt, o: tok2[:, ft, mt, o:o + 64], lv)
        pe.wait_ge(S("h_added"), 9)
        for h in range(GH):
            out = bank[2 + h // 2]
            c0 = (h % 2) * T
            mm(out[:, c0:c0 + P], tok2[:, 4 + h, 0, :], hacc[:, 0, h, :], start=True, stop=True)
            mm(out[:, c0 + P:c0 + T], tok2[:, 4 + h, 1, :], hacc[:, 1, h, :], start=True, stop=False)
            last = mm(out[:, c0 + P:c0 + T], tok2[:, 4 + h, 0, :], hx[:, h, :], start=False, stop=True)
        last.then_inc(S("h_out"), 1)
        head_sum("hn", ones, hE, 0)
        barrier(pe, 8)
        linear("out2", x_hi)
        barrier(pe, 9)
        norm_sum(4)
        pe.wait_ge(S("norm_out"), 5)
        linear("wq", x_hi)
        barrier(pe, 10)
        pe.wait_ge(S("subk_in"), 16)
        for tt in range(2):
            for hc in range(N_WQ):
                last = mm(bank[4 * tt + hc // 4][:, (hc % 4) * NK:(hc % 4 + 1) * NK], qp[:, hc, tt * P:(tt + 1) * P], subk[:, hc, :],
                          start=True, stop=True)
                if hc % 4 == 3:
                    last.then_inc(S("score_up"), 1)
        pe.wait_ge(S("score_taken"), 8)
        for tt in range(2):
            for k in range(KT):
                last = nc.tensor.transpose(bank[2 * tt + k // 4][:, (k % 4) * P:(k % 4 + 1) * P], hn[:, k, tt * P:(tt + 1) * P], ident)
        last.then_inc(S("htok_up"), 1)
        for tt in range(2):
            y = bank[2 * tt:2 * tt + 2]

            def add(slot, i, start, stop):
                pe.wait_ge(S("diag_ready"), i)
                for j in range(2):
                    last = mm(y[j][:, :], diag[:, slot, :], uv[slot][:, D + j * 512:D + (j + 1) * 512], start=start, stop=stop)
                last.then_inc(S("row_used"), 1)

            for s in range(UVS):
                add(s, tt * P + s + 1, s == 0, False)
            with pe.Fori(1, P // UVS - 1) as i:
                for s in range(UVS):
                    add(s, i * UVS + tt * P + s + 1, False, False)
            for s in range(UVS):
                add(s, tt * P + P - UVS + s + 1, False, s == UVS - 1)
        pe.wait_ge(S("y_tok"), 1)
        for tt in range(2):
            for k in range(KT):
                last = nc.tensor.transpose(bank[4 + k // 2][:, (k % 2) * T + tt * P:(k % 2) * T + (tt + 1) * P],
                                           yt[:, tt, k * P:(k + 1) * P], ident)
        last.then_inc(S("y_feat"), 1)
        norm_sum(5)

    @block.scalar
    def _(act):
        step = chain(act, "act_step")
        A_ = nc.scalar.activation
        act.dma_start(at(W0 + 4096, KT, T), A["memT"]).then_inc(S("mem_in"), 16)
        act.dma_start(lora_w[0:64, 0, :], A["decay_w2"]).then_inc(S("lora_w_in"), 16)
        act.dma_start(lora_w[64:128, 0, :], A["iclr_a2"]).then_inc(S("lora_w_in"), 16)
        act.dma_start(lora_w[:, 1, :], A["gate_g2"]).then_inc(S("lora_w_in"), 16)

        def norm_root(i):
            act.wait_ge(S("norm_mean"), i + 1)
            A_(norm_at[i][1], norm_at[i][1], ACT.Sqrt).then_inc(S("norm_root"), 1)

        def head_root(name, dst):
            act.wait_ge(S("head_mean"), ROOT[name])
            A_(dst, dst, ACT.Sqrt).then_inc(S("head_root"), 1)

        def high(page, i=None):
            n = 16 * (page // SLOTS + 1)
            act.wait_ge(S(f"page_in{page % SLOTS}"), n if i is None else i * 16 + n)
            act.wait_ge(S("page_done"), page - 3 if i is None else i * SLOTS + page - 3)
            A_(w_hi[:, page % SLOTS, :], ring[:, page % SLOTS, :], ACT.Copy).then_inc(S("hi_ready"), 1)

        def high_ahead(page, i=None):
            if page >= SPLIT0 and page + 3 < N_PAGES:
                high(page + 3, i)

        def take(stage, dst, func=ACT.Copy, part=None):
            first, n = part or (0, COUNTS[STAGES.index(stage)])
            page0 = PAGE0[stage] + first
            dst = dst[:, first:first + n, :]

            def one(b, i=None):
                page = page0 + b
                high_ahead(page, i)
                act.wait_ge(S("page_done"), page + 1 if i is None else i * SLOTS + page + 1)
                out = dst[:, b, :] if i is None else dst[:, bass.ds(i * SLOTS + b, 1), :]
                src = bank[page % SLOTS][:, 0:T]
                A_(out, src if i is None else src.unsqueeze(1), func).then_inc(S("tile_taken"), 1)

            groups = n // SLOTS
            if page0 + n == N_PAGES:
                groups -= 1
            if groups > 1:
                with act.Fori(0, groups) as i:
                    for b in range(SLOTS):
                        one(b, i)
            else:
                for b in range(groups * SLOTS):
                    one(b)
            for b in range(groups * SLOTS, n):
                one(b)

        def flat(v):
            return v.rearrange("p a b c -> p a (b c)")

        act.wait_ge(S("const_in"), 16)
        act.wait_ge(S("vec_in"), 16)
        for _ in range(SLOTS):
            act.drain().then_inc(S("tile_taken"), 1)
        norm_root(0)
        norm_root(1)
        take("in_a", proj)
        act.wait_ge(S("shifted"), 1)
        step(A_(proj[0:64, 12, :], proj[0:64, 12, :], ACT.Tanh))
        A_(proj[:, 13, :], proj[:, 13, :], ACT.Sigmoid).then_inc(S("lora_act"), 1)
        act.wait_ge(S("lora_up"), 1)
        for ft in range(4):
            col = (ft % 2) * T
            A_(logw[:, ft, :], bank[4 + ft // 2][:, col:col + T], ACT.Sigmoid, bias=V("decay_w0", ft))
            last = A_(iclr[:, ft, :], bank[6 + ft // 2][:, col:col + T], ACT.Sigmoid, bias=V("iclr_a0", ft))
        last.then_inc(S("lora_taken"), 1)
        take("sbv", flat(sbv))
        take("mk", mk)
        act.wait_ge(S("gate_up"), 1)
        A_(gT[:, 0:2, :], two(bank[4][:, :], T), ACT.Copy)
        A_(gT[:, 2:4, :], two(bank[5][:, :], T), ACT.Copy).then_inc(S("gate_taken"), 1)
        head_root("kk", tmp2)
        take("mv", flat(mv))
        head_root("sbq", inv_at["sbq"])
        head_root("sbk", inv_at["sbk"])
        act.wait_ge(S("cum_ready"), 1)
        A_(tmp1, cc, ACT.Exp).then_inc(S("exp_to"), 1)
        act.wait_ge(S("exp_to_used"), 1)
        A_(tmp2, cc, ACT.Exp, scale=-1.0).then_inc(S("exp_from"), 1)
        A_(tmp3, logw, ACT.Exp).then_inc(S("exp_before"), 1)
        act.wait_ge(S("fac_ready"), 1)
        A_(fac, fac, ACT.Exp).then_inc(S("fac_exp"), 1)
        take("gate", gates, ACT.Sigmoid, part=(0, 4))
        head_root("mq", inv_at["mq"])
        head_root("mk", inv_at["mk"])
        take("gate", gates, ACT.Sigmoid, part=(4, 4))
        act.wait_ge(S("vtok"), 1)
        for tt in range(2):
            A_(Vtok[:, tt, :], bank[4 + tt][:, :], ACT.Copy)
        act.wait_ge(S("bktok"), 1)
        A_(Btok, bank[6][:, :], ACT.Copy)
        A_(Ktok, bank[7][:, :], ACT.Copy)
        barrier(act, 1)
        for G in range(4):
            act.wait_ge(S("inv_flip"), G + 1)
            A_(DD[G], two(bank[2 * G][:, :], P), ACT.Copy).then_inc(S("inv_flip_copied"), 1)
        for lv in range(6):
            for G in range(4):
                act.wait_ge(S("cd"), 4 * lv + G + 1)
                A_(PP[G], two(bank[2 * G][:, :], P), ACT.Copy).then_inc(S("cd_copied"), 1)
        for c in range(2):
            act.wait_ge(S("g_up"), c + 1)
            gp = Gs.rearrange("p (f o i) -> p f o i", o=2, i=64)
            A_(gp[:, :, 0, :], two(bank[0][:, 0:T], 64), ACT.Copy, scale=-1.0)
            A_(gp[:, :, 1, :], two(bank[4][:, 0:T], 64), ACT.Copy, scale=-1.0).then_inc(S("g_copied"), 1)
            act.wait_ge(S("u_up"), c + 1)
            A_(Us, bank[1][:, :], ACT.Copy).then_inc(S("u_copied"), 1)
            act.wait_ge(S("y_up"), c + 1)
            A_(Y[:, :, c * P:(c + 1) * P], two(bank[2][:, :], P), ACT.Copy).then_inc(S("y_copied"), 1)
        head_root("gn_var", tmp2)
        barrier(act, 2)

        for h in range(SH):
            act.wait_ge(S("sbz_up"), h + 1)
            A_(sbz[:, h, :], bank[4 + h % 4][:, 0:zc], ACT.Copy).then_inc(S("sbz_taken"), 1)
        for half in range(2):
            r = slice(4 * half, 4 * half + 4)
            act.wait_ge(S("sb_negabs"), half + 1)
            step(A_(sba[:, r, :], sba[:, r, :], ACT.Exp))
            A_(sba[:, r, :], sba[:, r, :], ACT.Ln, bias=1.0).then_inc(S("sb_log"), 1)
        take("gate", gates, ACT.Sigmoid, part=(8, 4))
        take("gate", gates, ACT.Sigmoid, part=(12, 4))
        act.wait_ge(S("sb_logit"), 1)
        A_(sba[:, :, :], sba[:, :, :], ACT.Exp).then_inc(S("sb_exp"), 1)
        take("gate", gates, ACT.Sigmoid, part=(16, 4))
        for ft in range(4):
            act.wait_ge(S("sbo_up"), 2 * ft + 2)
            last = A_(ys[:, 4 + ft, :], bank[4 + ft][:, 0:T], ACT.Copy)
        last.then_inc(S("sbo_taken"), 1)

        def att_exp(name, h):
            act.wait_ge(S("att_z"), HEAD0[name] + h + 1)
            for tt in range(2):
                last = A_(att_p[ATT[name]][h % 2][:, tt, :], att_z[ATT[name]][h % 2][:, tt, :], ACT.Exp, bias=att_m[ATT[name]][h % 2][:, tt:tt + 1],
                          accum_out=att_s[ATT[name]][h % 2][:, tt:tt + 1])
            last.then_inc(S("att_e"), 1)

        def att_take(name, hd, dst, h):
            ft, o = h // (P // hd), (h % (P // hd)) * hd
            act.wait_ge(S("att_t"), HEAD0[name] + h + 1)
            A_(att_t[ATT[name]][h % 2], two(bank[6][:, :], T), ACT.Copy).then_inc(S("att_tc"), 1)
            act.wait_ge(S("att_o"), HEAD0[name] + h + 1)
            A_(dst[o:o + hd, ft, :], bank[7][o:o + hd, 0:T], ACT.Copy).then_inc(S("att_oc"), 1)

        att_exp("mem", 0)
        take("gate", gates, ACT.Sigmoid, part=(20, 4))
        for h in range(MH):
            if h + 1 < MH:
                att_exp("mem", h + 1)
            att_take("mem", MHD, ys[:, 8:12, :], h)
        barrier(act, 3)
        barrier(act, 4)
        for page in range(SPLIT0, SPLIT0 + 3):
            high(page)
        norm_root(2)
        page0 = PAGE0["up"]
        with act.Fori(0, N_UP // 4) as i:
            for b in range(4):
                high_ahead(page0 + b, i)
                if b == 0:
                    act.wait_ge(S("glu_done"), i * 2 + 2)
                act.wait_ge(S("page_done"), i * 4 + page0 + b + 1)
                cw = vec[:, bass.ds(i * 4 + VCOL["conv_w2"] + b, 1)]
                cb = vec[:, bass.ds(i * 4 + VCOL["conv_b"] + b, 1)]
                A_(conv_u[:, b, :], bank[(page0 + b) % SLOTS][:, 0:T], ACT.Identity, bias=cb, scale=cw)\
                    .then_inc(S("conv_centre"), 1)
            for pr in range(2):
                act.wait_ge(S("tile_taken"), i * 4 + SLOTS + TILE0["up"] + 2 * pr + 1)
                A_(sig_u[:, pr, :], conv_u[:, 2 * pr, :], ACT.Sigmoid).then_inc(S("glu_sig"), 1)
        barrier(act, 5)
        for page in range(PAGE0["down"], PAGE0["down"] + N_DOWN):
            high_ahead(page)
        barrier(act, 6)
        norm_root(3)
        take("in2", pj, part=(0, 12))
        act.wait_ge(S("tile_taken"), SLOTS + TILE0["in2"] + 12)
        act.wait_ge(S("lb_diff"), 1)
        A_(hE, pj[:, 4:8, :], ACT.Sigmoid)
        A_(hQ, pj[:, 0:4, :], ACT.Sigmoid)
        A_(hK, pj[:, 8:12, :], ACT.Sigmoid)
        A_(lbv[:, 4:8], lbv[:, 0:4], ACT.Sigmoid).then_inc(S("h_sig"), 1)
        take("in2", pj, part=(12, 8))
        act.wait_ge(S("h_f"), 1)
        A_(hE, hf, ACT.Ln).then_inc(S("h_log"), 1)
        take("tok2", flat(tok2))
        barrier(act, 7)
        att_exp("moba", 0)
        for lv in range(9):
            if lv < 8:
                act.wait_ge(S("h_diff"), lv + 1)
                A_(hE, hE, ACT.Exp).then_inc(S("h_exp"), 1)
                if lv + 1 < BH:
                    att_exp("moba", lv + 1)
                att_take("moba", BHD, cat[:, 0:4, :], lv)
        head_root("hn", hE)
        barrier(act, 8)
        for page in range(PAGE0["out2"], PAGE0["out2"] + N_OUT2):
            high_ahead(page)
        barrier(act, 9)
        norm_root(4)
        take("wq", qp)
        act.dma_start(subk, A["subkT"]).then_inc(S("subk_in"), 16)
        barrier(act, 10)
        for q in range(8):
            act.wait_ge(S("score_up"), q + 1)
            A_(scores[:, q // 4, 4 * (q % 4):4 * (q % 4) + 4, :], two(bank[q][:, :], NK), ACT.Copy).then_inc(S("score_taken"), 1)
        act.wait_ge(S("htok_up"), 1)
        for tt in range(2):
            for j in range(2):
                last = A_(htok[:, tt, j * 512:(j + 1) * 512], bank[2 * tt + j][:, :], ACT.Copy)
        last.then_inc(S("htok_in"), 1)

        def soft_exp(j):
            act.wait_ge(S("soft_in"), j + 1)
            A_(soft[:, j, :], soft[:, j, :], ACT.Exp, accum_out=rsum[:, j:j + 1]).then_inc(S("soft_exp"), 1)

        soft_exp(0)
        soft_exp(1)
        for j in range(2 * PH):
            with act.Fori(0, TOPK // UVS) as i:
                for s in range(UVS):
                    act.wait_ge(S("dot_ready"), i * UVS + j * TOPK + s + 1)
                    A_(e_gelu[:, s:s + 1], e_act[:, s:s + 1], ACT.Gelu).then_inc(S("gelu_ready"), 1)
            if j + 2 < 2 * PH:
                soft_exp(j + 2)
        act.wait_ge(S("row_used"), 2 * P)
        for tt in range(2):
            for j in range(2):
                last = A_(yt[:, tt, j * 512:(j + 1) * 512], bank[2 * tt + j][:, :], ACT.Copy)
        last.then_inc(S("y_tok"), 1)
        norm_root(5)

    @block.vector
    def _(dve):
        step = chain(dve, "dve_step")
        v = nc.vector
        tt_ = v.tensor_tensor
        stt = v.scalar_tensor_tensor
        ts = v.tensor_scalar

        def norm(i, src, gain, dst, out_sem="norm_out"):
            nsq, nroot, ninv = norm_at[i]
            tt_(nsq, src, src, ALU.mult).then_inc(S("norm_sq"), 1)
            dve.wait_ge(S("norm_sum"), i + 1)
            ts(nroot, bank[4][:, 0:T], 1.0 / D, 1e-6, ALU.mult, ALU.add).then_inc(S("norm_mean"), 1)
            dve.wait_ge(S("norm_root"), i + 1)
            step(v.reciprocal(ninv, nroot))
            for k in range(KT):
                last = stt(dst[:, k, :], src[:, k, :], V(gain, k), ninv, ALU.mult, ALU.mult)
            if i in (2, 3, 4):
                step(last)
                last = split(dst)
            last.then_inc(S(out_sem), 1)

        def split(src):
            step(v.tensor_copy(x_hi, src))
            return tt_(x_lo, src, x_hi.bitcast(F32), ALU.subtract)

        def head_inv(name, src, sq, root, b0, scale, eps):
            tt_(sq, src, src, ALU.mult).then_inc(S("head_sq"), 1)
            head_mean(name, root, b0, scale, eps)
            head_recip(name, root)

        def head_mean(name, root, b0, scale, eps):
            dve.wait_ge(S("head_sum"), SUM[name])
            for j in range(2):
                last = ts(root[:, 2 * j:2 * j + 2, :], two(bank[b0 + j][:, :], T), scale, eps, ALU.mult, ALU.add)
            last.then_inc(S("head_mean"), 1)

        def head_recip(name, root):
            dve.wait_ge(S("head_root"), ROOT[name])
            step(v.reciprocal(root, root))

        dve.wait_ge(S("const_in"), 16)
        dve.wait_ge(S("vec_in"), 16)
        dve.wait_ge(S("x_in"), 16)
        norm(0, x, "norm1_g", hn)
        dve.wait_ge(S("norm_out"), 1)
        dve.wait_ge(S("mem_in"), 16)
        norm(1, at(W0 + 4096, KT, T), "mem_g", memn)

        dve.wait_ge(S("tile_taken"), SLOTS + 14)
        tt_(shift_d[:, :, 1:T], proj[:, 0:14, 0:T - 1], proj[:, 0:14, 1:T], ALU.subtract)
        step(ts(shift_d[:, :, 0:1], proj[:, 0:14, 0:1], -1.0, None, ALU.mult))
        for i in list(range(12, 14)) + list(range(12)):
            last = stt(proj[:, i, :], shift_d[:, i, :], V("mu", i), proj[:, i, :], ALU.mult, ALU.add)
        done(dve, last, "shifted", 1)
        for ft in range(4):
            last = ts(kk[:, ft, :], raw_k[:, ft, :], V("k_k", ft), None, ALU.mult)
        step(last)
        tt_(tmp2, kk, kk, ALU.mult).then_inc(S("head_sq"), 1)
        dve.wait_ge(S("lora_taken"), 1)
        for ft in range(4):
            last = ts(tmp1[:, ft, :], iclr[:, ft, :], -1.0, V("k_a", ft), ALU.add, ALU.mult)
        step(last)
        step(stt(raw_k, tmp1, 1.0, raw_k, ALU.add, ALU.mult))
        for ft in range(4):
            last = stt(tmp3[:, ft, :], raw_r[:, ft, :], V("r_k", ft), raw_k[:, ft, :], ALU.mult, ALU.mult)
        last.then_inc(S("head_sq"), 1)
        dve.wait_ge(S("head_sum"), SUM["kk"])
        for j in range(2):
            last = ts(tmp2[:, 2 * j:2 * j + 2, :], two(bank[6 + j][:, :], T), 1e-24, None, ALU.max)
        last.then_inc(S("head_mean"), 1)
        dve.wait_ge(S("head_root"), ROOT["kk"])
        step(v.reciprocal(tmp2, tmp2))
        step(tt_(kk, kk, tmp2, ALU.mult))
        dve.wait_ge(S("head_sum"), SUM["bonus"])
        for j in range(2):
            last = tt_(bonus[:, 2 * j:2 * j + 2, :], two(bank[4 + j][:, :], T), raw_v[:, 2 * j:2 * j + 2, :], ALU.mult)
        last.then_inc(S("bonus_done"), 1)
        sq, sk, mq = proj[:, 14:18, :], proj[:, 18:22, :], proj[:, 22:26, :]
        for name, src in (("sbq", sq), ("sbk", sk)):
            tt_(inv_at[name], src, src, ALU.mult).then_inc(S("head_sq"), 1)
        step(ts(logw, logw, DECAY_SCALE, None, ALU.mult))
        step(v.memset(tmp1, 1.0))
        for ft in range(4):
            for c in range(2):
                r = slice(c * P, (c + 1) * P)
                last = v.tensor_tensor_scan(cc[:, ft, r], tmp1[:, ft, r], logw[:, ft, r], 0.0, ALU.mult, ALU.add)
        step(last)
        c8 = cc.rearrange("p a (c t) -> p (a c) t", t=P)
        step(v.tensor_copy(mid.unsqueeze(2), c8[:, :, 63:64]))
        step(tt_(c8, c8, each(mid, P), ALU.subtract))
        last = tt_(logw, cc, logw, ALU.subtract)
        done(dve, last, "cum_ready", 1)
        head_mean("sbq", inv_at["sbq"], 6, 1.0 / SHD, 1e-6)
        head_mean("sbk", inv_at["sbk"], 4, 1.0 / SHD, 1e-6)
        for name, src in (("mq", mq), ("mk", mk)):
            tt_(inv_at[name], src, src, ALU.mult).then_inc(S("head_sq"), 1)
        mid2 = mid.rearrange("p (a c) -> p a c", c=2)
        tt_(fac, cc[:, :, P - 1:P], mid2[:, :, 1:2], ALU.add).then_inc(S("fac_ready"), 1)
        dve.wait_ge(S("exp_to"), 1)
        c4 = lambda t_: t_.rearrange("p a (c t) -> p a c t", t=P)
        for ft in range(4):
            last = tt_(AR[:, ft, :, 1, :], c4(raw_r)[:, ft, :, :], c4(tmp1)[:, ft, :, :], ALU.mult)
        last.then_inc(S("exp_to_used"), 1)
        dve.wait_ge(S("exp_from"), 1)
        step(tt_(iclr, iclr, kk, ALU.mult))
        tt_(bT, iclr, tmp2, ALU.mult)
        tt_(kT, raw_k, tmp2, ALU.mult)
        dve.wait_ge(S("exp_before"), 1)
        for ft in range(4):
            last = tt_(AR[:, ft, :, 0, :], c4(kk)[:, ft, :, :], c4(tmp3)[:, ft, :, :], ALU.mult)
        last.then_inc(S("scaled"), 1)
        head_recip("sbq", inv_at["sbq"])
        head_recip("sbk", inv_at["sbk"])
        step(stt(sq, sq, V("sb_q_g"), inv_at["sbq"], ALU.mult, ALU.mult))
        stt(sk, sk, V("sb_k_g"), inv_at["sbk"], ALU.mult, ALU.mult)
        ts(sq, sq, SHD ** -0.5, None, ALU.mult)
        head_mean("mq", inv_at["mq"], 6, 1.0 / MHD, 1e-6)
        head_mean("mk", inv_at["mk"], 4, 1.0 / MHD, 1e-6)
        head_recip("mq", inv_at["mq"])
        head_recip("mk", inv_at["mk"])
        stt(mq, mq, V("mem_q_g"), inv_at["mq"], ALU.mult, ALU.mult)
        stt(mk, mk, V("mem_k_g"), inv_at["mk"], ALU.mult, ALU.mult)
        barrier(dve, 1)

        strict, incl = many(cst(C_STRICT), 2), many(cst(C_INCL), 2)
        for side in range(2):
            for G in range(4):
                dve.wait_ge(S("pairs"), 4 * side + G + 1)
                for q in range(2):
                    pb = bank[2 * G + q][:, :].rearrange("p (h s t) -> p h s t", h=2, s=2)
                    hs = slice(q, 4, 2)
                    if side == 0:
                        stt(MT[G][:, hs, :], pb[:, :, 0, :], -1.0, strict, ALU.mult, ALU.mult)
                        last = tt_(RB[G][:, hs, :], pb[:, :, 1, :], incl, ALU.mult)
                    else:
                        tt_(KA[G][:, hs, :], pb[:, :, 0, :], strict, ALU.mult)
                        last = tt_(RK[G][:, hs, :], pb[:, :, 1, :], incl, ALU.mult)
                done(dve, last, "pairs_read", 4 * side + G + 1)
                if side == 0:
                    step(tt_(DT[G], MT[G], many(cst(C_LEVEL), 4), ALU.mult))
                    tt_(DT[G], DT[G], many(ident, 4), ALU.add).then_inc(S("inv_start"), 1)
                    tt_(CT[G], MT[G], many(cst(C_LEVEL + P), 4), ALU.mult).then_inc(S("cross"), 1)
        for lv in range(6):
            for G in range(4):
                dve.wait_ge(S("dcd"), 4 * lv + G + 1)
                if lv < 5:
                    tt_(DD[G], DD[G], two(bank[2 * G + 1][:, :], P), ALU.add)
                tt_(DT[G], DT[G], two(bank[2 * G][:, :], P), ALU.add).then_inc(S("inv"), 1)
                if lv < 5:
                    tt_(CT[G], MT[G], many(cst(C_LEVEL + P * (lv + 2)), 4), ALU.mult).then_inc(S("cross"), 1)
        dve.wait_ge(S("state_up"), 1)
        dve.wait_ge(S("fac_exp"), 1)
        tt_(S1, two(bank[3][:, 0:T], 64), fac.broadcast_to([P, 4, 64]), ALU.mult).then_inc(S("state_done"), 1)
        dve.wait_ge(S("y_copied"), 2)
        dve.wait_ge(S("head_sum"), SUM["gn_mean"])
        for j in range(2):
            last = stt(Y[:, 2 * j:2 * j + 2, :], two(bank[4 + j][:, :], T), -1.0 / RHD, Y[:, 2 * j:2 * j + 2, :], ALU.mult, ALU.add)
        step(last)
        head_inv("gn_var", Y, Vtok_sq, tmp2, 6, 1.0 / RHD, 64e-5)
        step(tt_(Y, Y, tmp2, ALU.mult))
        for ft in range(4):
            last = ts(Y[:, ft, :], Y[:, ft, :], V("lnx_g", ft), V("lnx_b", ft), ALU.mult, ALU.add)
        step(last)
        step(tt_(Y, Y, bonus, ALU.add))
        tt_(ys[:, 0:4, :], Y, gT, ALU.mult)
        barrier(dve, 2)

        strict8 = lambda n: many(cst(C_STRICT), n)
        for half in range(2):
            r = slice(4 * half, 4 * half + 4)
            dve.wait_ge(S("sbz_taken"), 4 * half + 4)
            stt(sba[:, r, :], sbz[:, r, :], -1.0, sbz[:, r, :], ALU.mult, ALU.min).then_inc(S("sb_negabs"), 1)
            dve.wait_ge(S("sb_log"), half + 1)
            step(stt(sbb[:, r, :], sbz[:, r, :], 0.0, sba[:, r, :], ALU.max, ALU.add))
            tt_(sbb[:, r, 0:P], sbb[:, r, 0:P], strict8(4), ALU.mult)
            tt_(sbb[:, r, T:zc], sbb[:, r, T:zc], strict8(4), ALU.mult).then_inc(S("sb_soft"), 1)
        for h in range(SH):
            dve.wait_ge(S("sbc_up"), h + 1)
            tt_(sba[:, h, :], sbz[:, h, :], bank[4 + h % 4][:, 0:zc], ALU.subtract).then_inc(S("sbc_taken"), 1)
        dve.wait_ge(S("sbc_taken"), SH)
        ts(sba[:, :, :], sba[:, :, :], 0.0, None, ALU.min).then_inc(S("sb_logit"), 1)
        dve.wait_ge(S("sb_exp"), 1)
        tt_(sba[:, :, 0:P], sba[:, :, 0:P], strict8(8), ALU.mult)
        tt_(sba[:, :, T:zc], sba[:, :, T:zc], strict8(8), ALU.mult).then_inc(S("sb_attn"), 1)

        def att_logits(name, scale, bias, h):
            z, m = att_z[ATT[name]][h % 2], att_m[ATT[name]][h % 2]
            dve.wait_ge(S("att_s"), HEAD0[name] + h + 1)
            src = two(bank[4 + h % 2][:, :], T)
            if bias is None:
                step(ts(z, src, scale, None, ALU.mult))
            else:
                step(stt(z, src, scale, two(bias[:, h, :], T), ALU.mult, ALU.add))
            step(v.reduce_max(m, z, AX.X))
            ts(m, m, -1.0, None, ALU.mult).then_inc(S("att_z"), 1)

        def att_share(name, h):
            dve.wait_ge(S("att_e"), HEAD0[name] + h + 1)
            step(v.reciprocal(att_r[ATT[name]][h % 2], att_s[ATT[name]][h % 2]))
            tt_(att_p[ATT[name]][h % 2], att_p[ATT[name]][h % 2], each(att_r[ATT[name]][h % 2], T), ALU.mult).then_inc(S("att_p"), 1)

        att_logits("mem", MHD ** -0.5, None, 0)
        for h in range(MH):
            if h + 1 < MH:
                att_logits("mem", MHD ** -0.5, None, h + 1)
            att_share("mem", h)
        barrier(dve, 3)

        for n in range(3):
            dve.wait_ge(S("page_done"), PAGE0["branch"] + 4 * (n + 1))
            for j in range(KT):
                if n == 0:
                    last = tt_(merged[:, j, :], bank[j][:, 0:T], gates[:, j, :], ALU.mult)
                else:
                    gj = gates[:, 8 * n + j, :]
                    last = tt_(gj, bank[j][:, 0:T], gj, ALU.mult)
            done(dve, last, "branch_read", n + 1)
            if n:
                last = tt_(merged, merged, gates[:, 8 * n:8 * n + 8, :], ALU.add)
            else:
                last = dve.drain()
            done(dve, last, "branch_taken", n + 1)

        def add_tiles(stage):
            for j in range(KT):
                page = PAGE0[stage] + j
                dve.wait_ge(S("page_done"), page + 1)
                tt_(x[:, j, :], bank[page % SLOTS][:, 0:T], x[:, j, :], ALU.add).then_inc(S("tile_taken"), 1)

        add_tiles("out")
        barrier(dve, 4)
        norm(2, x, "norm2_g", hn)
        for _ in range(2):
            dve.drain().then_inc(S("glu_done"), 1)
        with dve.Fori(0, N_UP // 4) as i:
            for b in range(4):
                src = bank[(PAGE0["up"] + b) % SLOTS]
                w1 = vec[:, bass.ds(i * 4 + VCOL["conv_w1"] + b, 1)]
                w0 = vec[:, bass.ds(i * 4 + VCOL["conv_w0"] + b, 1)]
                dve.wait_ge(S("conv_centre"), i * 4 + b + 1)
                stt(conv_u[:, b, 1:T], src[:, 0:T - 1], w1, conv_u[:, b, 1:T], ALU.mult, ALU.add).then_inc(S("conv_tap"), 1)
                dve.wait_ge(S("conv_tap"), i * 4 + b + 1)
                stt(conv_u[:, b, 2:T], src[:, 0:T - 2], w0, conv_u[:, b, 2:T], ALU.mult, ALU.add).then_inc(S("tile_taken"), 1)
            for pr in range(2):
                dve.wait_ge(S("glu_sig"), i * 2 + pr + 1)
                tt_(sig_u[:, pr, :], sig_u[:, pr, :], conv_u[:, 2 * pr, :], ALU.mult).then_inc(S("glu_silu"), 1)
                dve.wait_ge(S("glu_silu"), i * 6 + 3 * pr + 1)
                tt_(glu[:, pr, :], sig_u[:, pr, :], conv_u[:, 2 * pr + 1, :], ALU.mult).then_inc(S("glu_silu"), 1)
                dve.wait_ge(S("glu_silu"), i * 6 + 3 * pr + 2)
                hi = ff_hi[:, bass.ds(i * 2 + pr, 1), :]
                v.tensor_copy(hi, glu[:, pr:pr + 1, :]).then_inc(S("glu_silu"), 1)
                dve.wait_ge(S("glu_silu"), i * 6 + 3 * pr + 3)
                tt_(ff_lo[:, bass.ds(i * 2 + pr, 1), :], glu[:, pr:pr + 1, :], hi.bitcast(F32), ALU.subtract)\
                    .then_inc(S("glu_done"), 1)
        barrier(dve, 5)
        dve.wait_ge(S("page_done"), PAGE0["down"] + N_DOWN)
        for j in range(KT):
            tt_(x[:, j, :], bank[j][:, 0:T], x[:, j, :], ALU.add)
        barrier(dve, 6)

        norm(3, x, "norm1_g_2", hn)
        for h in range(BH):
            ts(bias_h[:, h, :], cst(C_ALIBI, 2 * T), 2.0 ** (-8.0 * (h + 1) / BH), None, ALU.mult)
        tt_(lbv[:, 0:4], vec[:, VCOL["lb0"]:VCOL["lb0"] + 4], vec[:, VCOL["lb1"]:VCOL["lb1"] + 4], ALU.subtract)\
            .then_inc(S("lb_diff"), 1)
        dve.wait_ge(S("h_sig"), 1)
        step(ts(lbv[:, 8:12], lbv[:, 4:8], -1.0, 1.0, ALU.mult, ALU.add))
        for h in range(GH):
            last = ts(hf[:, h, :], hE[:, h, :], lbv[:, 8 + h:9 + h], lbv[:, 4 + h:5 + h], ALU.mult, ALU.add)
        done(dve, last, "h_f", 1)
        ts(hk, hf, -1.0, 1.0, ALU.mult, ALU.add)
        tt_(hq, hQ, pj[:, 0:4, :], ALU.mult)
        tt_(pj[:, 8:12, :], hK, pj[:, 8:12, :], ALU.mult).then_inc(S("h_sides"), 1)
        dve.wait_ge(S("h_sides"), 1)
        step(v.memset(hQ, 1.0))
        dve.wait_ge(S("h_log"), 1)
        for h in range(GH):
            last = v.tensor_tensor_scan(hcum[:, h, :], hQ[:, h, :], hE[:, h, :], 0.0, ALU.mult, ALU.add)
        step(last)
        barrier(dve, 7)

        def level_diff(lv):
            half = (LEVELS + [P])[lv - 1]
            cb = hcum.rearrange("p h (b c) -> p (h b) c", c=2 * half)
            eb = hE.rearrange("p h (b c) -> p (h b) c", c=2 * half)
            step(tt_(eb, cb, cb[:, :, half - 1:half].broadcast_to([P, cb.shape[1], 2 * half]), ALU.subtract))
            stt(hE, hE, -1.0, hE, ALU.mult, ALU.min).then_inc(S("h_diff"), 1)

        def level_add(lv):
            dve.wait_ge(S("h_pairs"), lv + 1)
            if lv == 0:
                for tt in range(2):
                    last = tt_(hacc[:, tt, :, :], two(bank[tt][:, :], P), many(ident, 4), ALU.mult)
            elif lv < 8:
                for tt in range(2):
                    last = tt_(hmul[:, 4 * tt:4 * tt + 4, :], two(bank[tt][:, :], P), many(cst(C_LEVEL + P * (lv - 1)), 4),
                               ALU.mult)
                step(last)
                for tt in range(2):
                    last = tt_(hacc[:, tt, :, :], hacc[:, tt, :, :], hmul[:, 4 * tt:4 * tt + 4, :], ALU.add)
            else:
                last = v.tensor_copy(hx, two(bank[0][:, :], P))
            done(dve, last, "h_added", lv + 1)

        att_logits("moba", BHD ** -0.5, bias_h, 0)
        for lv in range(9):
            if lv < 8:
                level_diff(lv + 1)
                if lv + 1 < BH:
                    att_logits("moba", BHD ** -0.5, bias_h, lv + 1)
                dve.wait_ge(S("h_exp"), lv + 1)
                dve.wait_ge(S("h_pairs"), lv + 1)
                tt_(hQ, hq, hE, ALU.mult)
                done(dve, tt_(hK, hk, hE, ALU.mult), "h_sides", lv + 2)
                att_share("moba", lv)
            level_add(lv)
        dve.wait_ge(S("h_out"), 1)
        for j in range(2):
            last = v.tensor_copy(hf[:, 2 * j:2 * j + 2, :], two(bank[2 + j][:, :], T))
        step(last)
        head_inv("hn", hf, hE, hE, 0, 1.0 / P, 1e-6)
        for h in range(GH):
            last = stt(hf[:, h, :], hf[:, h, :], V("rec_g", h), hE[:, h, :], ALU.mult, ALU.mult)
        step(last)
        step(tt_(cat[:, 4:8, :], hf, pj[:, 8:12, :], ALU.mult))
        dve.wait_ge(S("att_oc"), MH + BH)
        split(cat)
        barrier(dve, 8)
        add_tiles("out2")
        barrier(dve, 9)
        norm(4, x, "norm2_g_2", hn)
        barrier(dve, 10)

        def rank(j):
            tt, h = j // PH, j % PH
            dve.wait_ge(S("score_taken"), j // 2 + 1)
            hs = (2 * h, 2 * h + 1)
            sc = [scores[:, tt, hc, :] for hc in hs]
            wk = [work[:, i * NK:(i + 1) * NK] for i in range(2)]
            for i in range(2):
                last = v.max(top_v[:, i, 0:8], sc[i])
            step(last)
            for i in range(2):
                v.max_index(top_i[:, i, 0:8], top_v[:, i, 0:8], sc[i])
            for i in range(2):
                last = v.match_replace(wk[i], top_v[:, i, 0:8], sc[i], -BIG)
            step(last)
            for i in range(2):
                last = v.max(top_v[:, i, 8:16], wk[i])
            step(last)
            for i in range(2):
                v.max_index(top_i[:, i, 8:16], top_v[:, i, 8:16], wk[i])
            step(tt_(two(cand, TOPK), each(top_v[:, 0, :], TOPK), many(top_v[:, 1, :], TOPK), ALU.add))
            v.tensor_copy(top_f, top_i)
            step(v.max(sel_v[:, 0:8], cand))
            v.max_index(pos_u[:, 0:8], sel_v[:, 0:8], cand)
            step(v.match_replace(work, sel_v[:, 0:8], cand, -BIG))
            step(v.max(sel_v[:, 8:16], work))
            step(v.max_index(pos_u[:, 8:16], sel_v[:, 8:16], work))
            ts(soft[:, j, :], sel_v, sel_v[:, 0:1], None, ALU.subtract).then_inc(S("soft_in"), 1)
            ts(place_u[:, 0, :], pos_u, 4, None, ALU.logical_shift_right)
            step(ts(place_u[:, 1, :], pos_u, 15, None, ALU.bitwise_and))
            step(v.tensor_copy(place_f, place_u))
            for i in range(2):
                last = tt_(eqm[:, i, :, :], each(place_f[:, i, :], TOPK), many(cst(C_IOTA, TOPK), TOPK), ALU.is_equal)
            step(last)
            for i in range(2):
                last = tt_(eqm[:, i, :, :], eqm[:, i, :, :], many(top_f[:, i, :], TOPK), ALU.mult)
            step(last)
            step(v.reduce_sum(key_f, eqm.rearrange("p i a b -> p (i a) b"), AX.X))
            step(stt(key_f[:, 0:TOPK], key_f[:, 0:TOPK], float(NK), key_f[:, TOPK:2 * TOPK], ALU.mult, ALU.add))
            done(dve, v.tensor_copy(eidx[:, tt, h * TOPK:(h + 1) * TOPK], key_f[:, 0:TOPK]), "rows_ready", j + 1)

        def experts(j):
            tt, h = j // PH, j % PH
            dve.wait_ge(S("soft_exp"), j + 1)
            step(v.reciprocal(rinv, rsum[:, j:j + 1]))
            step(ts(gate_p[:, tt, h * TOPK:(h + 1) * TOPK], soft[:, j, :], rinv, None, ALU.mult))
            with dve.Fori(0, TOPK // UVS) as i:
                for s in range(UVS):
                    n = j * TOPK + s
                    dve.wait_ge(S(f"row_in{s}"), i * 16 + ((n // UVS) + 1) * 16)
                    stt(junk, uv[s][:, 0:D], 1.0, htok[:, tt, :], ALU.mult, ALU.mult, accum_out=e_act[:, s:s + 1])\
                        .then_inc(S("dot_ready"), 1)
                    dve.wait_ge(S("gelu_ready"), i * UVS + n + 1)
                    ts(diag[:, s, :], ident, e_gelu[:, s:s + 1], gate_p[:, tt, bass.ds(i * UVS + h * TOPK + s, 1)],
                       ALU.mult, ALU.mult).then_inc(S("diag_ready"), 1)

        rank(0)
        rank(1)
        dve.wait_ge(S("htok_in"), 1)
        for j in range(2 * PH):
            experts(j)
            if j + 2 < 2 * PH:
                rank(j + 2)
        dve.wait_ge(S("y_feat"), 1)
        for k in range(4):
            last = tt_(x[:, 2 * k:2 * k + 2, :], two(bank[4 + k][:, :], T), x[:, 2 * k:2 * k + 2, :], ALU.add)
        step(last)
        norm(5, x, "normf_g", hn, "final_out")

    @block.gpsimd
    def _(pool):
        def low(n, i=None):
            slot = (SPLIT0 + n) % SLOTS
            pool.wait_ge(S("hi_ready"), n + 1 if i is None else i * SLOTS + n + 1)
            nc.gpsimd.tensor_tensor(w_lo[:, slot, :], ring[:, slot, :], w_hi[:, slot, :].bitcast(F32), ALU.subtract)\
                .then_inc(S("lo_ready"), 1)

        split_pages = N_PAGES - SPLIT0
        with pool.Fori(0, split_pages // SLOTS) as i:
            for n in range(SLOTS):
                low(n, i)
        for n in range(split_pages // SLOTS * SLOTS, split_pages):
            low(n)
        pool.wait_ge(S("score_taken"), 8)

        def gather(slot, tt, col):
            nc.gpsimd.indirect_dma_start(out=uv[slot], out_offset=None, in_=A["experts"],
                                         in_offset=bass.IndirectOffsetOnAxis(ap=eidx[:, tt, col], axis=0))\
                .then_inc(S(f"row_in{slot}"), 16)

        for n in range(2 * P):
            s, tt, m = n % UVS, n // P, n % P
            if n % TOPK == 0:
                pool.wait_ge(S("rows_ready"), n // TOPK + 1)
            if n >= UVS:
                pool.wait_ge(S("row_used"), n - UVS + 1)
            gather(s, tt, slice(m, m + 1))

    block.__exit__(None, None, None)


def kernel(**inputs):
    import concourse.bacc as _bacc
    from concourse.bass_utils import run_bass_kernel_spmd as _run

    a = {k: np.asarray(v) for k, v in inputs.items()}

    def feat(m):
        r, f = m.shape
        return np.ascontiguousarray(m.reshape(r, f // P, P).transpose(2, 1, 0))

    def cols(m):
        i, o = m.shape
        return m.reshape(i // P, P, o // P, P).transpose(2, 1, 0, 3).reshape(o // P, P, i)

    def rows(m):
        return m.reshape(m.shape[0] // P, P, m.shape[1])

    w_in, w_up, kv, w2 = a["w_in"][0], a["w_up"][0], a["w_mem_kv"][0], a["w_in_2"][0]
    up = cols(w_up)
    up = np.stack([up[:FT], up[FT:]], axis=1).reshape(2 * FT, P, D)
    pages = np.concatenate([
        cols(w_in[:, 0:1792]), cols(w_in[:, 1792:2816]), cols(w_in[:, 3328:3840]),
        cols(w_in[:, 2816:3328]), cols(kv[:, 0:512]), cols(kv[:, 512:1024]), cols(w_in[:, 3840:6912]),
        rows(a["w_branch"][0].reshape(1536, D)), cols(a["w_out"][0]), up, rows(a["w_down"][0]),
        cols(w2[:, 1536:2560]), cols(w2[:, 3072:3584]), cols(w2[:, 0:1024]),
        cols(w2[:, 1024:1536]), cols(w2[:, 2560:3072]), cols(a["w_out_2"][0]), cols(a["peer_wq_2"][0])], axis=0)
    assert pages.shape == (N_PAGES, P, PAGE), pages.shape

    def vcol(m):
        return m.reshape(-1, P).T

    def pairs(m):
        t = m.reshape(2, FT, P).transpose(1, 0, 2).reshape(2 * FT, P)
        return t.T

    lb = a["rec_lb_logits_2"]
    vec = np.concatenate([
        vcol(a["shift_mu"]), vcol(a["norm1_g"]), vcol(a["decay_w0"]), vcol(a["iclr_a0"]), vcol(a["k_k"]), vcol(a["k_a"]),
        vcol(a["r_k"]), vcol(a["lnx_g"]), vcol(a["lnx_b"]), vcol(np.tile(a["sb_q_norm_g"][0], 2)),
        vcol(np.tile(a["sb_k_norm_g"][0], 2)), vcol(a["mem_norm_g"]), vcol(a["mem_q_norm_g"]), vcol(a["mem_k_norm_g"]),
        vcol(a["norm2_g"]), pairs(a["conv_w"][0, 0]), pairs(a["conv_w"][0, 1]), pairs(a["conv_w"][0, 2]), pairs(a["conv_b"][0]),
        vcol(a["norm1_g_2"]), vcol(lb[0]), vcol(lb[1]), vcol(a["rec_norm_g_2"]), vcol(a["norm2_g_2"]), vcol(a["normf_g_2"])],
        axis=1)
    sub = a["peer_subkeys_2"][0].reshape(N_WQ, NK, P).transpose(2, 0, 1)
    dram = {
        "const": constants(), "vec": vec, "xT": feat(a["x"][0]), "memT": feat(a["mem"][0]), "pages": pages,
        "decay_w2": a["decay_w2"][0], "iclr_a2": a["iclr_a2"][0], "gate_g2": a["gate_g2"][0], "subkT": sub,
        "experts": np.concatenate([a["peer_u_2"][0], a["peer_v_2"][0]], axis=1),
    }
    nc = _bacc.Bacc("TRN2", target_bir_lowering=False, num_devices=1)
    arrays, args = {}, {}
    for name, arr in dram.items():
        arr = np.ascontiguousarray(arr)
        arrays[f"in_{name}"] = arr
        args[name] = nc.dram_tensor(f"in_{name}", arr.shape, mybir.dt.from_np(arr.dtype), kind="ExternalInput").ap()
    args["out"] = nc.dram_tensor("out_T", (P, KT, T), F32, kind="ExternalOutput").ap()
    build(nc, args)
    r = _run(nc, [arrays], core_ids=[0])
    out = r.results[0]["out_T"]
    return np.ascontiguousarray(out.transpose(2, 1, 0).reshape(1, T, D))
```
